# Optimizing a Trainium2 kernel written in Bass

```python
import jax, jax.numpy as jnp
from jax import lax
import numpy as np

D_MODEL = 2048
BATCH = 1
SEQ = 256
DEPTH = 1

HEAD_DIM = 64
N_HEADS_TOTAL = D_MODEL // HEAD_DIM
HA = N_HEADS_TOTAL // 4
KVA = 2
HB = N_HEADS_TOTAL // 4
KVB = 2
HC = N_HEADS_TOTAL - HA - HB
SCALE = HEAD_DIM ** -0.5
BLOCK = 128
WINDOW_A = 128
CMP_BLOCK = 32
CMP_STRIDE = 16
CMP_HIDDEN = 128
SEL_BLOCK = 64
N_SELECT = 16
WINDOW_B = 512
FORCE_SCORE = 1e4
N_GROUPS = 4
EXPERTS_PER_GROUP = 8
N_EXPERTS = N_GROUPS * EXPERTS_PER_GROUP
TOP_K = 2
D_EXPERT = 512
MOE_BLOCK = 128
IN_SIZES = (HA * HEAD_DIM, KVA * HEAD_DIM, KVA * HEAD_DIM,
            HB * HEAD_DIM,
            KVB * HEAD_DIM, KVB * HEAD_DIM,
            KVB * HEAD_DIM, KVB * HEAD_DIM,
            KVB * HEAD_DIM, KVB * HEAD_DIM,
            HB * 3,
            HC * HEAD_DIM, HC * HEAD_DIM, HC * HEAD_DIM)
D_IN = sum(IN_SIZES)

kernel_name = "hybrid_swa_nsa_stickbreak_hmoe_deepnorm"

def layer_norm(x, g=None, b=None, eps=1e-5):
    xf = x.astype(jnp.float32)
    mu = xf.mean(-1, keepdims=True)
    var = jnp.square(xf - mu).mean(-1, keepdims=True)
    y = (xf - mu) * lax.rsqrt(var + eps)
    if g is not None:
        y = y * g.astype(jnp.float32) + b.astype(jnp.float32)
    return y.astype(x.dtype)

def group_rms(o, eps=1e-6):
    B, S = o.shape[:2]
    of = o.reshape(B, S, -1).astype(jnp.float32)
    return (of * lax.rsqrt(jnp.mean(of * of, -1, keepdims=True) + eps)).astype(o.dtype)

def alibi_slopes(n):
    return jnp.exp2(-8.0 * jnp.arange(1, n + 1, dtype=jnp.float32) / n)

def masked_softmax(s, mask, sink=None):
    s = jnp.where(mask, s, -jnp.inf)
    m = jnp.max(s, -1, keepdims=True)
    if sink is not None:
        m = jnp.maximum(m, sink)
    m = jnp.where(jnp.isfinite(m), m, 0.0)
    e = jnp.exp(s - m)
    den = e.sum(-1, keepdims=True)
    if sink is not None:
        den = den + jnp.exp(sink - m)
    return e / jnp.maximum(den, 1e-30)

def banded_window_attention(q, k, v, window, slopes, sinks=None):
    B, S, H, D = q.shape
    G = k.shape[2]
    R = H // G
    nb = S // BLOCK
    span = window + BLOCK
    kp = jnp.pad(k, ((0, 0), (window, 0), (0, 0), (0, 0)))
    vp = jnp.pad(v, ((0, 0), (window, 0), (0, 0), (0, 0)))
    qb = q.reshape(B, nb, BLOCK, G, R, D)
    slope = slopes.reshape(G, R)[None, :, :, None, None]
    sink = None if sinks is None else sinks.astype(jnp.float32).reshape(G, R)[None, :, :, None, None]
    offs_q = jnp.arange(BLOCK)
    offs_k = jnp.arange(span)

    def one_block(i):
        qi = lax.dynamic_index_in_dim(qb, i, axis=1, keepdims=False)
        ki = lax.dynamic_slice_in_dim(kp, i * BLOCK, span, axis=1)
        vi = lax.dynamic_slice_in_dim(vp, i * BLOCK, span, axis=1)
        t = i * BLOCK + offs_q
        s_pos = i * BLOCK - window + offs_k
        dist = t[:, None] - s_pos[None, :]
        mask = (dist >= 0) & (dist < window) & (s_pos[None, :] >= 0)
        s = jnp.einsum('bqgrd,bkgd->bgrqk', qi, ki).astype(jnp.float32) * SCALE
        s = s - slope * dist.astype(jnp.float32)
        p = masked_softmax(s, mask, sink)
        o = jnp.einsum('bgrqk,bkgd->bqgrd', p.astype(vi.dtype), vi)
        return o.reshape(B, BLOCK, H, D)

    out = lax.map(one_block, jnp.arange(nb))
    return out.transpose(1, 0, 2, 3, 4).reshape(B, S, H, D)

def compress_blocks(x, pe, w1, w2):
    B, S, G, D = x.shape
    nc = (S - CMP_BLOCK) // CMP_STRIDE + 1
    idx = jnp.arange(nc)[:, None] * CMP_STRIDE + jnp.arange(CMP_BLOCK)[None, :]
    blocks = x[:, idx] + pe[None, None, :, None, :]
    flat = blocks.transpose(0, 1, 3, 2, 4).reshape(B, nc, G, CMP_BLOCK * D)
    return jax.nn.gelu(flat @ w1) @ w2

def nsa_compressed_and_selected(q, kc, vc, ks_all, vs_all, slopes):
    B, S, H, D = q.shape
    G = kc.shape[2]
    R = H // G
    nb = S // BLOCK
    nc = kc.shape[1]
    nsel = S // SEL_BLOCK
    n_pick = min(N_SELECT, nsel)
    qb = q.reshape(B, nb, BLOCK, G, R, D)
    cmp_start = jnp.arange(nc) * CMP_STRIDE
    cmp_end = cmp_start + CMP_BLOCK - 1
    sel_idx = jnp.arange(nsel)
    sel_start = sel_idx * SEL_BLOCK
    overlap = ((cmp_end[:, None] >= sel_start[None, :]) &
               (cmp_start[:, None] < sel_start[None, :] + SEL_BLOCK)).astype(jnp.float32)
    kst = ks_all.transpose(0, 2, 1, 3)
    vst = vs_all.transpose(0, 2, 1, 3)
    slope = slopes.reshape(G, R)[None, :, :, None, None]
    bi = jnp.arange(B)[:, None, None, None]
    gi = jnp.arange(G)[None, None, :, None]
    offs_q = jnp.arange(BLOCK)
    offs_sel = jnp.arange(SEL_BLOCK)

    def one_block(i):
        qi = lax.dynamic_index_in_dim(qb, i, axis=1, keepdims=False)
        t = i * BLOCK + offs_q
        dist_c = t[:, None] - cmp_end[None, :]
        sc = jnp.einsum('bqgrd,bngd->bgrqn', qi, kc).astype(jnp.float32) * SCALE
        sc = sc - slope * dist_c.astype(jnp.float32)
        pc = masked_softmax(sc, dist_c >= 0)
        o_c = jnp.einsum('bgrqn,bngd->bqgrd', pc.astype(vc.dtype), vc)
        imp = jnp.einsum('bgrqn,nj->bqgj', pc, overlap)
        cur = t // SEL_BLOCK
        forced = (sel_idx[None, :] == 0) | (sel_idx[None, :] == cur[:, None]) | (sel_idx[None, :] == cur[:, None] - 1)
        valid = sel_start[None, :] <= t[:, None]
        imp = jnp.where(valid[None, :, None, :],
                        jnp.where(forced[None, :, None, :], FORCE_SCORE, imp), -1.0)
        _, sel = lax.top_k(imp, n_pick)
        tok = (sel[..., None] * SEL_BLOCK + offs_sel).reshape(B, BLOCK, G, n_pick * SEL_BLOCK)
        ks = kst[bi, gi, tok]
        vs = vst[bi, gi, tok]
        dist_s = (t[None, :, None, None] - tok).transpose(0, 2, 1, 3)[:, :, None]
        ss = jnp.einsum('bqgrd,bqgkd->bgrqk', qi, ks).astype(jnp.float32) * SCALE
        ss = ss - slope * dist_s.astype(jnp.float32)
        ps = masked_softmax(ss, dist_s >= 0)
        o_s = jnp.einsum('bgrqk,bqgkd->bqgrd', ps.astype(vs.dtype), vs)
        return o_c.reshape(B, BLOCK, H, D), o_s.reshape(B, BLOCK, H, D)

    o_c, o_s = lax.map(one_block, jnp.arange(nb))
    unblock = lambda o: o.transpose(1, 0, 2, 3, 4).reshape(B, S, H, D)
    return unblock(o_c), unblock(o_s)

def stick_breaking_attention(q, k, v):
    B, S, H, D = q.shape
    nb = S // BLOCK
    qb = q.reshape(B, nb, BLOCK, H, D)
    s_pos = jnp.arange(S)
    offs_q = jnp.arange(BLOCK)
    vf = v.astype(jnp.float32)

    def one_block(i):
        qi = lax.dynamic_index_in_dim(qb, i, axis=1, keepdims=False)
        t = i * BLOCK + offs_q
        mask = s_pos[None, :] < t[:, None]
        z = jnp.einsum('bqhd,bkhd->bhqk', qi, k).astype(jnp.float32) * SCALE
        log_1mb = jnp.where(mask, jax.nn.log_sigmoid(-z), 0.0)
        tail = lax.cumsum(log_1mb, axis=3, reverse=True) - log_1mb
        a = jnp.where(mask, jnp.exp(jax.nn.log_sigmoid(z) + tail), 0.0)
        return jnp.einsum('bhqk,bkhd->bqhd', a, vf)

    out = lax.map(one_block, jnp.arange(nb))
    return out.transpose(1, 0, 2, 3, 4).reshape(B, S, H, D).astype(q.dtype)

def hybrid_mixer(h, w_in, sinks, cmp_pe_k, cmp_w1_k, cmp_w2_k, cmp_pe_v, cmp_w1_v, cmp_w2_v, mix_gain, w_out):
    B, S, _ = h.shape
    proj = h @ w_in
    split_at = np.cumsum(IN_SIZES)[:-1].tolist()
    (qa, ka, va, qb, kb_c, vb_c, kb_s, vb_s, kb_w, vb_w, gb, qc, kc, vc) = jnp.split(proj, split_at, axis=-1)
    heads = lambda t: t.reshape(B, S, -1, HEAD_DIM)
    slopes = alibi_slopes(HA + HB)
    o_a = banded_window_attention(heads(qa), heads(ka), heads(va), WINDOW_A, slopes[:HA], sinks)
    qbh = heads(qb)
    k_cmp = compress_blocks(heads(kb_c), cmp_pe_k, cmp_w1_k, cmp_w2_k)
    v_cmp = compress_blocks(heads(vb_c), cmp_pe_v, cmp_w1_v, cmp_w2_v)
    o_cmp, o_slc = nsa_compressed_and_selected(qbh, k_cmp, v_cmp, heads(kb_s), heads(vb_s), slopes[HA:])
    o_win = banded_window_attention(qbh, heads(kb_w), heads(vb_w), WINDOW_B, slopes[HA:])
    g = jax.nn.sigmoid(gb.reshape(B, S, HB, 3))
    o_b = g[..., 0:1] * o_cmp + g[..., 1:2] * o_slc + g[..., 2:3] * o_win
    o_c = stick_breaking_attention(heads(qc), heads(kc), heads(vc))
    merged = jnp.concatenate([group_rms(o_a), group_rms(o_b), group_rms(o_c)], axis=-1) * mix_gain
    return merged @ w_out

def hierarchical_moe(h, w_rg, b_rg, w_re, b_re, w_gate, w_up, w_down):
    B, S, D = h.shape
    N = B * S
    xt = h.reshape(N, D)
    pg = jax.nn.softmax((xt @ w_rg + b_rg).astype(jnp.float32), axis=-1)
    g_sel = jnp.argmax(pg, axis=-1)
    p_group = jnp.max(pg, axis=-1)
    le = jnp.einsum('nd,gde->nge', xt, w_re) + b_re
    le_sel = jnp.take_along_axis(le, g_sel[:, None, None], axis=1)[:, 0]
    pe = jax.nn.softmax(le_sel.astype(jnp.float32), axis=-1)
    top_p, top_e = lax.top_k(pe, TOP_K)
    gate = p_group[:, None] * top_p / jnp.sum(top_p, -1, keepdims=True)
    expert = g_sel[:, None] * EXPERTS_PER_GROUP + top_e
    A = N * TOP_K
    e_flat = expert.reshape(A)
    tok = jnp.repeat(jnp.arange(N), TOP_K)
    w_flat = gate.reshape(A)
    counts = jnp.zeros((N_EXPERTS,), jnp.int32).at[e_flat].add(1)
    padded = (counts + MOE_BLOCK - 1) // MOE_BLOCK * MOE_BLOCK
    pad_end = jnp.cumsum(padded)
    pad_start = pad_end - padded
    start = jnp.cumsum(counts) - counts
    order = jnp.argsort(e_flat)
    e_sorted = e_flat[order]
    tok_sorted = tok[order]
    dest = pad_start[e_sorted] + (jnp.arange(A) - start[e_sorted])
    n_blocks = -(-A // MOE_BLOCK) + N_EXPERTS
    rows = n_blocks * MOE_BLOCK
    buf = jnp.zeros((rows, D), h.dtype).at[dest].set(xt[tok_sorted])
    blk_start = jnp.arange(n_blocks) * MOE_BLOCK
    blk_expert = jnp.minimum(jnp.sum(blk_start[:, None] >= pad_end[None, :], axis=1), N_EXPERTS - 1)

    def expert_block(args):
        xblk, e = args
        hid = jax.nn.silu(xblk @ w_gate[e]) * (xblk @ w_up[e])
        return hid @ w_down[e]

    yb = lax.map(expert_block, (buf.reshape(n_blocks, MOE_BLOCK, D), blk_expert)).reshape(rows, D)
    y = yb[dest] * w_flat[order][:, None].astype(h.dtype)
    out = jax.ops.segment_sum(y, tok_sorted, num_segments=N)
    return out.reshape(B, S, D)

def setup_inputs(seed: int = 0) -> dict:
    key = jax.random.key(seed)
    ks = jax.random.split(key, 28)
    L, D = DEPTH, D_MODEL
    beta = (8.0 * DEPTH) ** -0.25

    def nrm(k, shape, scale):
        return jax.random.normal(k, shape, jnp.float32) * scale

    return {
        "x": nrm(ks[0], (BATCH, SEQ, D), 1.0),
        "c": nrm(ks[1], (BATCH, D), 1.0),
        "w_ada": nrm(ks[2], (L, D, 6 * D), 0.1 * D ** -0.5),
        "b_ada": nrm(ks[3], (L, 6 * D), 0.02),
        "w_in": nrm(ks[4], (L, D, D_IN), D ** -0.5),
        "sinks": nrm(ks[5], (L, HA), 0.5),
        "cmp_pe_k": nrm(ks[6], (L, CMP_BLOCK, HEAD_DIM), 0.02),
        "cmp_w1_k": nrm(ks[7], (L, CMP_BLOCK * HEAD_DIM, CMP_HIDDEN), (CMP_BLOCK * HEAD_DIM) ** -0.5),
        "cmp_w2_k": nrm(ks[8], (L, CMP_HIDDEN, HEAD_DIM), CMP_HIDDEN ** -0.5),
        "cmp_pe_v": nrm(ks[9], (L, CMP_BLOCK, HEAD_DIM), 0.02),
        "cmp_w1_v": nrm(ks[10], (L, CMP_BLOCK * HEAD_DIM, CMP_HIDDEN), (CMP_BLOCK * HEAD_DIM) ** -0.5),
        "cmp_w2_v": nrm(ks[11], (L, CMP_HIDDEN, HEAD_DIM), CMP_HIDDEN ** -0.5),
        "mix_gain": 1.0 + nrm(ks[12], (L, D), 0.02),
        "w_out": nrm(ks[13], (L, D, D), beta * D ** -0.5),
        "ln1_g": 1.0 + nrm(ks[14], (L, D), 0.02),
        "ln1_b": nrm(ks[15], (L, D), 0.02),
        "w_rg": nrm(ks[16], (L, D, N_GROUPS), D ** -0.5),
        "b_rg": nrm(ks[17], (L, N_GROUPS), 0.01),
        "w_re": nrm(ks[18], (L, N_GROUPS, D, EXPERTS_PER_GROUP), D ** -0.5),
        "b_re": nrm(ks[19], (L, N_GROUPS, EXPERTS_PER_GROUP), 0.01),
        "w_gate": nrm(ks[20], (L, N_EXPERTS, D, D_EXPERT), D ** -0.5),
        "w_up": nrm(ks[21], (L, N_EXPERTS, D, D_EXPERT), D ** -0.5),
        "w_down": nrm(ks[22], (L, N_EXPERTS, D_EXPERT, D), beta * D_EXPERT ** -0.5),
        "ln2_g": 1.0 + nrm(ks[23], (L, D), 0.02),
        "ln2_b": nrm(ks[24], (L, D), 0.02),
    }

def reference(x, c, w_ada, b_ada, w_in, sinks, cmp_pe_k, cmp_w1_k, cmp_w2_k, cmp_pe_v, cmp_w1_v, cmp_w2_v,
              mix_gain, w_out, ln1_g, ln1_b, w_rg, b_rg, w_re, b_re, w_gate, w_up, w_down, ln2_g, ln2_b):
    alpha = (2.0 * DEPTH) ** 0.25
    cs = jax.nn.silu(c)
    for l in range(DEPTH):
        mod = (cs @ w_ada[l] + b_ada[l])[:, None, :]
        sh1, sc1, g1, sh2, sc2, g2 = jnp.split(mod, 6, axis=-1)
        h = layer_norm(x) * (1.0 + sc1) + sh1
        y = hybrid_mixer(h, w_in[l], sinks[l], cmp_pe_k[l], cmp_w1_k[l], cmp_w2_k[l],
                         cmp_pe_v[l], cmp_w1_v[l], cmp_w2_v[l], mix_gain[l], w_out[l])
        x = layer_norm(alpha * x + (1.0 + g1) * y, ln1_g[l], ln1_b[l])
        h = layer_norm(x) * (1.0 + sc2) + sh2
        y = hierarchical_moe(h, w_rg[l], b_rg[l], w_re[l], b_re[l], w_gate[l], w_up[l], w_down[l])
        x = layer_norm(alpha * x + (1.0 + g2) * y, ln2_g[l], ln2_b[l])
    return x


_drawn_inputs = setup_inputs


def setup_inputs(seed=0):
    import zlib

    import numpy as np

    out = dict(_drawn_inputs(seed))
    spreads = {}
    factors = {'sinks': 2.877,
     'cmp_pe_k': 23.55,
     'cmp_pe_v': 8.0,
     'mix_gain': 11.197,
     'b_rg': 31.185,
     'b_re': 8.0,
     'ln2_g': 8.304,
     'ln2_b': 8.182}
    for name, (base, spread) in spreads.items():
        noise = np.random.default_rng([zlib.crc32(name.encode()), seed]).standard_normal(out[name].shape)
        drawn = base * np.exp(spread * noise) if base else spread * noise
        out[name] = __import__('jax').numpy.asarray(drawn.astype(out[name].dtype))
    for name, factor in factors.items():
        out[name] = (out[name] * factor).astype(out[name].dtype)
    return out
```

```python
from contextlib import ExitStack

import numpy as np
import concourse.bass as bass
from concourse import mybir

ALU = mybir.AluOpType
ACT = mybir.ActivationFunctionType
F32 = mybir.dt.float32
I32 = mybir.dt.int32
AX = mybir.AxisListType

P = 128
D = 2048
SEQ = 256
TB = SEQ // P
KC = D // P
HD = 64
HA = HB = 8
HC = 16
SCALE = HD ** -0.5
ALPHA = 2.0 ** 0.25
MASKED = -1e30
CMP_LEN, CMP_STEP = 32, 16
NCMP = (SEQ - CMP_LEN) // CMP_STEP + 1
NG, EPG, NE, DE = 4, 8, 32, 512
WIN = 64
PAIRS = NE // 2
PASSES = SEQ // WIN
BN = 512
SLOTS = 8
UNIT = 2048
SLOPES = [2.0 ** (-8.0 * (h + 1) / (HA + HB)) for h in range(HA + HB)]
GELU_C = 2.0 * (2.0 / np.pi) ** 0.5

WIN_GROUPS = [(0, 512), (512, 256), (768, 512), (1280, 256), (1536, 512)] + [
    (2072 + 512 * j, 512) for j in range(6)]
AB_GROUPS = 5
GATE_COL = 2048
K_A, K_CMP, V_CMP, K_SEL, K_WIN, K_C = 0, 1, 2, 3, 4, 5
V_A, V_SEL, V_WIN, V_C = 0, 128, 256, 384
VCOLS = 384 + HC * HD


def first_unit(group):
    return sum(KC * width // UNIT for _, width in WIN_GROUPS[:group])


def w_in_units(w):
    units = []
    for gi, (c0, width) in enumerate(WIN_GROUPS):
        cols = w[:, c0:c0 + width]
        if gi in (0, 2):
            cols = cols.reshape(D, 2, 4, HD).transpose(0, 2, 1, 3).reshape(D, width)
        kn = UNIT // width
        units.append(cols.reshape(KC // kn, kn, P, width).transpose(0, 2, 1, 3).reshape(-1, P, UNIT))
    return np.concatenate(units)


def weight_units():
    units = [("ada", k, half, "dve") for k in range(KC) for half in (0, 1)]

    def merge(groups, halves):
        w = []
        for g in groups:
            width = WIN_GROUPS[g][1]
            n = KC * width // UNIT
            w += [("win", g, i, "pe") for i in range(n)]
        a = [("ada", k, half, "dve") for k in range(KC) for half in halves]
        out, taken = [], 0
        for i, u in enumerate(w):
            out.append(u)
            upto = (i + 1) * len(a) // len(w)
            out += a[taken:upto]
            taken = upto
        return out

    units += merge(range(AB_GROUPS), (2, 3))
    units += [("w1", s, i, "pe") for s in (0, 1) for i in (0, 1)]
    units += merge(range(AB_GROUPS, len(WIN_GROUPS)), (4, 5))
    units += [("wout", k, 0, "pe") for k in range(KC)]
    return units


UNITS = weight_units()
N_UNITS = len(UNITS)
PAIR_UNITS = 24
N_SMALL = 11
MISC_PAIR, MISC_FLUSH = 14, 8
MOE_STEPS, MOE_FLUSH_STEPS = 3, 2
POOL_CONST, POOL_SETUP = 8, 10


def pair_unit(j):
    if j < 16:
        quarter, r = divmod(j, 4)
        return ("gate", "up")[r // 2], r % 2, quarter
    quarter, r = divmod(j - 16, 2)
    return "down", r, quarter


class Steps:

    def __init__(self, eng, sem):
        self.eng, self.sem, self.n, self.turn = eng, sem, 0, 0

    def __call__(self, ins, k=1):
        ins.then_inc(self.sem, k)
        self.n += k

    def wait(self, eng=None):
        (eng or self.eng).wait_ge(self.sem, self.turn + self.n)


def build(nc, x, cT, w_ada, b_ada, w_in, w_gb, sinks, pe_k, pe_v, w1_k, w1_v, w2_k, w2_v, gain, w_out,
          ln1_g, ln1_b, w_route, b_route, w_gate, w_up, w_down, ln2_g, ln2_b, out):
    with ExitStack() as ctx:
        def sb(name, shape, dt=F32):
            return ctx.enter_context(nc.sbuf_tensor(name, shape, dt))

        def sem(name):
            return ctx.enter_context(nc.semaphore(name))

        ps = ctx.enter_context(nc.psum_tensor("ps", [P, 8, BN], F32))
        psf = ps[:].rearrange("p b n -> p (b n)")

        ring = sb("ring", [P, SLOTS, UNIT])
        tokens = sb("tokens", [P, TB, D])
        featT = sb("featT", [P, KC, SEQ])
        queryT = sb("queryT", [P, 2, 8, SEQ])
        keyval = sb("keyval", [P, 13 * SEQ + TB * VCOLS])
        work = sb("work", [P, 3 * 1536])
        bias = sb("bias", [P, 2 * 8 * 384])
        g1b = sb("g1b", [P, D])
        g2b = sb("g2b", [P, D])

        acc1 = keyval[:, 0:2 * D]
        acc2 = tokens[:].rearrange("p a b -> p (a b)")
        acc3 = bias[:, 0:2 * D]
        merged = tokens
        keyT = keyval[:, 0:13 * SEQ].rearrange("p (k t) -> p k t", k=13)
        value = keyval[:, 13 * SEQ:].rearrange("p (c n) -> p c n", c=TB)
        xn2 = queryT[:].rearrange("p a b t -> p (a b t)").rearrange("p (c d) -> p c d", c=TB)
        ysum = featT[:].rearrange("p k t -> p (k t)").rearrange("p (c d) -> p c d", c=TB)
        x_pair = keyval[:, 0:KC * P].rearrange("p (k s) -> p k s", k=KC)
        y_pair = keyval[:, KC * P:2 * KC * P]
        biasX = bias[:, 0:16 * 256].rearrange("p (h k) -> p h k", h=16)
        biasY = bias[:, 16 * 256:].rearrange("p (h k) -> p h k", h=16)
        rowg, rowb = bias[:, 0:D], bias[:, D:2 * D]
        swork = [work[:, 0:1536], work[:, 1536:3072]]
        ptw = work[:, 3072:4608]
        e_gate, hid, hidT = work[:, 0:DE], work[:, DE:2 * DE], work[:, 2 * DE:3 * DE]

        dist = work[:, 0:384]
        rt = work[:, 3072:3840].rearrange("p (i c e) -> p i c e", i=12, c=TB)
        sel = work[:, 3840:4096].rearrange("p (c e s) -> p c e s", c=TB, e=2)
        selg = work[:, 4096:4352].rearrange("p (c e s) -> p c e s", c=TB, e=2)
        scatter = work[:, 4352:4608]

        ident = sb("ident", [P, P])
        ones = sb("ones", [P, P])
        neg_ones = sb("neg_ones", [P, P])
        neg_tri = sb("neg_tri", [P, P])
        before = sb("before", [P, P])
        slot_id = sb("slot_id", [P, 2, WIN])
        cmp_bias = sb("cmp_bias", [P, TB, HB, NCMP])
        cmp_mask = sb("cmp_mask", [P, TB * HB, NCMP])
        cvec = sb("cvec", [P, KC])
        cs = sb("cs", [P, KC])
        ctmp = sb("ctmp", [P, KC])
        sinkb = sb("sinkb", [P, HA])
        gaincol = sb("gaincol", [P, KC])
        pe2 = sb("pe2", [P, 2, CMP_LEN])
        w2 = sb("w2", [P, 2, HD])
        wr = sb("wr", [P, KC, NG + NE])
        brow = sb("brow", [P, NG + NE])
        gbw = sb("gbw", [P, KC, 3 * HB])
        gates = sb("gates", [P, TB, HB, 3])
        cols = sb("cols", [P, 4, KC])
        stats = sb("stats", [P, TB, 4, 6])
        mv = sb("mv", [P, TB, 2])
        rstd = sb("rstd", [P, TB])
        mx = sb("mx", [P, 2, TB, 4])
        nmx = sb("nmx", [P, 2, TB, 4])
        den = sb("den", [P, 2, TB, 4])
        den2 = sb("den2", [P, 2, TB, 4])
        hidc = sb("hidc", [P, 4, 2, 2, 16])
        kcmpT = sb("kcmpT", [P, 16])
        vblk = sb("vblk", [P, 2, 256])
        cst = sb("cst", [P, 4, TB * HB])
        ssq = sb("ssq", [P, TB, 3])
        minus_half = sb("minus_half", [P, TB * 3])
        lg = sb("lg", [P, TB, NG + NE])
        r1 = sb("r1", [P, 10, TB])
        rankm = sb("rankm", [P, TB, NE])
        gate_te = sb("gate_te", [P, TB, NE])
        more = sb("more", [P, PASSES], I32)

        full = [sem(f"ring_full_{i}") for i in range(SLOTS)]
        pe_freed = sem("pe_freed")
        dve_freed = sem("dve_freed")
        x_in, c_in, small_in, ln_in, xr_in = (sem(n) for n in ("x_in", "c_in", "small_in", "ln_in", "xr_in"))
        bias1_in, bias2_in, bias3_in = (sem(n) for n in ("bias1_in", "bias2_in", "bias3_in"))
        stored = sem("stored")
        pool_s = sem("pool_steps")
        dve_s = sem("dve_steps")
        act_s = sem("act_steps")
        ec_ready = sem("ec_ready")
        xn_ready = sem("xn_ready")
        xnT_full = sem("xnT_full")
        xnT_copied = sem("xnT_copied")
        acc_ready = sem("acc_ready")
        acc_zeroed = sem("acc_zeroed")
        ada_sums = sem("ada_sums")
        ada_taken = sem("ada_taken")
        hT_ready = sem("hT_ready")
        gate_mm = sem("gate_mm")
        var_ready, rstd_ready = sem("var_ready"), sem("rstd_ready")
        cmp_o_taken = sem("cmp_o_taken")
        x2T_even, x2T_odd = sem("x2T_even"), sem("x2T_odd")
        proj_taken = sem("proj_taken")
        cmp_in_ready, cmp_act, cmp_kv, cmp_kv_taken, cmp_s, cmp_p, cmp_pt, cmp_pt_taken, cmp_o = (
            sem(n) for n in ("cmp_in_ready", "cmp_act", "cmp_kv", "cmp_kv_taken", "cmp_s", "cmp_p",
                             "cmp_pt", "cmp_pt_taken", "cmp_o"))
        cmp_h_ready, cmp_e, cmp_sm, cmp_ex = (sem(n) for n in ("cmp_h_ready", "cmp_e", "cmp_sm", "cmp_ex"))
        gate_e = sem("gate_e")
        s_done, s_taken, m_ready, exp_done, sink_done, pt_full, pt_taken, o_full, o_taken = (
            sem(n) for n in ("s_done", "s_taken", "m_ready", "exp_done", "sink_done", "pt_full", "pt_taken",
                             "o_full", "o_taken"))
        z_done, l_done, sp_done, lmask, zr_done, clamp_done, a_done, a_masked, oc_full, oc_taken = (
            sem(n) for n in ("z_done", "l_done", "sp_done", "lmask", "zr_done", "clamp_done", "a_done",
                             "a_masked", "oc_full", "oc_taken"))
        sq_done, merged_ready, mT_full, mT_ready = (sem(n) for n in ("sq_done", "merged_ready", "mT_full", "mT_ready"))
        y_ready, xn2_ready, x2T_full, x2T_ready, route_mm, lg_ready, rtab_ready, rank_full, route_ready = (
            sem(n) for n in ("y_ready", "xn2_ready", "x2T_full", "x2T_ready", "route_mm", "lg_ready",
                             "rtab_ready", "rank_full", "route_ready"))
        rexp_in, rexp_out = sem("rexp_in"), sem("rexp_out")
        misc_full, misc_free, sel_ready, xg_ready, gu_done, e_ready, hid_ready, hidT_ready = (
            sem(n) for n in ("misc_full", "misc_free", "sel_ready", "xg_ready", "gu_done", "e_ready",
                             "hid_ready", "hidT_ready"))
        y_done, ysb_ready, comb_done, wc_ready, selg_ready, moe_s, fin_s, out_ready, passes_s = (
            sem(n) for n in ("y_done", "ysb_ready", "comb_done", "wc_ready", "selg_ready", "moe_steps",
                             "fin_steps", "out_ready", "passes_s"))

        uses = [0] * SLOTS
        unit_at, need = [], []
        seen = {"pe": 0, "dve": 0}
        for n, u in enumerate(UNITS):
            s = n % SLOTS
            uses[s] += 1
            unit_at.append((s, 16 * uses[s]))
            seen[u[3]] += 1
            need.append((u[3], seen[u[3]]))
        PE_BASE = seen["pe"]

        def arrived(eng, n):
            eng.wait_ge(full[unit_at[n][0]], unit_at[n][1])

        def index_of(kind, a, b):
            return next(n for n, u in enumerate(UNITS) if u[:3] == (kind, a, b))

        def freed_after(kind, a, b):
            return need[index_of(kind, a, b)][1]

        def group_done(gi):
            return freed_after("win", gi, KC * WIN_GROUPS[gi][1] // UNIT - 1)

        def pair_slot(j):
            return (N_UNITS + j) % SLOTS

        def pair_value(j):
            return 16 * (uses[pair_slot(j)] + j // SLOTS + 1)

        block = ctx.enter_context(nc.Block())

        @block.sync
        def _(sp):
            for n, (kind, a, b, _) in enumerate(UNITS):
                slot = ring[:, n % SLOTS, :]
                if n >= SLOTS:
                    who, count = need[n - SLOTS]
                    sp.wait_ge(pe_freed if who == "pe" else dve_freed, count)
                if kind == "ada":
                    sp.dma_start(slot, w_ada[a * P:(a + 1) * P, b * D:(b + 1) * D]).then_inc(full[n % SLOTS], 16)
                elif kind == "win":
                    sp.dma_start(slot, w_in[first_unit(a) + b]).then_inc(full[n % SLOTS], 16)
                elif kind == "w1":
                    w1 = (w1_k, w1_v)[a]
                    sp.dma_start(slot, w1[:, b * UNIT:(b + 1) * UNIT]).then_inc(full[n % SLOTS], 16)
                else:
                    sp.dma_start(slot, w_out[a * P:(a + 1) * P, :]).then_inc(full[n % SLOTS], 16)

            def load_pair(p, q):
                for j in range(PAIR_UNITS):
                    what, which, quarter = pair_unit(j)
                    slot = ring[:, pair_slot(j), :]
                    if what == "down":
                        off = sp.snap((p * 2 + which) * DE + quarter * P)
                        src = w_down[bass.ds(off, P), :]
                        dst = slot
                    else:
                        w = w_gate if what == "gate" else w_up
                        off = sp.snap((p * 2 + which) * D + quarter * 4 * P)
                        src = w[bass.ds(off, 4 * P), :].rearrange("(k p) n -> p k n", p=P)
                        dst = slot.rearrange("p (k n) -> p k n", k=4)
                    value = sp.snap(q * PAIR_UNITS + (PE_BASE + j - SLOTS + 1))
                    sp.wait_ge(pe_freed, value)
                    sp.dma_start(dst, src).then_inc(full[pair_slot(j)], 16)

            with sp.Fori(0, PAIRS) as p:
                load_pair(p, p)
            sp.wait_ge(route_ready, PASSES)
            with sp.Fori(1, PASSES) as w:
                go = sp.value_load(more[0:1, bass.ds(w, 1)])
                with sp.If(go > 0):
                    with sp.Fori(0, PAIRS) as p:
                        load_pair(p, w * PAIRS + p)
            for c in range(TB):
                sp.wait_ge(out_ready, c + 1)
                sp.dma_start(out[c * P:(c + 1) * P, :], tokens[:, c, :]).then_inc(stored, 16)
            sp.wait_ge(stored, 16 * TB)

        @block.gpsimd
        def _(pool):
            st = Steps(pool, pool_s)
            g = nc.gpsimd
            st(g.memset(acc1, 0.0))
            st(g.memset(minus_half[:], -0.5))
            st(g.memset(ident[:], 0.0))
            st(g.memset(ones[:], 1.0))
            st(g.memset(neg_ones[:], -1.0))
            st.wait()
            st(g.affine_select(out=ident[:], in_=ident[:], compare_op=ALU.not_equal, fill=1.0, base=0,
                               pattern=[[-1, P]], channel_multiplier=1))
            st(g.affine_select(out=neg_tri[:], in_=neg_ones[:], compare_op=ALU.is_ge, fill=0.0, base=0,
                               pattern=[[-1, P]], channel_multiplier=1))
            st(g.affine_select(out=before[:], in_=ones[:], compare_op=ALU.is_gt, fill=0.0, base=0,
                               pattern=[[1, P]], channel_multiplier=-1))
            st(g.iota(slot_id[:], pattern=[[0, 2], [1, WIN]], base=0, channel_multiplier=0,
                      allow_small_or_imprecise_dtypes=True))
            st(g.memset(queryT[:].rearrange("p a b t -> p (a b t)"), 0.0))
            st(g.iota(dist[:, 0:256], pattern=[[-1, 256]], base=P, channel_multiplier=1,
                      allow_small_or_imprecise_dtypes=True))
            st(g.iota(dist[:, 256:384], pattern=[[-1, P]], base=0, channel_multiplier=1,
                      allow_small_or_imprecise_dtypes=True))
            st(g.iota(cmp_bias[:], pattern=[[P, TB], [0, HB], [-CMP_STEP, NCMP]], base=1 - CMP_LEN,
                      channel_multiplier=1, allow_small_or_imprecise_dtypes=True))
            st(g.memset(cmp_mask[:], 1.0))
            st(g.memset(vblk[:], 0.0))
            st.wait()
            st(g.affine_select(out=cmp_mask[:], in_=cmp_mask[:], compare_op=ALU.is_ge, fill=0.0,
                               base=1 - CMP_LEN, pattern=[[P, TB], [0, HB], [-CMP_STEP, NCMP]],
                               channel_multiplier=1))
            for h in range(HB):
                st(g.tensor_scalar(cmp_bias[:, :, h, :], cmp_bias[:, :, h, :], -SLOPES[HA + h], None, ALU.mult))
            for h in range(HA + HB):
                st(g.tensor_scalar(biasX[:, h, :], dist[:, 0:256], -SLOPES[h], None, ALU.mult))
                st(g.tensor_scalar(biasY[:, h, :], dist[:, 256:384], -SLOPES[h], None, ALU.mult))
            st.wait()
            st(g.affine_select(out=cmp_bias[:], in_=cmp_bias[:], compare_op=ALU.is_ge, fill=MASKED,
                               base=1 - CMP_LEN, pattern=[[P, TB], [0, HB], [-CMP_STEP, NCMP]],
                               channel_multiplier=1))
            st(g.affine_select(out=biasY, in_=biasY, compare_op=ALU.is_ge, fill=MASKED, base=0,
                               pattern=[[0, 16], [-1, P]], channel_multiplier=1))
            st(g.affine_select(out=biasX, in_=biasX, compare_op=ALU.is_ge, fill=MASKED, base=P,
                               pattern=[[0, 16], [-1, 256]], channel_multiplier=1))
            st.wait()
            st(g.affine_select(out=biasX[:, 0:HA, :], in_=biasX[:, 0:HA, :], compare_op=ALU.is_ge, fill=MASKED,
                               base=-1, pattern=[[0, HA], [1, 256]], channel_multiplier=-1))
            st.wait()
            norms = [0]

            def rsqrt_variance(c):
                norms[0] += 1
                pool.wait_ge(var_ready, norms[0])
                g.tensor_tensor(rstd[:, c:c + 1], rstd[:, c:c + 1], minus_half[:, 0:1], ALU.pow).then_inc(rstd_ready, 1)

            for c in range(TB):
                rsqrt_variance(c)
            pool.wait_ge(xnT_copied, 8)
            g.memset(acc2, 0.0).then_inc(acc_zeroed, 1)
            kpe = work[:, 0:2048]
            g.memset(kpe, 0.0).then_inc(acc_zeroed, 1)
            pool.wait_ge(s_taken, 6)
            g.memset(acc3, 0.0).then_inc(acc_zeroed, 1)
            def diagonal(b, ready, done):
                s = swork[b % 2]
                pool.wait_ge(ready, b + 1)
                for v in (s[:, 0:1024].rearrange("p (h q) -> p h q", h=4)[:, :, 0:P],
                          s[:, 1024:1536].rearrange("p (h q) -> p h q", h=4)):
                    g.affine_select(out=v, in_=v, compare_op=ALU.is_gt, fill=0.0, base=0,
                                    pattern=[[0, 4], [1, P]], channel_multiplier=-1).then_inc(done, 1)

            diagonal(0, sp_done, lmask)
            for b in range(HC // 4):
                if b + 1 < HC // 4:
                    diagonal(b + 1, sp_done, lmask)
                diagonal(b, a_done, a_masked)
            norms[0] += 1
            pool.wait_ge(var_ready, norms[0])
            flat = ssq[:].rearrange("p c g -> p (c g)")
            g.tensor_tensor(flat, flat, minus_half[:], ALU.pow).then_inc(rstd_ready, 1)
            for c in (0, 0, 1, 1, 0, 1):
                rsqrt_variance(c)

        @block.scalar
        def _(act):
            sc = nc.scalar
            act.dma_start(cvec[:], cT).then_inc(c_in, 16)
            act.dma_start(tokens[:], x.rearrange("(c p) d -> p c d", p=P)).then_inc(x_in, 16)
            smalls = [(gaincol[:], gain), (sinkb[:], sinks[0:1, :].partition_broadcast(P)),
                      (brow[:], b_route[0:1, :].partition_broadcast(P)), (wr[:], w_route),
                      (pe2[0:HD, 0, :], pe_k), (pe2[HD:P, 0, :], pe_k),
                      (pe2[0:HD, 1, :], pe_v), (pe2[HD:P, 1, :], pe_v),
                      (w2[:, 0, :], w2_k), (w2[:, 1, :], w2_v),
                      (gbw[:], w_gb)]
            for dst, src in smalls:
                act.dma_start(dst, src).then_inc(small_in, 16)
            assert len(smalls) == N_SMALL
            act.wait_ge(pool_s, 1)
            act.dma_start(acc1[0:1, :], b_ada[0:1, 0:2 * D]).then_inc(bias1_in, 16)
            act.wait_ge(c_in, 16)
            sc.activation(ctmp[:], cvec[:], ACT.Exp, scale=-1.0).then_inc(ec_ready, 1)
            for b in range(8):
                act.wait_ge(xnT_full, b + 1)
                sc.copy(featT[:, 2 * b:2 * b + 2, :].rearrange("p k t -> p (k t)"), ps[:, b, :]).then_inc(xnT_copied, 1)
            act.wait_ge(acc_zeroed, 1)
            act.dma_start(acc2[0:1, :], b_ada[0:1, 2 * D:4 * D]).then_inc(bias2_in, 16)

            def split_heads(banks, tiles, scale):
                src = psf[:, banks * BN:(banks + 2) * BN]
                for half in (0, 1):
                    rows = slice(half * HD, (half + 1) * HD)
                    dst = queryT[rows, half, tiles:tiles + 4, :].rearrange("p a t -> p (a t)")
                    sc.mul(dst, src[rows, :], scale).then_inc(proj_taken, 1)

            def take(dst, src):
                sc.copy(dst, src).then_inc(proj_taken, 1)

            act.wait_ge(pool_s, POOL_SETUP)
            for gi in range(AB_GROUPS):
                bank = 2 * (gi % 2)
                act.wait_ge(pe_freed, group_done(gi))
                if gi == 0:
                    split_heads(bank, 0, 1.0)
                elif gi == 1:
                    act.wait_ge(ada_taken, 1)
                    take(keyT[:, K_A, :], ps[:, bank, 0:SEQ])
                    take(value[:, :, V_A:V_A + P], ps[:, bank + 1, 0:2 * P].rearrange("p (c n) -> p c n", c=TB))
                elif gi == 2:
                    split_heads(bank, 4, 1.0)
                elif gi == 3:
                    take(keyT[:, K_CMP, :], ps[:, bank, 0:SEQ])
                    take(keyT[:, V_CMP, :], ps[:, bank, SEQ:2 * SEQ])
                elif gi == 4:
                    take(keyT[:, K_SEL:K_WIN + 1, :].rearrange("p k t -> p (k t)"), ps[:, bank, :])
                    take(value[:, :, V_SEL:V_WIN + P], ps[:, bank + 1, :].rearrange("p (c n) -> p c n", c=TB))
            act.wait_ge(gate_mm, 1)
            sc.activation(gates[:].rearrange("p c h g -> p (c h g)"), ps[:, 7, 0:TB * 3 * HB], ACT.Exp,
                          scale=-1.0).then_inc(gate_e, 1)
            act.wait_ge(cmp_h_ready, 1)
            sc.activation(hidc[:, 2, :, :, 0:NCMP], hidc[:, 2, :, :, 0:NCMP], ACT.Exp, scale=-GELU_C).then_inc(cmp_e, 1)
            act.wait_ge(cmp_sm, 1)
            pc = work[:, 2048:2560].rearrange("p (a n) -> p a n", n=32)
            sc.activation(pc[:, :, 0:NCMP], pc[:, :, 0:NCMP], ACT.Exp).then_inc(cmp_ex, 1)
            for b in range(6):
                s = swork[b % 2]
                act.wait_ge(m_ready, b + 1)
                for blk, h, v in softmax_parts(s):
                    sc.activation(v, v, ACT.Exp, bias=nmx[:, b % 2, blk, h:h + 1],
                                  accum_out=den[:, b % 2, blk, h:h + 1]).then_inc(exp_done, 1)
                if b < 2:
                    sc.activation(den2[:, b], den2[:, b], ACT.Exp).then_inc(sink_done, 1)
                act.wait_ge(pt_full, b + 1)
                if b >= 1:
                    act.wait_ge(o_full, b)
                sc.copy(ptw, psf[:, 3 * BN:6 * BN]).then_inc(pt_taken, 1)
            act.wait_ge(acc_zeroed, 3)
            act.dma_start(acc3[0:1, :], b_ada[0:1, 4 * D:6 * D]).then_inc(bias3_in, 16)
            for gi in range(AB_GROUPS, len(WIN_GROUPS)):
                bank = 2 * (gi % 2)
                act.wait_ge(pe_freed, group_done(gi))
                r = gi - AB_GROUPS
                if r < 2:
                    split_heads(bank, 4 * r, SCALE)
                elif r < 4:
                    k0 = K_C + 4 * (r - 2)
                    for j in (0, 1):
                        take(keyT[:, k0 + 2 * j:k0 + 2 * j + 2, :].rearrange("p k t -> p (k t)"), ps[:, bank + j, :])
                else:
                    v0 = V_C + 512 * (r - 4)
                    for c in range(TB):
                        take(value[:, c, v0:v0 + 512], ps[:, bank + c, :])
            def log_part(b):
                s = swork[b % 2]
                act.wait_ge(z_done, b + 1)
                if b >= 2:
                    act.wait_ge(oc_full, b - 1)
                sc.activation(s, psf[:, (b % 2) * 3 * BN:(b % 2) * 3 * BN + 1536], ACT.Abs).then_inc(act_s, 1)
                act.wait_ge(act_s, 2 * b + 1)
                sc.activation(s, s, ACT.Exp, scale=-1.0).then_inc(act_s, 1)
                act.wait_ge(act_s, 2 * b + 2)
                sc.activation(s, s, ACT.Ln, bias=1.0).then_inc(l_done, 1)

            log_part(0)
            for b in range(HC // 4):
                if b + 1 < HC // 4:
                    log_part(b + 1)
                act.wait_ge(clamp_done, b + 1)
                sc.activation(swork[b % 2], swork[b % 2], ACT.Exp).then_inc(a_done, 1)
            act.wait_ge(oc_taken, HC // 4)
            for blk in range(TB):
                if blk:
                    act.wait_ge(sq_done, 3)
                for gi, (lo, hi) in enumerate(((0, 512), (512, 1024), (1024, 2048))):
                    sc.activation(work[:, lo:hi], merged[:, blk, lo:hi], ACT.Square,
                                  accum_out=ssq[:, blk, gi:gi + 1]).then_inc(sq_done, 1)
            act.wait_ge(mT_full, 8)
            act.dma_start(tokens[:], x.rearrange("(c p) d -> p c d", p=P)).then_inc(xr_in, 16)
            act.wait_ge(ada_taken, 5)
            act.dma_start(rowg, ln1_g[0:1, :].partition_broadcast(P)).then_inc(ln_in, 16)
            act.dma_start(rowb, ln1_b[0:1, :].partition_broadcast(P)).then_inc(ln_in, 16)
            for b in range(1, 8, 2):
                act.wait_ge(x2T_full, b + 1)
                for k in (2 * b, 2 * b + 1):
                    sc.activation(featT[:, k, :], ps[:, b, (k % 2) * SEQ:(k % 2 + 1) * SEQ], ACT.Identity,
                                  bias=cols[:, 2, k:k + 1], scale=cols[:, 3, k:k + 1]).then_inc(x2T_odd, 1)
            act.wait_ge(rexp_in, 1)
            sc.activation(rt[:, 0, :, 0:NG], rt[:, 0, :, 0:NG], ACT.Exp).then_inc(rexp_out, 1)
            act.wait_ge(rexp_in, 2)
            sc.activation(rt[:, 1, :, 0:EPG], rt[:, 1, :, 0:EPG], ACT.Exp).then_inc(rexp_out, 1)

            def pair_act(q, w):
                act.wait_ge(pe_freed, q * PAIR_UNITS + (PE_BASE + 16))
                sc.activation(e_gate, ps[:, 0, :], ACT.Exp, scale=-1.0).then_inc(e_ready, 1)
                act.wait_ge(pe_freed, q * PAIR_UNITS + (PE_BASE + 24))
                act.wait_ge(misc_full, q * MISC_PAIR + w * MISC_FLUSH + 12)
                sc.copy(y_pair, psf[:, 2 * BN:6 * BN]).then_inc(ysb_ready, 1)

            with act.Fori(0, PAIRS) as p:
                pair_act(p, 0)
            act.wait_ge(xn2_ready, 2)
            act.dma_start(rowg, ln2_g[0:1, :].partition_broadcast(P)).then_inc(ln_in, 16)
            act.dma_start(rowb, ln2_b[0:1, :].partition_broadcast(P)).then_inc(ln_in, 16)
            act.wait_ge(route_ready, PASSES)
            with act.Fori(1, PASSES) as w:
                go = act.value_load(more[0:1, bass.ds(w, 1)])
                with act.If(go > 0):
                    with act.Fori(0, PAIRS) as p:
                        pair_act(w * PAIRS + p, w)

        @block.tensor
        def _(pe):
            mm = pe.matmul
            pe.wait_ge(pool_s, POOL_CONST)
            pe.wait_ge(xn_ready, TB)
            for b in range(8):
                for k in (2 * b, 2 * b + 1):
                    for c in range(TB):
                        last = pe.transpose(ps[:, b, (k % 2) * SEQ + c * P:(k % 2) * SEQ + (c + 1) * P],
                                            tokens[:, c, k * P:(k + 1) * P], ident[:])
                last.then_inc(xnT_full, 1)

            def ada_columns(acc, bank):
                for k in range(acc.shape[1] // P):
                    last = mm(ps[:, bank, k:k + 1], acc[:, k * P:(k + 1) * P], ones[:, 0:1], start=True, stop=True)
                last.then_inc(ada_sums, 1)

            def ada_rows(acc, bank):
                for n in range(4):
                    last = mm(ps[:, bank + n, :], ones[:], acc[:, n * BN:(n + 1) * BN], start=True, stop=True)
                last.then_inc(ada_sums, 1)

            pe.wait_ge(xnT_copied, 8)
            pe.wait_ge(dve_freed, 2 * KC)
            ada_columns(acc1, 0)

            def project(gi):
                bank = 2 * (gi % 2)
                if gi >= 2:
                    pe.wait_ge(proj_taken, 2 * (gi - 1))
                width = WIN_GROUPS[gi][1]
                kn = UNIT // width
                for i in range(KC // kn):
                    n = index_of("win", gi, i)
                    arrived(pe, n)
                    slot = ring[:, n % SLOTS, :].rearrange("p (k n) -> p k n", k=kn)
                    for kk in range(kn):
                        k = i * kn + kk
                        first, final = k == 0, k == KC - 1
                        w = slot[:, kk, :]

                        def tile_T(lhsT, b, half):
                            return mm(ps[:, b, half * SEQ:(half + 1) * SEQ], lhsT, featT[:, k, :],
                                      start=first and half == 0, stop=final, skip_group_check=True)

                        if gi in (0, 2):
                            for j in range(4):
                                last = tile_T(w[:, j * P:(j + 1) * P], bank + j // 2, j % 2)
                        elif gi == 1:
                            tile_T(w[:, 0:P], bank, 0)
                            for c in range(TB):
                                last = mm(ps[:, bank + 1, c * P:(c + 1) * P], featT[:, k, c * P:(c + 1) * P],
                                          w[:, P:2 * P], start=first and c == 0, stop=final, skip_group_check=True)
                        elif gi == 3:
                            tile_T(w[:, 0:P], bank, 0)
                            last = tile_T(w[:, P:2 * P], bank, 1)
                        elif gi == 4:
                            tile_T(w[:, 0:P], bank, 0)
                            tile_T(w[:, 2 * P:3 * P], bank, 1)
                            vals = w.rearrange("p (s n) -> p s n", s=4)[:, 1:4:2, :]
                            for c in range(TB):
                                last = mm(ps[:, bank + 1, c * 2 * P:(c + 1) * 2 * P], featT[:, k, c * P:(c + 1) * P],
                                          vals, start=first and c == 0, stop=final, skip_group_check=True)
                        elif gi < AB_GROUPS + 4:
                            for j in range(4):
                                last = tile_T(w[:, j * P:(j + 1) * P], bank + j // 2, j % 2)
                        else:
                            for c in range(TB):
                                last = mm(ps[:, bank + c, :], featT[:, k, c * P:(c + 1) * P], w,
                                          start=first, stop=final)
                    last.then_inc(pe_freed, 1)

            pe.wait_ge(hT_ready, KC)
            pe.wait_ge(ada_taken, 1)
            for gi in range(AB_GROUPS):
                project(gi)
            pe.wait_ge(small_in, 16 * N_SMALL)
            for c in range(TB):
                for k in range(KC):
                    last = mm(ps[:, 7, c * 24:(c + 1) * 24], featT[:, k, c * P:(c + 1) * P], gbw[:, k, :],
                              start=k == 0, stop=k == KC - 1)
            last.then_inc(gate_mm, 1)
            pe.wait_ge(gate_e, 1)
            pe.wait_ge(dve_freed, 2 * 2 * KC)
            ada_rows(acc2[:, 0:D], 4)
            pe.wait_ge(ada_taken, 2)
            ada_columns(acc2[:, D:2 * D], 4)
            kpe = work[:, 0:2048].rearrange("p (s v g t) -> p s v g t", s=2, v=2, g=2)
            pe.wait_ge(cmp_in_ready, 8)
            pe.wait_ge(ada_taken, 3)
            for s in (0, 1):
                for l in range(CMP_LEN):
                    if l % 16 == 0:
                        n = index_of("w1", s, l // 16)
                        arrived(pe, n)
                    w1 = ring[:, n % SLOTS, :].rearrange("p (l h) -> p l h", l=16)[:, l % 16, :]
                    var = l // CMP_STEP
                    win = kpe[:, s, var].rearrange("p g (n j) -> p g n j", j=CMP_STEP)[:, :, var:var + NCMP, l % CMP_STEP]
                    last = mm(ps[:, 4 + s, 0:2 * NCMP], w1, win, start=l == 0, stop=l == CMP_LEN - 1)
                    if l % 16 == 15:
                        last.then_inc(pe_freed, 1)
            pe.wait_ge(cmp_act, 1)
            for g in (0, 1):
                mm(ps[g * HD:(g + 1) * HD, 6, 0:NCMP], w2[:, 0, :], hidc[:, 3, 0, g, 0:NCMP], start=True, stop=True)
            for g in (0, 1):
                for i in range(4):
                    last = mm(ps[32 * i:32 * i + NCMP, 7, g * HD:(g + 1) * HD], hidc[:, 3, 1, g, 0:NCMP], w2[:, 1, :],
                              start=True, stop=True)
            last.then_inc(cmp_kv, 1)
            pe.wait_ge(cmp_kv_taken, 5)
            for blk in range(TB):
                for h in range(HB):
                    last = mm(ps[:, 7, (blk * HB + h) * 16:(blk * HB + h) * 16 + NCMP],
                              queryT[:, h // 4, 4 + h % 4, blk * P:(blk + 1) * P], kcmpT[:, 0:NCMP], start=True, stop=True)
            last.then_inc(cmp_s, 1)
            pc = work[:, 2048:2560].rearrange("p (a n) -> p a n", a=4)
            pcT = work[:, 2560:3072].rearrange("p (a q) -> p a q", a=4)
            pe.wait_ge(cmp_p, 1)
            for a in range(4):
                last = pe.transpose(ps[:, 6, a * P:(a + 1) * P], pc[:, a, :], ident[:])
            last.then_inc(cmp_pt, 1)
            pe.wait_ge(cmp_pt_taken, 1)
            for a in range(4):
                last = mm(psf[:, 4 * BN + a * 256:4 * BN + (a + 1) * 256], pcT[:, a, :], vblk[:, a % 2, :],
                          start=True, stop=True)
            last.then_inc(cmp_o, 1)

            def scores(b):
                tiles, ktile = (0, K_A) if b < 2 else (4, (K_SEL, K_WIN)[(b - 2) // 2])
                g = b % 2
                if b >= 1:
                    pe.wait_ge(s_taken, b)
                for h in range(4):
                    q = queryT[:, g, tiles + h, :]
                    mm(psf[:, h * 256:(h + 1) * 256], q[:, P:2 * P], keyT[:, ktile, :], start=True, stop=True)
                    last = mm(psf[:, 2 * BN + h * P:2 * BN + (h + 1) * P], q[:, 0:P], keyT[:, ktile, 0:P],
                              start=True, stop=True)
                last.then_inc(s_done, 1)

            def weigh(b):
                s = swork[b % 2]
                v0 = (V_A, V_SEL, V_WIN)[b // 2] + (b % 2) * HD
                pe.wait_ge(exp_done, 8 * (b + 1))
                if b == 0:
                    pe.wait_ge(cmp_o_taken, 2)
                for n in range(12):
                    last = pe.transpose(psf[:, 3 * BN + n * P:3 * BN + (n + 1) * P], s[:, n * P:(n + 1) * P], ident[:])
                last.then_inc(pt_full, 1)
                pe.wait_ge(pt_taken, b + 1)
                if b >= 1:
                    pe.wait_ge(o_taken, b)
                for h in range(4):
                    mm(ps[:, 6, h * HD:(h + 1) * HD], ptw[:, (8 + h) * P:(9 + h) * P], value[:, 0, v0:v0 + HD],
                       start=True, stop=True)
                    for c in range(TB):
                        last = mm(ps[:, 6, 256 + h * HD:256 + (h + 1) * HD], ptw[:, (2 * h + c) * P:(2 * h + c + 1) * P],
                                  value[:, c, v0:v0 + HD], start=c == 0, stop=c == TB - 1)
                last.then_inc(o_full, 1)

            pe.wait_ge(proj_taken, 2 * AB_GROUPS)
            scores(0)
            for b in range(6):
                if b + 1 < 6:
                    scores(b + 1)
                weigh(b)

            pe.wait_ge(s_taken, 6)
            for gi in range(AB_GROUPS, len(WIN_GROUPS)):
                project(gi)
            pe.wait_ge(dve_freed, 3 * 2 * KC)
            ada_columns(acc3[:, 0:D], 4)
            pe.wait_ge(ada_taken, 4)
            ada_rows(acc3[:, D:2 * D], 4)
            pe.wait_ge(ada_taken, 5)
            pe.wait_ge(proj_taken, 2 * len(WIN_GROUPS))

            def z_scores(b):
                base = (b % 2) * 3 * BN
                if b >= 2:
                    pe.wait_ge(clamp_done, b - 1)
                for i in range(4):
                    tile, half = 2 * b + i // 2, i % 2
                    k = keyT[:, K_C + tile, :]
                    q = queryT[:, half, tile, :]
                    mm(psf[:, base + i * 256:base + (i + 1) * 256], k[:, 0:P], q, start=i % 2 == 0, stop=False,
                       skip_group_check=True)
                    last = mm(psf[:, base + 1024 + i * P:base + 1024 + (i + 1) * P], k[:, P:2 * P], q[:, P:2 * P],
                              start=i == 0, stop=False, skip_group_check=True)
                last.then_inc(z_done, 1)

            def suffix_sums(b):
                base = (b % 2) * 3 * BN
                s = swork[b % 2]
                pe.wait_ge(lmask, 2 * (b + 1))
                for n in range(3):
                    mm(psf[:, base + n * BN:base + (n + 1) * BN], neg_tri[:], s[:, n * BN:(n + 1) * BN],
                       start=False, stop=False, skip_group_check=True)
                for n in range(2):
                    dst = psf[:, base + n * BN:base + (n + 1) * BN].rearrange("p (h q) -> p h q", h=2)[:, :, P:2 * P]
                    src = s[:, 1024 + n * 256:1024 + (n + 1) * 256].rearrange("p (h q) -> p h q", h=2)
                    last = mm(dst, neg_ones[:], src, start=False, stop=True, skip_group_check=True)
                last.then_inc(zr_done, 1)

            def stick_values(b):
                s = swork[b % 2]
                bank = 6 + b % 2
                pe.wait_ge(a_masked, 2 * (b + 1))
                if b >= 2:
                    pe.wait_ge(oc_taken, b - 1)
                for i in range(4):
                    v0 = V_C + (4 * b + i) * HD
                    mm(ps[:, bank, i * HD:(i + 1) * HD], s[:, i * 256:i * 256 + P], value[:, 0, v0:v0 + HD],
                       start=True, stop=True)
                    mm(ps[:, bank, 256 + i * HD:256 + (i + 1) * HD], s[:, i * 256 + P:(i + 1) * 256],
                       value[:, 0, v0:v0 + HD], start=True, stop=False)
                    last = mm(ps[:, bank, 256 + i * HD:256 + (i + 1) * HD], s[:, 1024 + i * P:1024 + (i + 1) * P],
                              value[:, 1, v0:v0 + HD], start=False, stop=True)
                last.then_inc(oc_full, 1)

            z_scores(0)
            for b in range(HC // 4):
                if b + 1 < HC // 4:
                    z_scores(b + 1)
                suffix_sums(b)
                stick_values(b)

            pe.wait_ge(merged_ready, 6)
            for b in range(8):
                for k in (2 * b, 2 * b + 1):
                    for c in range(TB):
                        last = pe.transpose(ps[:, b, (k % 2) * SEQ + c * P:(k % 2) * SEQ + (c + 1) * P],
                                            merged[:, c, k * P:(k + 1) * P], ident[:])
                last.then_inc(mT_full, 1)
            pe.wait_ge(mT_ready, KC)
            for k in range(KC):
                n = index_of("wout", k, 0)
                arrived(pe, n)
                for c in range(TB):
                    for j in range(4):
                        last = mm(ps[:, 4 * c + j, :], featT[:, k, c * P:(c + 1) * P],
                                  ring[:, n % SLOTS, j * BN:(j + 1) * BN], start=k == 0, stop=k == KC - 1)
                last.then_inc(pe_freed, 1)

            pe.wait_ge(xn2_ready, TB)
            for b in range(8):
                for k in (2 * b, 2 * b + 1):
                    for c in range(TB):
                        last = pe.transpose(ps[:, b, (k % 2) * SEQ + c * P:(k % 2) * SEQ + (c + 1) * P],
                                            xn2[:, c, k * P:(k + 1) * P], ident[:])
                last.then_inc(x2T_full, 1)
            pe.wait_ge(x2T_even, 8)
            pe.wait_ge(x2T_odd, 8)
            for c in range(TB):
                for k in range(KC):
                    last = mm(ps[:, 0, c * 36:(c + 1) * 36], featT[:, k, c * P:(c + 1) * P], wr[:, k, :],
                              start=k == 0, stop=k == KC - 1)
            last.then_inc(route_mm, 1)
            routed = rt[:, 2]
            pe.wait_ge(rtab_ready, 1)
            mm(ps[:, 1, 0:NE], before[:], routed[:, 0, :], start=True, stop=True)
            mm(ps[:, 1, NE:2 * NE], ones[:], routed[:, 0, :], start=True, stop=False)
            mm(ps[:, 1, NE:2 * NE], before[:], routed[:, 1, :], start=False, stop=True)
            mm(ps[:, 1, 2 * NE:3 * NE], ones[:], routed[:, 0, :], start=True, stop=False)
            mm(ps[:, 1, 2 * NE:3 * NE], ones[:], routed[:, 1, :], start=False, stop=True).then_inc(rank_full, 1)

            def scatter_pair(use):
                for c in range(TB):
                    for n in range(4):
                        mm(use(), scatter[:, c * P:(c + 1) * P], y_pair[:, n * BN:(n + 1) * BN],
                           start=True, stop=True).then_inc(misc_full, 1)

            def misc(turn):
                count = [0]

                def use():
                    count[0] += 1
                    pe.wait_ge(misc_free, turn + count[0])
                    return ps[:, 6 + (count[0] - 1) % 2, :]
                return use

            def pair_pe(q, w):
                turn = q * MISC_PAIR + w * MISC_FLUSH
                use = misc(turn)
                pe.wait_ge(sel_ready, q + 1)
                for b in range(4):
                    bank = use()
                    for k in range(4 * b, 4 * b + 4):
                        for c in range(TB):
                            last = mm(bank[:, (k % 4) * P:(k % 4 + 1) * P], xn2[:, c, k * P:(k + 1) * P],
                                      sel[:, c].rearrange("p e s -> p (e s)"), start=c == 0, stop=c == TB - 1)
                    last.then_inc(misc_full, 1)
                pe.wait_ge(misc_free, turn + 6)
                pe.wait_ge(hid_ready, q)
                for quarter in range(4):
                    for m in (0, 1):
                        j = 4 * quarter + 2 * m
                        for e in (0, 1):
                            pe.wait_ge(full[pair_slot(j + e)], q * (16 * PAIR_UNITS // SLOTS) + pair_value(j + e))
                        for kk in range(4):
                            k = 4 * quarter + kk
                            for e in (0, 1):
                                last = mm(ps[e * WIN:(e + 1) * WIN, m, :], x_pair[:, k, e * WIN:(e + 1) * WIN],
                                          ring[:, pair_slot(j + e), kk * BN:(kk + 1) * BN],
                                          start=k == 0, stop=k == KC - 1)
                                if kk == 3:
                                    last.then_inc(pe_freed, 1)
                pe.wait_ge(ysb_ready, q)
                scatter_pair(use)
                pe.wait_ge(selg_ready, q + 1)
                bank = use()
                for c in range(TB):
                    last = pe.transpose(bank[:, c * P:(c + 1) * P], selg[:, c].rearrange("p e s -> p (e s)"), ident[:])
                last.then_inc(misc_full, 1)
                pe.wait_ge(hid_ready, q + 1)
                bank = use()
                for k in range(DE // P):
                    last = pe.transpose(bank[:, k * P:(k + 1) * P], hid[:, k * P:(k + 1) * P], ident[:])
                last.then_inc(misc_full, 1)
                pe.wait_ge(misc_free, turn + 16)
                for k in range(DE // P):
                    j = 16 + 2 * k
                    for e in (0, 1):
                        pe.wait_ge(full[pair_slot(j + e)], q * (16 * PAIR_UNITS // SLOTS) + pair_value(j + e))
                    for n in range(4):
                        for e in (0, 1):
                            last = mm(ps[e * WIN:(e + 1) * WIN, 2 + n, :],
                                      hidT[:, k * P + e * WIN:k * P + (e + 1) * WIN],
                                      ring[:, pair_slot(j + e), n * BN:(n + 1) * BN],
                                      start=k == 0, stop=k == DE // P - 1)
                            if n == 3:
                                last.then_inc(pe_freed, 1)

            def flush_pe(w):
                use = misc((w + 1) * (PAIRS * MISC_PAIR) + w * MISC_FLUSH)
                pe.wait_ge(ysb_ready, (w + 1) * PAIRS)
                pe.wait_ge(misc_free, (w + 1) * (PAIRS * MISC_PAIR) + w * MISC_FLUSH + 1)
                scatter_pair(use)

            with pe.Fori(0, PAIRS) as p:
                pair_pe(p, 0)
            flush_pe(0)
            pe.wait_ge(route_ready, PASSES)
            with pe.Fori(1, PASSES) as w:
                go = pe.value_load(more[0:1, bass.ds(w, 1)])
                with pe.If(go > 0):
                    with pe.Fori(0, PAIRS) as p:
                        pair_pe(w * PAIRS + p, w)
                    flush_pe(w)

        @block.vector
        def _(dve):
            st = Steps(dve, dve_s)
            freed = [0]

            def ada(count, acc, first):
                units = [n for n, u in enumerate(UNITS) if u[3] == "dve"][freed[0]:freed[0] + count]
                for n in units:
                    k, half = UNITS[n][1:3]
                    arrived(dve, n)
                    if freed[0] >= first + 2:
                        dve.wait_ge(dve_freed, freed[0] - 1)
                    dst = acc[:, (half % 2) * D:(half % 2 + 1) * D]
                    dve.scalar_tensor_tensor(out=dst, in0=ring[:, n % SLOTS, :], scalar=cs[:, k:k + 1], in1=dst,
                                             op0=ALU.mult, op1=ALU.add).then_inc(dve_freed, 1)
                    freed[0] += 1

            norms = [0]

            def normalise(src, dst, c):
                for n in range(4):
                    st(dve.bn_stats(stats[:, c, n, :], src[:, n * BN:(n + 1) * BN]))
                st.wait()
                st(dve.bn_aggr(mv[:, c, :], stats[:, c].rearrange("p n s -> p (n s)")))
                st.wait()
                dve.tensor_scalar(rstd[:, c:c + 1], mv[:, c, 1:2], 1e-5, None, ALU.add).then_inc(var_ready, 1)
                norms[0] += 1
                dve.wait_ge(rstd_ready, norms[0])
                return dve.tensor_scalar(dst, src, mv[:, c, 0:1], rstd[:, c:c + 1], ALU.subtract, ALU.mult)

            dve.wait_ge(x_in, 16)
            for c in range(TB):
                normalise(tokens[:, c, :], tokens[:, c, :], c).then_inc(xn_ready, 1)
            dve.wait_ge(ec_ready, 1)
            st(dve.tensor_scalar(ctmp[:], ctmp[:], 1.0, None, ALU.add))
            st.wait()
            st(dve.reciprocal(ctmp[:], ctmp[:]))
            st.wait()
            st(dve.tensor_tensor(cs[:], cvec[:], ctmp[:], ALU.mult))
            st.wait()
            dve.wait_ge(bias1_in, 16)
            ada(2 * KC, acc1, 0)
            dve.wait_ge(ada_sums, 1)
            st(dve.tensor_copy(cols[:, 0, :], ps[:, 0, 0:KC]))
            dve.tensor_scalar(cols[:, 1, :], ps[:, 0, KC:2 * KC], 1.0, None, ALU.add).then_inc(ada_taken, 1)
            st.wait()
            dve.wait_ge(ada_taken, 1)
            dve.wait_ge(xnT_copied, 8)
            for k in range(KC):
                dve.tensor_scalar(featT[:, k, :], featT[:, k, :], cols[:, 1, k:k + 1], cols[:, 0, k:k + 1],
                                  ALU.mult, ALU.add).then_inc(hT_ready, 1)
            dve.wait_ge(acc_zeroed, 1)
            dve.wait_ge(bias2_in, 16)
            ada(2 * KC, acc2, 2 * KC)
            dve.wait_ge(ada_sums, 2)
            dve.tensor_scalar(g1b[:], psf[:, 4 * BN:8 * BN], 1.0, None, ALU.add).then_inc(ada_taken, 1)
            dve.wait_ge(ada_sums, 3)
            dve.tensor_copy(cols[:, 2, :], ps[:, 4, 0:KC]).then_inc(ada_taken, 1)
            kpe = work[:, 0:2048].rearrange("p (s v g t) -> p s v g t", s=2, v=2, g=2)
            dve.wait_ge(acc_zeroed, 2)
            dve.wait_ge(small_in, 16 * N_SMALL)
            dve.wait_ge(proj_taken, 8)
            for s in (0, 1):
                for v in (0, 1):
                    for g in (0, 1):
                        rows = slice(g * HD, (g + 1) * HD)
                        pe16 = pe2[rows, s, v * 16:(v + 1) * 16].unsqueeze(1).broadcast_to([HD, 16, 16])
                        dve.tensor_tensor(kpe[rows, s, v, g].rearrange("p (n j) -> p n j", n=16),
                                          keyT[rows, K_CMP + s, :].rearrange("p (n j) -> p n j", n=16), pe16,
                                          ALU.add).then_inc(cmp_in_ready, 1)
            H = [hidc[:, i, :, :, 0:NCMP] for i in range(4)]
            dve.wait_ge(pe_freed, freed_after("w1", 1, 1))
            st(dve.tensor_copy(H[0], ps[:, 4:6, 0:2 * NCMP].rearrange("p s (g n) -> p s g n", g=2)))
            st.wait()
            st(dve.tensor_tensor(H[1], H[0], H[0], ALU.mult))
            st.wait()
            st(dve.tensor_scalar(H[1], H[1], 0.044715, 1.0, ALU.mult, ALU.add))
            st.wait()
            dve.tensor_tensor(H[2], H[1], H[0], ALU.mult).then_inc(cmp_h_ready, 1)
            pc = work[:, 2048:2560]
            st(dve.memset(pc, 0.0))
            dve.wait_ge(cmp_e, 1)
            st(dve.tensor_scalar(H[1], H[2], 1.0, None, ALU.add))
            st.wait()
            st(dve.reciprocal(H[1], H[1]))
            st.wait()
            dve.tensor_tensor(H[3], H[0], H[1], ALU.mult).then_inc(cmp_act, 1)
            dve.wait_ge(cmp_kv, 1)
            dve.tensor_copy(kcmpT[:, 0:NCMP], ps[:, 6, 0:NCMP]).then_inc(cmp_kv_taken, 1)
            for i in range(4):
                rows = slice(32 * i, 32 * i + NCMP)
                dve.tensor_copy(vblk[rows, :, i * HD:(i + 1) * HD],
                                ps[rows, 7, 0:2 * HD].rearrange("p (g d) -> p g d", g=2)).then_inc(cmp_kv_taken, 1)
            pcv = pc.rearrange("p (a n) -> p a n", n=32)[:, :, 0:NCMP]
            sv = ps[:, 7, 0:256].rearrange("p (a n) -> p a n", n=16)[:, :, 0:NCMP]
            dve.wait_ge(cmp_s, 1)
            st(dve.scalar_tensor_tensor(out=pcv, in0=sv, scalar=SCALE, in1=cmp_bias[:].rearrange("p c h n -> p (c h) n"),
                                        op0=ALU.mult, op1=ALU.add))
            st.wait()
            st(dve.tensor_reduce(cst[:, 0, :], pcv, AX.X, ALU.max))
            st.wait()
            wide = [P, TB * HB, NCMP]
            dve.tensor_tensor(pcv, pcv, cst[:, 0, :].unsqueeze(2).broadcast_to(wide), ALU.subtract).then_inc(cmp_sm, 1)
            dve.wait_ge(cmp_ex, 1)
            dve.tensor_tensor(pcv, pcv, cmp_mask[:], ALU.mult).then_inc(cmp_p, 1)
            dve.wait_ge(cmp_p, 1)
            st(dve.tensor_reduce(cst[:, 1, :], pcv, AX.X, ALU.add))
            dve.wait_ge(gate_e, 1)
            gf = gates[:].rearrange("p c h g -> p (c h g)")
            st(dve.tensor_scalar(gf, gf, 1.0, None, ALU.add))
            st.wait()
            st(dve.reciprocal(gf, gf))
            st(dve.tensor_scalar(cst[:, 2, :], cst[:, 1, :], 1e-30, None, ALU.max))
            st.wait()
            st(dve.reciprocal(cst[:, 2, :], cst[:, 2, :]))
            st.wait()
            st(dve.tensor_tensor(cst[:, 3, :], cst[:, 2, :], gates[:].rearrange("p c h g -> p (c h) g")[:, :, 0], ALU.mult))
            dve.wait_ge(cmp_pt, 1)
            dve.tensor_copy(work[:, 2560:3072], ps[:, 6, :]).then_inc(cmp_pt_taken, 1)
            st.wait()
            dve.wait_ge(cmp_o, 1)
            for c in range(TB):
                o = psf[:, (4 + c) * BN:(5 + c) * BN].rearrange("p (h d) -> p h d", h=HB)
                r = cst[:, 3, c * HB:(c + 1) * HB].unsqueeze(2).broadcast_to([P, HB, HD])
                dve.tensor_tensor(merged[:, c, 512:1024].rearrange("p (h d) -> p h d", h=HB), o, r,
                                  ALU.mult).then_inc(cmp_o_taken, 1)

            def front(b):
                s, m, nm = swork[b % 2], mx[:, b % 2], nmx[:, b % 2]
                h0 = (0 if b < 2 else HA) + (b % 2) * 4
                dve.wait_ge(s_done, b + 1)
                X, Y = s[:, 0:1024].rearrange("p (h k) -> p h k", h=4), s[:, 1024:1536].rearrange("p (h k) -> p h k", h=4)
                st(dve.scalar_tensor_tensor(out=X, in0=psf[:, 0:1024].rearrange("p (h k) -> p h k", h=4), scalar=SCALE,
                                            in1=biasX[:, h0:h0 + 4, :], op0=ALU.mult, op1=ALU.add))
                dve.scalar_tensor_tensor(out=Y, in0=psf[:, 1024:1536].rearrange("p (h k) -> p h k", h=4), scalar=SCALE,
                                         in1=biasY[:, h0:h0 + 4, :], op0=ALU.mult, op1=ALU.add).then_inc(s_taken, 1)
                st.wait()
                st(dve.tensor_reduce(m[:, 1, :], X, AX.X, ALU.max))
                dve.wait_ge(s_taken, b + 1)
                st(dve.tensor_reduce(m[:, 0, :], Y, AX.X, ALU.max))
                st.wait()
                if b < 2:
                    sink = sinkb[:, 4 * b:4 * b + 4].unsqueeze(1).broadcast_to([P, TB, 4])
                    st(dve.tensor_tensor(m, m, sink, ALU.max))
                    st.wait()
                    st(dve.tensor_tensor(den2[:, b], sink, m, ALU.subtract))
                    st.wait()
                dve.tensor_scalar(nm, m, -1.0, None, ALU.mult).then_inc(m_ready, 1)

            def back(b):
                s, dn = swork[b % 2], den[:, b % 2]
                dve.wait_ge(exp_done, 8 * (b + 1))
                if b < 2:
                    dve.wait_ge(sink_done, b + 1)
                    st(dve.tensor_tensor(dn, dn, den2[:, b], ALU.add))
                    st.wait()
                st(dve.reciprocal(dn, dn))
                st.wait()
                if b >= 2:
                    gate = gates[:, :, (b % 2) * 4:(b % 2) * 4 + 4, 1 + (b - 2) // 2]
                    st(dve.tensor_tensor(dn, dn, gate, ALU.mult))
                    st.wait()
                r = dn.unsqueeze(3).broadcast_to([P, TB, 4, HD])
                o = ps[:, 6, :].rearrange("p (c h d) -> p c h d", c=TB, h=4)
                n0 = (0 if b < 2 else 512) + (b % 2) * 256
                dst = merged[:, :, n0:n0 + 256].rearrange("p c (h d) -> p c h d", h=4)
                dve.wait_ge(o_full, b + 1)
                if b < 2:
                    dve.tensor_tensor(dst, o, r, ALU.mult).then_inc(o_taken, 1)
                else:
                    tmp = s[:, 0:512].rearrange("p (c h d) -> p c h d", c=TB, h=4)
                    dve.tensor_tensor(tmp, o, r, ALU.mult).then_inc(o_taken, 1)
                    dve.wait_ge(o_taken, b + 1)
                    st(dve.tensor_tensor(dst, dst, tmp, ALU.add))
                    st.wait()

            dve.wait_ge(cmp_o_taken, 2)
            front(0)
            for b in range(6):
                if b + 1 < 6:
                    front(b + 1)
                back(b)
            dve.wait_ge(acc_zeroed, 3)
            dve.wait_ge(bias3_in, 16)
            ada(2 * KC, acc3, 4 * KC)
            dve.wait_ge(ada_sums, 4)
            dve.tensor_scalar(cols[:, 3, :], ps[:, 4, 0:KC], 1.0, None, ALU.add).then_inc(ada_taken, 1)
            dve.wait_ge(ada_sums, 5)
            dve.tensor_scalar(g2b[:], psf[:, 4 * BN:8 * BN], 1.0, None, ALU.add).then_inc(ada_taken, 1)

            def softplus(b):
                s = swork[b % 2]
                dve.wait_ge(l_done, b + 1)
                dve.scalar_tensor_tensor(out=s, in0=psf[:, (b % 2) * 1536:(b % 2 + 1) * 1536], scalar=0.0, in1=s,
                                         op0=ALU.max, op1=ALU.add).then_inc(sp_done, 1)

            def take_sticks(b):
                dve.wait_ge(oc_full, b + 1)
                dve.tensor_copy(merged[:, :, 1024 + b * 256:1024 + (b + 1) * 256],
                                ps[:, 6 + b % 2, :].rearrange("p (c n) -> p c n", c=TB)).then_inc(oc_taken, 1)

            softplus(0)
            for b in range(HC // 4):
                if b + 1 < HC // 4:
                    softplus(b + 1)
                dve.wait_ge(zr_done, b + 1)
                dve.tensor_scalar(swork[b % 2], psf[:, (b % 2) * 1536:(b % 2 + 1) * 1536], 0.0, None,
                                  ALU.min).then_inc(clamp_done, 1)
                if b >= 1:
                    take_sticks(b - 1)
            take_sticks(HC // 4 - 1)

            dve.wait_ge(sq_done, 3 * TB)
            dve.tensor_scalar(ssq[:, :, 0:2], ssq[:, :, 0:2], 1.0 / 512, 1e-6, ALU.mult, ALU.add)
            dve.tensor_scalar(ssq[:, :, 2:3], ssq[:, :, 2:3], 1.0 / 1024, 1e-6, ALU.mult, ALU.add).then_inc(var_ready, 1)
            norms[0] += 1
            dve.wait_ge(rstd_ready, norms[0])
            for c in range(TB):
                for gi, (lo, hi) in enumerate(((0, 512), (512, 1024), (1024, 2048))):
                    dve.tensor_scalar(merged[:, c, lo:hi], merged[:, c, lo:hi], ssq[:, c, gi:gi + 1], None,
                                      ALU.mult).then_inc(merged_ready, 1)
            for k in range(KC):
                dve.wait_ge(mT_full, k // 2 + 1)
                dve.tensor_scalar(featT[:, k, :], ps[:, k // 2, (k % 2) * SEQ:(k % 2 + 1) * SEQ], gaincol[:, k:k + 1],
                                  None, ALU.mult).then_inc(mT_ready, 1)
            dve.wait_ge(pe_freed, PE_BASE)
            dve.wait_ge(xr_in, 16)
            dve.wait_ge(ln_in, 32)

            def residual_norm(c, branch, gate):
                st(dve.tensor_tensor(xn2[:, c, :], branch, gate, ALU.mult))
                st.wait()
                st(dve.scalar_tensor_tensor(out=tokens[:, c, :], in0=tokens[:, c, :], scalar=ALPHA, in1=xn2[:, c, :],
                                            op0=ALU.mult, op1=ALU.add))
                st.wait()
                st(normalise(tokens[:, c, :], tokens[:, c, :], c))
                st.wait()
                st(dve.tensor_tensor(tokens[:, c, :], tokens[:, c, :], rowg, ALU.mult))
                st.wait()
                return dve.tensor_tensor(tokens[:, c, :], tokens[:, c, :], rowb, ALU.add)

            for c in range(TB):
                st(residual_norm(c, psf[:, 4 * c * BN:4 * (c + 1) * BN], g1b[:]))
                st.wait()
                normalise(tokens[:, c, :], xn2[:, c, :], c).then_inc(xn2_ready, 1)
            for b in range(0, 8, 2):
                dve.wait_ge(x2T_full, b + 1)
                for k in (2 * b, 2 * b + 1):
                    dve.tensor_scalar(featT[:, k, :], ps[:, b, (k % 2) * SEQ:(k % 2 + 1) * SEQ], cols[:, 3, k:k + 1],
                                      cols[:, 2, k:k + 1], ALU.mult, ALU.add).then_inc(x2T_even, 1)

            dve.wait_ge(route_mm, 1)
            st(dve.tensor_tensor(lg[:], ps[:, 0, 0:TB * (NG + NE)].rearrange("p (c n) -> p c n", c=TB),
                                 brow[:].unsqueeze(1).broadcast_to([P, TB, NG + NE]), ALU.add))
            st.wait()

            def bc(v, n):
                return v.unsqueeze(2).broadcast_to([P, TB, n])

            def first_max(values, n, top, onehot, tmp, index):
                st(dve.tensor_reduce(top, values, AX.X, ALU.max))
                st.wait()
                st(dve.tensor_tensor(tmp, values, bc(top, n), ALU.not_equal))
                st.wait()
                st(dve.scalar_tensor_tensor(out=tmp, in0=tmp, scalar=64.0,
                                            in1=number[:, 0:n].unsqueeze(1).broadcast_to([P, TB, n]),
                                            op0=ALU.mult, op1=ALU.add))
                st.wait()
                st(dve.tensor_reduce(index, tmp, AX.X, ALU.min))
                st.wait()
                st(dve.tensor_tensor(onehot, number[:, 0:n].unsqueeze(1).broadcast_to([P, TB, n]), bc(index, n),
                                     ALU.is_equal))
                st.wait()

            def T(i, n):
                return rt[:, i, :, 0:n]

            number = slot_id[:, 0, :]
            glog = lg[:, :, 0:NG]
            gmax, gidx, psum_g, m8, v1, i1, v2, i2, tot, cnt = (r1[:, i, :] for i in range(10))
            first_max(glog, NG, gmax, T(3, NG), T(4, NG), gidx)
            dve.tensor_tensor(T(0, NG), glog, bc(gmax, NG), ALU.subtract).then_inc(rexp_in, 1)
            gone = T(3, NG)
            prod = T(5, NE).rearrange("p c (g e) -> p c g e", g=NG)
            st(dve.tensor_tensor(prod, lg[:, :, NG:].rearrange("p c (g e) -> p c g e", g=NG),
                                 gone.unsqueeze(3).broadcast_to([P, TB, NG, EPG]), ALU.mult))
            st.wait()
            st(dve.tensor_reduce(T(6, EPG), T(5, NE).rearrange("p c (g e) -> p c e g", g=NG), AX.X, ALU.add))
            st.wait()
            st(dve.tensor_reduce(m8, T(6, EPG), AX.X, ALU.max))
            st.wait()
            dve.tensor_tensor(T(1, EPG), T(6, EPG), bc(m8, EPG), ALU.subtract).then_inc(rexp_in, 1)
            dve.wait_ge(rexp_out, 1)
            st(dve.tensor_reduce(psum_g, T(0, NG), AX.X, ALU.add))
            st.wait()
            dve.wait_ge(rexp_out, 2)
            first_max(T(1, EPG), EPG, v1, T(7, EPG), T(4, EPG), i1)
            st(dve.scalar_tensor_tensor(out=T(8, EPG), in0=T(7, EPG), scalar=-2.0, in1=T(1, EPG), op0=ALU.mult, op1=ALU.add))
            st.wait()
            first_max(T(8, EPG), EPG, v2, T(9, EPG), T(4, EPG), i2)
            st(dve.tensor_tensor(tot, v1, v2, ALU.add))
            st.wait()
            st(dve.tensor_tensor(tot, tot, psum_g, ALU.mult))
            st.wait()
            st(dve.reciprocal(tot, tot))
            st.wait()
            st(dve.tensor_tensor(v1, v1, tot, ALU.mult))
            st(dve.tensor_tensor(v2, v2, tot, ALU.mult))
            st.wait()
            st(dve.tensor_tensor(T(10, EPG), T(7, EPG), bc(v1, EPG), ALU.mult))
            st(dve.tensor_tensor(T(11, EPG), T(9, EPG), bc(v2, EPG), ALU.mult))
            st.wait()
            st(dve.tensor_tensor(T(10, EPG), T(10, EPG), T(11, EPG), ALU.add))
            st(dve.tensor_tensor(T(7, EPG), T(7, EPG), T(9, EPG), ALU.add))
            st.wait()
            for dst, per, done in ((gate_te[:], T(10, EPG), None), (T(2, NE), T(7, EPG), rtab_ready)):
                for g in range(NG):
                    ins = dve.tensor_tensor(dst[:, :, g * EPG:(g + 1) * EPG], per, bc(T(3, NG)[:, :, g], EPG), ALU.mult)
                    if done is not None and g == NG - 1:
                        ins.then_inc(done, 1)
                    else:
                        st(ins)
            st(dve.memset(ysum, 0.0))
            dve.memset(y_pair, 0.0).then_inc(misc_free, 1)
            dve.memset(scatter, 0.0).then_inc(misc_free, 1)
            dve.wait_ge(rank_full, 1)
            dve.wait_ge(rtab_ready, 1)
            st(dve.scalar_tensor_tensor(out=rankm[:], in0=ps[:, 1, 0:2 * NE].rearrange("p (c e) -> p c e", c=TB),
                                        scalar=1.0, in1=T(2, NE), op0=ALU.add, op1=ALU.mult))
            st(dve.tensor_reduce(cnt[:, 0:1], ps[:, 1, 2 * NE:3 * NE], AX.X, ALU.max))
            st.wait()
            st(dve.tensor_scalar(rankm[:], rankm[:], -1.0, None, ALU.add))
            for w in range(PASSES):
                dve.tensor_scalar(more[:, w:w + 1], cnt[:, 0:1], float(WIN * w), None,
                                  ALU.is_gt).then_inc(route_ready, 1)
            dve.wait_ge(misc_free, 2)
            st.wait()

            mo = Steps(dve, moe_s)

            def scatter_add(full_at):
                for i in range(8):
                    dst = ysum[:, i // 4, (i % 4) * BN:(i % 4 + 1) * BN]
                    dve.wait_ge(misc_full, full_at + (i + 1))
                    dve.tensor_tensor(dst, dst, ps[:, 6 + i % 2, :], ALU.add).then_inc(misc_free, 1)

            def pair_dve(p, q, w):
                turn = q * MISC_PAIR + w * MISC_FLUSH
                mo.turn, mo.n = q * MOE_STEPS + w * MOE_FLUSH_STEPS, 0
                two = [P, TB, 2, WIN]
                ranks = rankm[:, :, bass.ds(p * 2, 2)].unsqueeze(3).broadcast_to(two)
                weights = gate_te[:, :, bass.ds(p * 2, 2)].unsqueeze(3).broadcast_to(two)
                mo.wait()
                dve.tensor_tensor(sel, slot_id[:].unsqueeze(1).broadcast_to(two), ranks,
                                  ALU.is_equal).then_inc(sel_ready, 1)
                dve.wait_ge(sel_ready, q + 1)
                dve.tensor_tensor(selg, sel, weights, ALU.mult).then_inc(selg_ready, 1)
                dve.wait_ge(pe_freed, q * PAIR_UNITS + (PE_BASE + 16 - PAIR_UNITS))
                for b in range(4):
                    dve.wait_ge(misc_full, turn + (b + 1))
                    for k in range(4 * b, 4 * b + 4):
                        ins = dve.tensor_scalar(x_pair[:, k, :], ps[:, 6 + b % 2, (k % 4) * P:(k % 4 + 1) * P],
                                                cols[:, 3, k:k + 1], cols[:, 2, k:k + 1], ALU.mult, ALU.add)
                    ins.then_inc(misc_free, 1)
                dve.wait_ge(e_ready, q + 1)
                mo(dve.tensor_scalar(e_gate, e_gate, 1.0, None, ALU.add))
                mo.wait()
                mo(dve.reciprocal(e_gate, e_gate))
                mo.wait()
                mo(dve.tensor_tensor(e_gate, e_gate, ps[:, 0, :], ALU.mult))
                mo.wait()
                dve.tensor_tensor(hid, e_gate, ps[:, 1, :], ALU.mult).then_inc(hid_ready, 1)
                scatter_add(turn + 4)
                dve.wait_ge(misc_full, turn + 13)
                dve.tensor_copy(scatter, ps[:, 6, 0:SEQ]).then_inc(misc_free, 1)
                dve.wait_ge(misc_full, turn + 14)
                dve.wait_ge(pe_freed, q * PAIR_UNITS + PE_BASE)
                dve.tensor_copy(hidT, ps[:, 7, :]).then_inc(misc_free, 1)
                assert mo.n == MOE_STEPS, mo.n

            def flush_dve(w):
                mo.turn, mo.n = (w + 1) * (PAIRS * MOE_STEPS) + w * MOE_FLUSH_STEPS, 0
                turn = (w + 1) * (PAIRS * MISC_PAIR) + w * MISC_FLUSH
                scatter_add(turn)
                dve.wait_ge(misc_free, turn + 10)
                mo(dve.memset(scatter, 0.0))
                mo(dve.tensor_scalar(rankm[:], rankm[:], -float(WIN), None, ALU.add))
                assert mo.n == MOE_FLUSH_STEPS, mo.n

            with dve.Fori(0, PAIRS) as p:
                pair_dve(p, p, 0)
            flush_dve(0)
            with dve.Fori(1, PASSES) as w:
                go = dve.value_load(more[0:1, bass.ds(w, 1)])
                with dve.If(go > 0):
                    with dve.Fori(0, PAIRS) as p:
                        pair_dve(p, w * PAIRS + p, w)
                    flush_dve(w)

            st.sem, st.n = fin_s, 0
            dve.wait_ge(ln_in, 64)
            for c in range(TB):
                st(dve.tensor_tensor(xn2[:, c, :], ysum[:, c, :], g2b[:], ALU.mult))
                st.wait()
                st(dve.scalar_tensor_tensor(out=tokens[:, c, :], in0=tokens[:, c, :], scalar=ALPHA, in1=xn2[:, c, :],
                                            op0=ALU.mult, op1=ALU.add))
                st.wait()
                st(normalise(tokens[:, c, :], tokens[:, c, :], c))
                st.wait()
                st(dve.tensor_tensor(tokens[:, c, :], tokens[:, c, :], rowg, ALU.mult))
                st.wait()
                dve.tensor_tensor(tokens[:, c, :], tokens[:, c, :], rowb, ALU.add).then_inc(out_ready, 1)


def softmax_parts(s):
    for h in range(4):
        yield 1, h, s[:, h * 256:(h + 1) * 256]
    for h in range(4):
        yield 0, h, s[:, 1024 + h * P:1024 + (h + 1) * P]


def kernel(x, c, w_ada, b_ada, w_in, sinks, cmp_pe_k, cmp_w1_k, cmp_w2_k, cmp_pe_v, cmp_w1_v, cmp_w2_v,
           mix_gain, w_out, ln1_g, ln1_b, w_rg, b_rg, w_re, b_re, w_gate, w_up, w_down, ln2_g, ln2_b):
    import concourse.bacc as bacc
    from concourse.bass_utils import run_bass_kernel_spmd

    def a(v):
        return np.asarray(v)

    def by_feature(v):
        return v.reshape(-1, P).T

    def w1(v):
        return a(v)[0].reshape(CMP_LEN, HD, P).transpose(1, 0, 2).reshape(HD, CMP_LEN * P)

    route = np.concatenate([a(w_rg)[0], a(w_re)[0].transpose(1, 0, 2).reshape(D, NE)], axis=1)
    arrays = {
        "x": a(x)[0],
        "cT": by_feature(a(c)[0]),
        "w_ada": a(w_ada)[0],
        "b_ada": a(b_ada),
        "w_in": w_in_units(a(w_in)[0]),
        "w_gb": a(w_in)[0][:, GATE_COL:GATE_COL + 3 * HB].reshape(KC, P, 3 * HB).transpose(1, 0, 2),
        "sinks": a(sinks),
        "pe_k": a(cmp_pe_k)[0].T,
        "pe_v": a(cmp_pe_v)[0].T,
        "w1_k": np.concatenate([w1(cmp_w1_k)] * 2),
        "w1_v": np.concatenate([w1(cmp_w1_v)] * 2),
        "w2_k": a(cmp_w2_k)[0],
        "w2_v": a(cmp_w2_v)[0],
        "gain": by_feature(a(mix_gain)[0]),
        "w_out": a(w_out)[0],
        "ln1_g": a(ln1_g),
        "ln1_b": a(ln1_b),
        "w_route": route.reshape(KC, P, NG + NE).transpose(1, 0, 2),
        "b_route": np.concatenate([a(b_rg), a(b_re).reshape(1, NE)], axis=1),
        "w_gate": a(w_gate)[0].reshape(NE * D, DE),
        "w_up": a(w_up)[0].reshape(NE * D, DE),
        "w_down": a(w_down)[0].reshape(NE * DE, D),
        "ln2_g": a(ln2_g),
        "ln2_b": a(ln2_b),
    }
    nc = bacc.Bacc("TRN2", target_bir_lowering=False, num_devices=1, dynamic_dma_scratch_size=4096)
    named, aps = {}, []
    for name, v in arrays.items():
        v = np.ascontiguousarray(v)
        named[f"in_{name}"] = v
        aps.append(nc.dram_tensor(f"in_{name}", v.shape, mybir.dt.from_np(v.dtype), kind="ExternalInput").ap())
    out = nc.dram_tensor("out", (SEQ, D), F32, kind="ExternalOutput").ap()
    build(nc, *aps, out)
    r = run_bass_kernel_spmd(nc, [named], core_ids=[0])
    return r.results[0]["out"].reshape(1, SEQ, D)
```

```python
from contextlib import ExitStack

import numpy as np
import concourse.bass as bass
from concourse import mybir

ALU = mybir.AluOpType
ACT = mybir.ActivationFunctionType
F32 = mybir.dt.float32
I32 = mybir.dt.int32
AX = mybir.AxisListType

P = 128
D = 2048
SEQ = 256
TB = SEQ // P
KC = D // P
HD = 64
HA = HB = 8
HC = 16
SCALE = HD ** -0.5
ALPHA = 2.0 ** 0.25
MASKED = -1e30
CMP_LEN, CMP_STEP = 32, 16
NCMP = (SEQ - CMP_LEN) // CMP_STEP + 1
NG, EPG, NE, DE = 4, 8, 32, 512
WIN = 64
PAIRS = NE // 2
PASSES = SEQ // WIN
BN = 512
SLOTS = 8
MOE_SLOTS = 12
HELD = 4
UNIT = 2048
SLOPES = [2.0 ** (-8.0 * (h + 1) / (HA + HB)) for h in range(HA + HB)]
GELU_C = 2.0 * (2.0 / np.pi) ** 0.5

WIN_GROUPS = [(0, 512), (512, 256), (768, 512), (1280, 256), (1536, 512)] + [
    (2072 + 512 * j, 512) for j in (0, 2, 4, 1, 3, 5)]
AB_GROUPS = 5
GATE_COL = 2048
K_A, K_CMP, V_CMP, K_SEL, K_WIN, K_C = 0, 1, 2, 3, 4, 5
V_A, V_SEL, V_WIN, V_C = 0, 128, 256, 384
VCOLS = 384 + HC * HD


def first_unit(group):
    return sum(KC * width // UNIT for _, width in WIN_GROUPS[:group])


def w_in_units(w):
    units = []
    for gi, (c0, width) in enumerate(WIN_GROUPS):
        cols = w[:, c0:c0 + width]
        if gi in (0, 2):
            cols = cols.reshape(D, 2, 4, HD).transpose(0, 2, 1, 3).reshape(D, width)
        kn = UNIT // width
        units.append(cols.reshape(KC // kn, kn, P, width).transpose(0, 2, 1, 3).reshape(-1, P, UNIT))
    return np.concatenate(units)


def w_mod_units(w):
    w = w[:, 0:2 * D].reshape(KC // 2, 2, P, 2, 4, BN)
    return w.transpose(4, 0, 2, 1, 3, 5).reshape(-1, P, UNIT)


def units_of(group):
    return KC * WIN_GROUPS[group][1] // UNIT


def weave(items, extra, gaps=None):
    total = gaps or sum(u[0] in BIG_UNITS for u in items)
    out, done = [], 0
    for u in items:
        out.append(u)
        if u[0] in BIG_UNITS:
            done += 1
            out += extra[(done - 1) * len(extra) // total:done * len(extra) // total]
    return out


PE_UNITS = ("win", "w1", "wout")
BIG_UNITS = ("win", "wout")


def schedule():
    items = [("mod", 0, i) for i in range(KC // 2)]
    for q in range(4):
        group_units = [("win", 0, q), ("win", 2, q)]
        if q % 2:
            group_units = [("win", 0, q), ("win", 1, q // 2), ("win", 2, q), ("win", 3, q // 2)]
        items.append(("modulate", q, 0))
        if q < 3:
            items += weave(group_units, [("mod", q + 1, i) for i in range(KC // 2)])
    rest = iter([("win", g, i) for g in range(4, len(WIN_GROUPS)) for i in range(units_of(g))])

    def w(n):
        return [next(rest) for _ in range(n)]

    def do(kind, a, b=0):
        return [(kind, a, b)]

    segments = [
        (2, group_units + do("scores", 0) + w(2) + do("turn", 0) + w(1) + do("values", 0)
            + do("scores", 1) + do("gates", 0) + w(1) + do("cmp_in", 0) + w(1) + do("turn", 1) + w(1)
            + do("values", 1) + w(1)),
        (3, do("rows", 2) + w(1) + do("w1", 0, 0) + do("scores", 2) + w(1) + do("w1", 0, 1) + w(1)
            + do("w1", 1, 0) + do("turn", 2) + w(1) + do("w1", 1, 1) + w(1) + do("cmp_kv", 0)
            + do("scores", 3) + w(1) + do("cmp_s", 0) + w(1)
            + do("cmp_t", 0) + do("turn", 3) + do("cmp_o", 0) + do("cmp_o", 1)
            + do("values", 2) + w(1) + do("values", 3) + do("scores", 4) + w(1)),
        (4, do("columns", 3) + do("turn", 4) + w(1) + do("values", 4) + do("scores", 5) + w(2)
            + do("turn", 5) + w(1) + do("values", 5)
            + do("z", 0) + w(2) + do("suffix", 0) + w(1) + do("sticks", 0) + do("z", 1) + w(2)
            + do("suffix", 1) + w(1) + do("sticks", 1)),
        (5, do("columns", 4) + do("z", 2) + w(2) + do("suffix", 2) + do("z", 3)
            + do("sticks", 2) + do("suffix", 3) + do("sticks", 3) + [("wout", k, 0) for k in range(KC)]),
    ]
    assert next(rest, None) is None
    for sixth, segment in segments:
        total = sum(u[0] in BIG_UNITS for u in segment) - (HELD if sixth == 5 else 0)
        items += weave(segment, [("ada", k, sixth) for k in range(KC)], total)
    return items


SCHEDULE = schedule()
UNITS = [u for u in SCHEDULE if u[0] in PE_UNITS + ("ada", "mod")]
FIRST_WOUT = SCHEDULE.index(("wout", 0, 0))
N_UNITS = len(UNITS)
PAIR_UNITS = 24
N_SMALL = 11
MISC_PAIR, MISC_FLUSH = 14, 8
MOE_STEPS, MOE_FLUSH_STEPS = 3, 2
POOL_CONST, POOL_ROWS, POOL_SETUP, POOL_MASKS = 7, 9, 11, 21 + HB + 2 * (HA + HB)


def pair_unit(j):
    if j < 16:
        quarter, r = divmod(j, 4)
        return ("gate", "up")[r // 2], r % 2, quarter
    quarter, r = divmod(j - 16, 2)
    return "down", r, quarter


class Steps:

    def __init__(self, eng, sem):
        self.eng, self.sem, self.n, self.turn = eng, sem, 0, 0

    def __call__(self, ins, k=1):
        ins.then_inc(self.sem, k)
        self.n += k

    def wait(self, eng=None):
        (eng or self.eng).wait_ge(self.sem, self.turn + self.n)


def build(nc, x, cT, w_ada, w_mod, b_ada, b_cols, w_in, w_gb, sinks, pe_k, pe_v, w1_k, w1_v, w2_k, w2_v, gain, w_out,
          ln1_g, ln1_b, w_route, b_route, w_gate, w_up, w_down, ln2_g, ln2_b, out):
    with ExitStack() as ctx:
        def sb(name, shape, dt=F32):
            return ctx.enter_context(nc.sbuf_tensor(name, shape, dt))

        def sem(name):
            return ctx.enter_context(nc.semaphore(name))

        ps = ctx.enter_context(nc.psum_tensor("ps", [P, 8, BN], F32))
        psf = ps[:].rearrange("p b n -> p (b n)")

        ring = sb("ring", [P, SLOTS, UNIT])
        tokens = sb("tokens", [P, TB, D])
        featT = sb("featT", [P, KC, SEQ])
        queryT = sb("queryT", [P, 2, 8, SEQ])
        keyval = sb("keyval", [P, 13 * SEQ + TB * VCOLS])
        work = sb("work", [P, 3 * 1536])
        bias = sb("bias", [P, 2 * 8 * 384])
        g1b = sb("g1b", [P, D])
        g2b = sb("g2b", [P, D])

        acc_col = sb("acc_col", [P, D])
        kpe_side = [tokens[:, s, D // 2:].rearrange("p (v g t) -> p v g t", v=2, g=2) for s in (0, 1)]
        merged = tokens
        keyT = keyval[:, 0:13 * SEQ].rearrange("p (k t) -> p k t", k=13)
        value = keyval[:, 13 * SEQ:].rearrange("p (c n) -> p c n", c=TB)
        xn2 = queryT[:].rearrange("p a b t -> p (a b t)").rearrange("p (c d) -> p c d", c=TB)
        ysum = featT[:].rearrange("p k t -> p (k t)").rearrange("p (c d) -> p c d", c=TB)
        x_pair = keyval[:, 0:KC * P].rearrange("p (k s) -> p k s", k=KC)
        y_pair = keyval[:, KC * P:2 * KC * P]
        biasX = bias[:, 0:16 * 256].rearrange("p (h k) -> p h k", h=16)
        biasY = bias[:, 16 * 256:].rearrange("p (h k) -> p h k", h=16)
        rowg, rowb = bias[:, 0:D], bias[:, D:2 * D]
        row2g, row2b = bias[:, D:2 * D], keyval[:, 2 * KC * P:2 * KC * P + D]
        slots = [ring[:, i, :] for i in range(SLOTS)] + [acc_col[:], bias[:, 2 * D:3 * D], g1b[:], bias[:, 0:D]]
        pc = keyT[:, 11:13, :].rearrange("p k t -> p (k t)")
        pcT = value[:, 1, V_C + 512:V_C + 1024]
        swork = [work[:, 0:1536], work[:, 1536:3072]]
        ptw = work[:, 3072:4608]
        e_gate, hid, hidT = work[:, 0:DE], work[:, DE:2 * DE], work[:, 2 * DE:3 * DE]

        dist = work[:, 0:384]
        rt = work[:, 3072:3840].rearrange("p (i c e) -> p i c e", i=12, c=TB)
        sel = work[:, 3840:4096].rearrange("p (c e s) -> p c e s", c=TB, e=2)
        selg = work[:, 4096:4352].rearrange("p (c e s) -> p c e s", c=TB, e=2)
        scatter = work[:, 4352:4608]

        ident = sb("ident", [P, P])
        ones = sb("ones", [P, P])
        neg_ones = sb("neg_ones", [P, P])
        neg_tri = sb("neg_tri", [P, P])
        before = sb("before", [P, P])
        slot_id = sb("slot_id", [P, 2, WIN])
        cmp_bias = sb("cmp_bias", [P, TB, HB, NCMP])
        cmp_mask = sb("cmp_mask", [P, TB * HB, NCMP])
        cvec = sb("cvec", [P, KC])
        cs = sb("cs", [P, KC])
        ctmp = sb("ctmp", [P, KC])
        sinkb = sb("sinkb", [P, HA])
        gaincol = sb("gaincol", [P, KC])
        pe2 = sb("pe2", [P, 2, CMP_LEN])
        w2 = sb("w2", [P, 2, HD])
        wr = sb("wr", [P, KC, NG + NE])
        bcols = sb("bcols", [P, 4, KC])
        brow = sb("brow", [P, NG + NE])
        gbw = sb("gbw", [P, KC, 3 * HB])
        gates = sb("gates", [P, TB, HB, 3])
        cols = sb("cols", [P, 4, KC])
        stats = sb("stats", [P, TB, 4, 6])
        mv = sb("mv", [P, TB, 2])
        rstd = sb("rstd", [P, TB])
        free_mark = sb("free_mark", [P, 2])
        nb = sb("nb", [P, TB])
        mx = sb("mx", [P, 2, TB, 4])
        nmx = sb("nmx", [P, 2, TB, 4])
        den = sb("den", [P, 2, TB, 4])
        den2 = sb("den2", [P, 2, TB, 4])
        hidc = sb("hidc", [P, 4, 2, 2, 16])
        kcmpT = sb("kcmpT", [P, 16])
        vblk = sb("vblk", [P, 2, 256])
        cst = sb("cst", [P, 4, TB * HB])
        ssq = sb("ssq", [P, TB, 3])
        minus_half = sb("minus_half", [P, TB * 3])
        lg = sb("lg", [P, TB, NG + NE])
        r1 = sb("r1", [P, 10, TB])
        rankm = sb("rankm", [P, TB, NE])
        gate_te = sb("gate_te", [P, TB, NE])
        more = sb("more", [P, PASSES], I32)

        full = [sem(f"ring_full_{i}") for i in range(MOE_SLOTS)]
        pe_freed = sem("pe_freed")
        dve_freed = sem("dve_freed")
        x_in = [sem(f"x_in_{c}") for c in range(TB)]
        c_in, small_in, ln_in, xr_in = (sem(n) for n in ("c_in", "small_in", "ln_in", "xr_in"))
        gate_bias_in, cols_in = sem("gate_bias_in"), sem("cols_in")
        bank3_taken = sem("bank3_taken")
        ab_merged = sem("ab_merged")
        g2_sum, g2_taken = sem("g2_sum"), sem("g2_taken")
        stored = sem("stored")
        pool_s = sem("pool_steps")
        dve_s = sem("dve_steps")
        act_s = sem("act_steps")
        ec_ready = sem("ec_ready")
        xn_ready = sem("xn_ready")
        xnT_full = sem("xnT_full")
        xnT_copied = sem("xnT_copied")
        acc_ready = sem("acc_ready")
        kpe_zeroed = sem("kpe_zeroed")
        ada_sums = sem("ada_sums")
        mod_sums, mod_taken = sem("mod_sums"), sem("mod_taken")
        ada_taken = sem("ada_taken")
        hT_ready = sem("hT_ready")
        gate_mm = sem("gate_mm")
        var_ready, rstd_ready = sem("var_ready"), sem("rstd_ready")
        x2T_even, x2T_odd = sem("x2T_even"), sem("x2T_odd")
        proj_taken = sem("proj_taken")
        cmp_in_ready, cmp_act, cmp_kv, cmp_s, cmp_p, cmp_pt, cmp_o = (
            sem(n) for n in ("cmp_in_ready", "cmp_act", "cmp_kv", "cmp_s", "cmp_p",
                             "cmp_pt", "cmp_o"))
        cmp_h_ready, cmp_e, cmp_sm, cmp_ex = (sem(n) for n in ("cmp_h_ready", "cmp_e", "cmp_sm", "cmp_ex"))
        gate_e = sem("gate_e")
        s_done, s_taken, m_ready, exp_done, sink_done, pt_full, pt_taken, o_full = (
            sem(n) for n in ("s_done", "s_taken", "m_ready", "exp_done", "sink_done", "pt_full", "pt_taken",
                             "o_full"))
        z_done, l_done, sp_done, lmask, zr_done, clamp_done, a_done, a_masked, oc_full = (
            sem(n) for n in ("z_done", "l_done", "sp_done", "lmask", "zr_done", "clamp_done", "a_done",
                             "a_masked", "oc_full"))
        sq_done, merged_ready, mT_full, mT_even, mT_odd = (
            sem(n) for n in ("sq_done", "merged_ready", "mT_full", "mT_even", "mT_odd"))
        y_full, nb_ready, xn2_ready, x2T_full, route_mm, lg_ready, rtab_ready, rank_full, route_ready = (
            sem(n) for n in ("y_full", "nb_ready", "xn2_ready", "x2T_full", "route_mm", "lg_ready",
                             "rtab_ready", "rank_full", "route_ready"))
        moe_zeroed = sem("moe_zeroed")
        rexp_in, rexp_out = sem("rexp_in"), sem("rexp_out")
        misc_full, misc_free, sel_ready, xg_ready, gu_done, e_ready, hid_ready, hidT_ready = (
            sem(n) for n in ("misc_full", "misc_free", "sel_ready", "xg_ready", "gu_done", "e_ready",
                             "hid_ready", "hidT_ready"))
        y_done, ysb_ready, comb_done, wc_ready, selg_ready, moe_s, fin_s, out_ready, passes_s = (
            sem(n) for n in ("y_done", "ysb_ready", "comb_done", "wc_ready", "selg_ready", "moe_steps",
                             "fin_steps", "out_ready", "passes_s"))

        uses = [0] * SLOTS
        unit_at, need = [], []
        seen = {"pe": 0, "dve": 0}
        for n, u in enumerate(UNITS):
            s = n % SLOTS
            uses[s] += 1
            unit_at.append((s, 16 * uses[s]))
            reader = "pe" if u[0] in PE_UNITS else "dve"
            seen[reader] += 1
            need.append((reader, seen[reader]))
        PE_BASE = seen["pe"]

        def arrived(eng, n):
            eng.wait_ge(full[unit_at[n][0]], unit_at[n][1])

        def index_of(kind, a, b):
            return UNITS.index((kind, a, b))

        def freed_after(kind, a, b):
            return need[index_of(kind, a, b)][1]

        def group_done(gi):
            return freed_after("win", gi, units_of(gi) - 1)

        def bank_of(gi):
            return 2 * gi if gi < 2 else 4 + 2 * (gi % 2)

        bank3_uses = [u for u in SCHEDULE if u[0] in ("values", "rows", "gates", "w1", "cmp_kv", "cmp_s", "cmp_t",
                                                      "cmp_o", "columns", "sticks")
                      and (u[0] != "w1" or u[1:] == (1, 1))]

        def bank3_turn(*item):
            return bank3_uses.index(item)

        def z_base(b):
            return (0, 0, 0, 4)[b] * BN

        def ada_done(sixth):
            return need[UNITS.index(("ada", KC - 1, sixth))][1]

        def pair_slot(j):
            j %= MOE_SLOTS
            return SLOTS + j if j < 2 else (N_UNITS + j - 2) % SLOTS if j < SLOTS + 2 else j

        def pair_value(j):
            s = pair_slot(j)
            return 16 * ((uses[s] if s < SLOTS else 0) + j // MOE_SLOTS + 1)

        PAIR_FULL = 16 * PAIR_UNITS // MOE_SLOTS

        block = ctx.enter_context(nc.Block())

        @block.sync
        def _(sp):
            for c in range(TB):
                sp.dma_start(tokens[:, c, :], x[c * P:(c + 1) * P, :]).then_inc(x_in[c], 16)
            for n, (kind, a, b) in enumerate(UNITS):
                slot = ring[:, n % SLOTS, :]
                if n >= SLOTS:
                    who, count = need[n - SLOTS]
                    sp.wait_ge(pe_freed if who == "pe" else dve_freed, count)
                if kind == "ada":
                    sp.dma_start(slot, w_ada[a * P:(a + 1) * P, b * D:(b + 1) * D]).then_inc(full[n % SLOTS], 16)
                elif kind == "mod":
                    sp.dma_start(slot, w_mod[a * (KC // 2) + b]).then_inc(full[n % SLOTS], 16)
                elif kind == "win":
                    sp.dma_start(slot, w_in[first_unit(a) + b]).then_inc(full[n % SLOTS], 16)
                elif kind == "w1":
                    w1 = (w1_k, w1_v)[a]
                    sp.dma_start(slot, w1[:, b * UNIT:(b + 1) * UNIT]).then_inc(full[n % SLOTS], 16)
                else:
                    sp.dma_start(slot, w_out[a * P:(a + 1) * P, :]).then_inc(full[n % SLOTS], 16)

            def load(j, p, q):
                what, which, quarter = pair_unit(j)
                slot = slots[pair_slot(j)]
                if what == "down":
                    off = sp.snap((p * 2 + which) * DE + quarter * P)
                    src = w_down[bass.ds(off, P), :]
                    dst = slot
                else:
                    w = w_gate if what == "gate" else w_up
                    off = sp.snap((p * 2 + which) * D + quarter * 4 * P)
                    src = w[bass.ds(off, 4 * P), :].rearrange("(k p) n -> p k n", p=P)
                    dst = slot.rearrange("p (k n) -> p k n", k=4)
                value = sp.snap(q * PAIR_UNITS + (PE_BASE + j - MOE_SLOTS + 1))
                sp.wait_ge(pe_freed, value)
                sp.dma_start(dst, src).then_inc(full[pair_slot(j)], 16)

            HALF = PAIR_UNITS // 2
            for j in range(MOE_SLOTS):
                what, which, quarter = pair_unit(j)
                w = w_gate if what == "gate" else w_up
                if j == 0:
                    sp.wait_ge(ada_sums, 3)
                    sp.wait_ge(m_ready, 6)
                elif 2 <= j < SLOTS + 2:
                    who, count = need[N_UNITS + j - 2 - SLOTS]
                    sp.wait_ge(pe_freed if who == "pe" else dve_freed, count)
                elif j == SLOTS + 2:
                    sp.wait_ge(xn2_ready, 2)
                sp.dma_start(slots[pair_slot(j)].rearrange("p (k n) -> p k n", k=4),
                             w[which * D + quarter * 4 * P:which * D + (quarter + 1) * 4 * P, :]
                             .rearrange("(k p) n -> p k n", p=P)).then_inc(full[pair_slot(j)], 16)
            with sp.Fori(0, PAIRS - 1) as p:
                for j in range(HALF, PAIR_UNITS):
                    load(j, p, p)
                for j in range(HALF):
                    load(j, p + 1, p + 1)
            for j in range(HALF, PAIR_UNITS):
                load(j, PAIRS - 1, PAIRS - 1)
            sp.wait_ge(route_ready, PASSES)
            with sp.Fori(1, PASSES) as w:
                go = sp.value_load(more[0:1, bass.ds(w, 1)])
                with sp.If(go > 0):
                    with sp.Fori(0, PAIRS) as p:
                        for j in range(PAIR_UNITS):
                            load(j, p, w * PAIRS + p)
            for c in range(TB):
                sp.wait_ge(out_ready, c + 1)
                sp.dma_start(out[c * P:(c + 1) * P, :], tokens[:, c, :]).then_inc(stored, 16)
            sp.wait_ge(stored, 16 * TB)

        @block.gpsimd
        def _(pool):
            st = Steps(pool, pool_s)
            g = nc.gpsimd
            st(g.memset(minus_half[:], -0.5))
            st(g.memset(ident[:], 0.0))
            st(g.memset(ones[:], 1.0))
            st(g.memset(neg_ones[:], -1.0))
            st.wait()
            st(g.affine_select(out=ident[:], in_=ident[:], compare_op=ALU.not_equal, fill=1.0, base=0,
                               pattern=[[-1, P]], channel_multiplier=1))
            st(g.affine_select(out=neg_tri[:], in_=neg_ones[:], compare_op=ALU.is_ge, fill=0.0, base=0,
                               pattern=[[-1, P]], channel_multiplier=1))
            st(g.affine_select(out=before[:], in_=ones[:], compare_op=ALU.is_gt, fill=0.0, base=0,
                               pattern=[[1, P]], channel_multiplier=-1))
            norms = [0]

            def rsqrt_variance(c):
                norms[0] += 1
                pool.wait_ge(var_ready, norms[0])
                g.tensor_tensor(rstd[:, c:c + 1], rstd[:, c:c + 1], minus_half[:, 0:1], ALU.pow).then_inc(rstd_ready, 1)

            for c in range(TB):
                rsqrt_variance(c)
            st(g.memset(g1b[:], 0.0))
            st(g.memset(g2b[:], 0.0))
            st(g.iota(slot_id[:], pattern=[[0, 2], [1, WIN]], base=0, channel_multiplier=0,
                      allow_small_or_imprecise_dtypes=True))
            st(g.memset(queryT[:].rearrange("p a b t -> p (a b t)"), 0.0))
            st(g.iota(dist[:, 0:256], pattern=[[-1, 256]], base=P, channel_multiplier=1,
                      allow_small_or_imprecise_dtypes=True))
            st(g.iota(dist[:, 256:384], pattern=[[-1, P]], base=0, channel_multiplier=1,
                      allow_small_or_imprecise_dtypes=True))
            st(g.iota(cmp_bias[:], pattern=[[P, TB], [0, HB], [-CMP_STEP, NCMP]], base=1 - CMP_LEN,
                      channel_multiplier=1, allow_small_or_imprecise_dtypes=True))
            st(g.memset(cmp_mask[:], 1.0))
            st(g.memset(vblk[:], 0.0))
            st.wait()
            st(g.affine_select(out=cmp_mask[:], in_=cmp_mask[:], compare_op=ALU.is_ge, fill=0.0,
                               base=1 - CMP_LEN, pattern=[[P, TB], [0, HB], [-CMP_STEP, NCMP]],
                               channel_multiplier=1))
            for h in range(HB):
                st(g.tensor_scalar(cmp_bias[:, :, h, :], cmp_bias[:, :, h, :], -SLOPES[HA + h], None, ALU.mult))
            for h in range(HA + HB):
                st(g.tensor_scalar(biasX[:, h, :], dist[:, 0:256], -SLOPES[h], None, ALU.mult))
                st(g.tensor_scalar(biasY[:, h, :], dist[:, 256:384], -SLOPES[h], None, ALU.mult))
            st.wait()
            st(g.affine_select(out=cmp_bias[:], in_=cmp_bias[:], compare_op=ALU.is_ge, fill=MASKED,
                               base=1 - CMP_LEN, pattern=[[P, TB], [0, HB], [-CMP_STEP, NCMP]],
                               channel_multiplier=1))
            st(g.affine_select(out=biasY, in_=biasY, compare_op=ALU.is_ge, fill=MASKED, base=0,
                               pattern=[[0, 16], [-1, P]], channel_multiplier=1))
            st(g.affine_select(out=biasX, in_=biasX, compare_op=ALU.is_ge, fill=MASKED, base=P,
                               pattern=[[0, 16], [-1, 256]], channel_multiplier=1))
            st.wait()
            st(g.affine_select(out=biasX[:, 0:HA, :], in_=biasX[:, 0:HA, :], compare_op=ALU.is_ge, fill=MASKED,
                               base=-1, pattern=[[0, HA], [1, 256]], channel_multiplier=-1))
            st.wait()
            assert st.n == POOL_MASKS, st.n
            pool.wait_ge(xnT_full, 8)
            for side in (0, 1):
                g.memset(tokens[:, side, D // 2:], 0.0).then_inc(kpe_zeroed, 1)
            def diagonal(b, ready, done):
                s = swork[b % 2]
                pool.wait_ge(ready, b + 1)
                for v in (s[:, 0:1024].rearrange("p (h q) -> p h q", h=4)[:, :, 0:P],
                          s[:, 1024:1536].rearrange("p (h q) -> p h q", h=4)):
                    g.affine_select(out=v, in_=v, compare_op=ALU.is_gt, fill=0.0, base=0,
                                    pattern=[[0, 4], [1, P]], channel_multiplier=-1).then_inc(done, 1)

            for kind, b, _ in SCHEDULE:
                if kind == "suffix":
                    diagonal(b, sp_done, lmask)
                elif kind == "sticks":
                    diagonal(b, a_done, a_masked)
            norms[0] += 1
            pool.wait_ge(var_ready, norms[0])
            flat = ssq[:].rearrange("p c g -> p (c g)")
            g.tensor_tensor(flat, flat, minus_half[:], ALU.pow).then_inc(rstd_ready, 1)
            for c in (0, 0, 1, 1):
                rsqrt_variance(c)
            g.memset(y_pair, 0.0).then_inc(moe_zeroed, 1)
            g.memset(scatter, 0.0).then_inc(moe_zeroed, 1)
            pool.wait_ge(route_mm, 1)
            g.memset(ysum, 0.0).then_inc(moe_zeroed, 1)
            for c in (0, 1):
                rsqrt_variance(c)

        @block.scalar
        def _(act):
            sc = nc.scalar
            act.dma_start(cvec[:], cT).then_inc(c_in, 16)
            act.dma_start(bcols[:], b_cols).then_inc(cols_in, 16)
            smalls = [(gaincol[:], gain), (sinkb[:], sinks[0:1, :].partition_broadcast(P)),
                      (brow[:], b_route[0:1, :].partition_broadcast(P)), (wr[:], w_route),
                      (pe2[0:HD, 0, :], pe_k), (pe2[HD:P, 0, :], pe_k),
                      (pe2[0:HD, 1, :], pe_v), (pe2[HD:P, 1, :], pe_v),
                      (w2[:, 0, :], w2_k), (w2[:, 1, :], w2_v),
                      (gbw[:], w_gb)]
            for dst, src in smalls:
                act.dma_start(dst, src).then_inc(small_in, 16)
            assert len(smalls) == N_SMALL
            act.wait_ge(c_in, 16)
            sc.activation(ctmp[:], cvec[:], ACT.Exp, scale=-1.0).then_inc(ec_ready, 1)
            for b in range(8):
                act.wait_ge(xnT_full, b + 1)
                sc.copy(featT[:, 2 * b:2 * b + 2, :].rearrange("p k t -> p (k t)"), ps[:, b, :]).then_inc(xnT_copied, 1)
            act.wait_ge(pool_s, POOL_ROWS)
            act.dma_start(g1b[0:1, :], b_ada[0:1, 2 * D:3 * D]).then_inc(gate_bias_in, 16)
            act.dma_start(g2b[0:1, :], b_ada[0:1, 5 * D:6 * D]).then_inc(gate_bias_in, 16)

            def split_heads(banks, tiles, scale):
                src = psf[:, banks * BN:(banks + 2) * BN]
                for half in (0, 1):
                    rows = slice(half * HD, (half + 1) * HD)
                    dst = queryT[rows, half, tiles:tiles + 4, :].rearrange("p a t -> p (a t)")
                    sc.mul(dst, src[rows, :], scale).then_inc(proj_taken, 1)

            def take(dst, src):
                sc.copy(dst, src).then_inc(proj_taken, 1)

            def take_group(gi):
                bank = bank_of(gi)
                act.wait_ge(pe_freed, group_done(gi))
                if gi == 0:
                    act.wait_ge(pool_s, POOL_SETUP)
                    split_heads(bank, 0, 1.0)
                elif gi == 1:
                    take(keyT[:, K_A, :], ps[:, bank, 0:SEQ])
                    take(value[:, :, V_A:V_A + P], ps[:, bank + 1, 0:2 * P].rearrange("p (c n) -> p c n", c=TB))
                elif gi == 2:
                    split_heads(bank, 4, 1.0)
                elif gi == 3:
                    take(keyT[:, K_CMP, :], ps[:, bank, 0:SEQ])
                    take(keyT[:, V_CMP, :], ps[:, bank, SEQ:2 * SEQ])
                elif gi == 4:
                    take(keyT[:, K_SEL:K_WIN + 1, :].rearrange("p k t -> p (k t)"), ps[:, bank, :])
                    take(value[:, :, V_SEL:V_WIN + P], ps[:, bank + 1, :].rearrange("p (c n) -> p c n", c=TB))
                else:
                    what, half = (gi - AB_GROUPS) % 3, (gi - AB_GROUPS) // 3
                    if what == 0:
                        split_heads(bank, 4 * half, SCALE)
                    elif what == 1:
                        k0 = K_C + 4 * half
                        for j in (0, 1):
                            take(keyT[:, k0 + 2 * j:k0 + 2 * j + 2, :].rearrange("p k t -> p (k t)"), ps[:, bank + j, :])
                    else:
                        v0 = V_C + 512 * half
                        for c in range(TB):
                            take(value[:, c, v0:v0 + 512], ps[:, bank + c, :])

            def gates_exp():
                act.wait_ge(bank3_taken, bank3_turn("gates", 0, 0) + 1)
                gf = gates[:].rearrange("p c h g -> p (c h g)")
                sc.activation(gf, gf, ACT.Exp, scale=-1.0).then_inc(gate_e, 1)

            def gelu_exp():
                act.wait_ge(cmp_h_ready, 1)
                sc.activation(hidc[:, 2, :, :, 0:NCMP], hidc[:, 2, :, :, 0:NCMP], ACT.Exp, scale=-GELU_C).then_inc(cmp_e, 1)

            def cmp_exp():
                act.wait_ge(cmp_sm, 1)
                v = pc.rearrange("p (a n) -> p a n", n=32)[:, :, 0:NCMP]
                sc.activation(v, v, ACT.Exp).then_inc(cmp_ex, 1)

            def softmax_exp(b):
                s = swork[b % 2]
                act.wait_ge(m_ready, b + 1)
                for blk, h, v in softmax_parts(s):
                    sc.activation(v, v, ACT.Exp, bias=nmx[:, b % 2, blk, h:h + 1],
                                  accum_out=den[:, b % 2, blk, h:h + 1]).then_inc(exp_done, 1)
                if b < 2:
                    sc.activation(den2[:, b], den2[:, b], ACT.Exp).then_inc(sink_done, 1)

            def take_turned(b):
                act.wait_ge(pt_full, b + 1)
                if b >= 1:
                    act.wait_ge(o_full, b)
                sc.copy(ptw, psf[:, 0:3 * BN]).then_inc(pt_taken, 1)

            def squares(blocks, groups):
                for blk in blocks:
                    for gi in groups:
                        lo, hi = ((0, 512), (512, 1024), (1024, 2048))[gi]
                        if squared[0]:
                            act.wait_ge(sq_done, squared[0])
                        sc.activation(ptw[:, 0:hi - lo], merged[:, blk, lo:hi], ACT.Square,
                                      accum_out=ssq[:, blk, gi:gi + 1]).then_inc(sq_done, 1)
                        squared[0] += 1

            squared = [0]

            def log_part(b):
                s = swork[b % 2]
                act.wait_ge(z_done, b + 1)
                if b < 2:
                    act.wait_ge(ab_merged, b + 3)
                else:
                    act.wait_ge(oc_full, b - 1)
                sc.activation(s, psf[:, z_base(b):z_base(b) + 1536], ACT.Abs).then_inc(act_s, 1)
                act.wait_ge(act_s, 2 * b + 1)
                sc.activation(s, s, ACT.Exp, scale=-1.0).then_inc(act_s, 1)
                act.wait_ge(act_s, 2 * b + 2)
                sc.activation(s, s, ACT.Ln, bias=1.0).then_inc(l_done, 1)

            for kind, a, b in SCHEDULE[:FIRST_WOUT]:
                if kind == "win" and b == units_of(a) - 1:
                    take_group(a)
                elif kind == "gates":
                    gates_exp()
                elif (kind, a, b) == ("w1", 1, 1):
                    gelu_exp()
                elif kind == "cmp_s":
                    cmp_exp()
                elif kind == "scores":
                    softmax_exp(a)
                elif kind == "turn":
                    take_turned(a)
                elif kind == "z":
                    log_part(a)
                elif kind == "suffix":
                    act.wait_ge(clamp_done, a + 1)
                    sc.activation(swork[a % 2], swork[a % 2], ACT.Exp).then_inc(a_done, 1)
                if (kind, a) == ("turn", 5):
                    act.dma_start(rowg, ln1_g[0:1, :].partition_broadcast(P)).then_inc(ln_in, 16)
                    act.dma_start(rowb, ln1_b[0:1, :].partition_broadcast(P)).then_inc(ln_in, 16)
                if (kind, a) == ("z", 1):
                    squares(range(TB), (0, 1))
            act.wait_ge(bank3_taken, len(bank3_uses))
            squares(range(TB), (2,))
            for b in range(1, 8, 2):
                act.wait_ge(mT_full, b + 1)
                for k in (2 * b, 2 * b + 1):
                    sc.mul(featT[:, k, :], ps[:, b, (k % 2) * SEQ:(k % 2 + 1) * SEQ],
                           gaincol[:, k:k + 1]).then_inc(mT_odd, 1)
            act.wait_ge(mT_full, 8)
            act.dma_start(tokens[:], x.rearrange("(c p) d -> p c d", p=P)).then_inc(xr_in, 16)
            for c in range(TB):
                act.wait_ge(nb_ready, c + 1)
                sc.activation(xn2[:, c, :], tokens[:, c, :], ACT.Identity, bias=nb[:, c:c + 1],
                              scale=rstd[:, c:c + 1]).then_inc(xn2_ready, 1)
                for b in (1, 3):
                    act.wait_ge(x2T_full, 4 * c + b + 1)
                    for k in range(4 * b, 4 * b + 4):
                        sc.activation(featT[:, k, c * P:(c + 1) * P], ps[:, 4 * c + b, (k % 4) * P:(k % 4 + 1) * P],
                                      ACT.Identity, bias=cols[:, 2, k:k + 1],
                                      scale=cols[:, 3, k:k + 1]).then_inc(x2T_odd, 1)
            act.wait_ge(rexp_in, 1)
            sc.activation(rt[:, 0, :, 0:NG], rt[:, 0, :, 0:NG], ACT.Exp).then_inc(rexp_out, 1)
            act.wait_ge(rexp_in, 2)
            sc.activation(rt[:, 1, :, 0:EPG], rt[:, 1, :, 0:EPG], ACT.Exp).then_inc(rexp_out, 1)

            act.wait_ge(g2_sum, 1)
            sc.activation(g2b[:], psf[:, 4 * BN:8 * BN], ACT.Identity, bias=1.0).then_inc(g2_taken, 1)

            def pair_act(q, w):
                act.wait_ge(pe_freed, q * PAIR_UNITS + (PE_BASE + 16))
                sc.activation(e_gate, ps[:, 0, :], ACT.Exp, scale=-1.0).then_inc(e_ready, 1)
                act.wait_ge(pe_freed, q * PAIR_UNITS + (PE_BASE + 24))
                act.wait_ge(misc_full, q * MISC_PAIR + w * MISC_FLUSH + 12)
                sc.copy(y_pair, psf[:, 2 * BN:6 * BN]).then_inc(ysb_ready, 1)

            with act.Fori(0, PAIRS) as p:
                pair_act(p, 0)
            act.wait_ge(xn2_ready, 2)
            act.dma_start(row2g, ln2_g[0:1, :].partition_broadcast(P)).then_inc(ln_in, 16)
            act.dma_start(row2b, ln2_b[0:1, :].partition_broadcast(P)).then_inc(ln_in, 16)
            act.wait_ge(route_ready, PASSES)
            with act.Fori(1, PASSES) as w:
                go = act.value_load(more[0:1, bass.ds(w, 1)])
                with act.If(go > 0):
                    with act.Fori(0, PAIRS) as p:
                        pair_act(w * PAIRS + p, w)

        @block.tensor
        def _(pe):
            mm = pe.matmul
            pe.wait_ge(pool_s, POOL_CONST)
            pe.wait_ge(xn_ready, TB)
            for b in range(8):
                for k in (2 * b, 2 * b + 1):
                    for c in range(TB):
                        last = pe.transpose(ps[:, b, (k % 2) * SEQ + c * P:(k % 2) * SEQ + (c + 1) * P],
                                            tokens[:, c, k * P:(k + 1) * P], ident[:])
                last.then_inc(xnT_full, 1)

            def ada_columns(acc, bank, c0):
                for k in range(acc.shape[1] // P):
                    last = mm(ps[:, bank, c0 + k:c0 + k + 1], acc[:, k * P:(k + 1) * P], ones[:, 0:1],
                              start=True, stop=True)
                return last

            def ada_rows(acc, bank):
                for n in range(4):
                    last = mm(ps[:, bank + n, :], ones[:], acc[:, n * BN:(n + 1) * BN], start=True, stop=True)
                last.then_inc(ada_sums, 1)

            def project(gi, i):
                bank = bank_of(gi)
                if i == 0 and gi >= 4:
                    pe.wait_ge(proj_taken, 2 * (gi - 1))
                if gi == 5 and i == 0:
                    pe.wait_ge(mod_taken, 4)
                width = WIN_GROUPS[gi][1]
                kn = UNIT // width
                pe.wait_ge(hT_ready, (i + 1) * kn)
                n = index_of("win", gi, i)
                arrived(pe, n)
                slot = ring[:, n % SLOTS, :].rearrange("p (k n) -> p k n", k=kn)
                for kk in range(kn):
                    k = i * kn + kk
                    first, final = k == 0, k == KC - 1
                    w = slot[:, kk, :]

                    def tile_T(lhsT, b, half):
                        return mm(ps[:, b, half * SEQ:(half + 1) * SEQ], lhsT, featT[:, k, :],
                                  start=first and half == 0, stop=final, skip_group_check=True)

                    if gi in (0, 2):
                        for j in range(4):
                            last = tile_T(w[:, j * P:(j + 1) * P], bank + j // 2, j % 2)
                    elif gi == 1:
                        tile_T(w[:, 0:P], bank, 0)
                        for c in range(TB):
                            last = mm(ps[:, bank + 1, c * P:(c + 1) * P], featT[:, k, c * P:(c + 1) * P],
                                      w[:, P:2 * P], start=first and c == 0, stop=final, skip_group_check=True)
                    elif gi == 3:
                        tile_T(w[:, 0:P], bank, 0)
                        last = tile_T(w[:, P:2 * P], bank, 1)
                    elif gi == 4:
                        tile_T(w[:, 0:P], bank, 0)
                        tile_T(w[:, 2 * P:3 * P], bank, 1)
                        vals = w.rearrange("p (s n) -> p s n", s=4)[:, 1:4:2, :]
                        for c in range(TB):
                            last = mm(ps[:, bank + 1, c * 2 * P:(c + 1) * 2 * P], featT[:, k, c * P:(c + 1) * P],
                                      vals, start=first and c == 0, stop=final, skip_group_check=True)
                    elif (gi - AB_GROUPS) % 3 < 2:
                        for j in range(4):
                            last = tile_T(w[:, j * P:(j + 1) * P], bank + j // 2, j % 2)
                    else:
                        for c in range(TB):
                            last = mm(ps[:, bank + c, :], featT[:, k, c * P:(c + 1) * P], w,
                                      start=first, stop=final)
                last.then_inc(pe_freed, 1)


            def bank3(*item):
                turn = bank3_turn(*item)
                if turn:
                    pe.wait_ge(bank3_taken, turn)

            def gate_products():
                bank3("gates", 0, 0)
                pe.wait_ge(small_in, 16 * N_SMALL)
                for c in range(TB):
                    for k in range(KC):
                        last = mm(ps[:, 3, c * 24:(c + 1) * 24], featT[:, k, c * P:(c + 1) * P], gbw[:, k, :],
                                  start=k == 0, stop=k == KC - 1)
                last.then_inc(gate_mm, 1)

            def cmp_hidden(s, half):
                if (s, half) == (0, 0):
                    bank3("w1", 1, 1)
                    pe.wait_ge(cmp_in_ready, 8)
                n = index_of("w1", s, half)
                arrived(pe, n)
                for j in range(CMP_STEP):
                    w1 = ring[:, n % SLOTS, j * P:(j + 1) * P]
                    win = kpe_side[s][:, half].rearrange("p g (n j) -> p g n j", j=CMP_STEP)[:, :, half:half + NCMP, j]
                    last = mm(ps[:, 3, s * 64:s * 64 + 2 * NCMP], w1, win, start=half == 0 and j == 0,
                              stop=half == 1 and j == CMP_STEP - 1)
                last.then_inc(pe_freed, 1)

            def cmp_keys_values():
                pe.wait_ge(cmp_act, 1)
                bank3("cmp_kv", 0, 0)
                for g in (0, 1):
                    mm(ps[g * HD:(g + 1) * HD, 3, 0:NCMP], w2[:, 0, :], hidc[:, 3, 0, g, 0:NCMP], start=True, stop=True)
                for g in (0, 1):
                    for i in range(4):
                        last = mm(ps[32 * i:32 * i + NCMP, 3, P + g * HD:P + (g + 1) * HD], hidc[:, 3, 1, g, 0:NCMP],
                                  w2[:, 1, :], start=True, stop=True)
                last.then_inc(cmp_kv, 1)

            def cmp_scores():
                bank3("cmp_s", 0, 0)
                for blk in range(TB):
                    for h in range(HB):
                        last = mm(ps[:, 3, (blk * HB + h) * 16:(blk * HB + h) * 16 + NCMP],
                                  queryT[:, h // 4, 4 + h % 4, blk * P:(blk + 1) * P], kcmpT[:, 0:NCMP],
                                  start=True, stop=True)
                last.then_inc(cmp_s, 1)

            def cmp_transpose():
                bank3("cmp_t", 0, 0)
                pe.wait_ge(cmp_p, 1)
                for a in range(4):
                    last = pe.transpose(ps[:, 3, a * P:(a + 1) * P], pc[:, a * P:(a + 1) * P], ident[:])
                last.then_inc(cmp_pt, 1)

            def cmp_values(c):
                bank3("cmp_o", c, 0)
                for a in (2 * c, 2 * c + 1):
                    last = mm(ps[:, 3, (a % 2) * 256:(a % 2 + 1) * 256], pcT[:, a * P:(a + 1) * P], vblk[:, a % 2, :],
                              start=True, stop=True)
                last.then_inc(cmp_o, 1)

            def scores(b):
                tiles, ktile = (0, K_A) if b < 2 else (4, (K_SEL, K_WIN)[(b - 2) // 2])
                g = b % 2
                pe.wait_ge(proj_taken, 4 if b < 2 else 2 * AB_GROUPS)
                if b >= 1:
                    pe.wait_ge(pt_taken, b)
                if b == 2:
                    pe.wait_ge(ada_taken, 1)
                for h in range(4):
                    q = queryT[:, g, tiles + h, :]
                    mm(psf[:, h * 256:(h + 1) * 256], q[:, P:2 * P], keyT[:, ktile, :], start=True, stop=True)
                    last = mm(psf[:, 2 * BN + h * P:2 * BN + (h + 1) * P], q[:, 0:P], keyT[:, ktile, 0:P],
                              start=True, stop=True)
                last.then_inc(s_done, 1)

            def turn_probabilities(b):
                s = swork[b % 2]
                pe.wait_ge(s_taken, b + 1)
                pe.wait_ge(exp_done, 8 * (b + 1))
                for n in range(12):
                    last = pe.transpose(psf[:, n * P:(n + 1) * P], s[:, n * P:(n + 1) * P], ident[:])
                last.then_inc(pt_full, 1)

            def weigh(b):
                v0 = (V_A, V_SEL, V_WIN)[b // 2] + (b % 2) * HD
                pe.wait_ge(pt_taken, b + 1)
                bank3("values", b, 0)
                for h in range(4):
                    mm(ps[:, 3, h * HD:(h + 1) * HD], ptw[:, (8 + h) * P:(9 + h) * P], value[:, 0, v0:v0 + HD],
                       start=True, stop=True)
                    for c in range(TB):
                        last = mm(ps[:, 3, 256 + h * HD:256 + (h + 1) * HD], ptw[:, (2 * h + c) * P:(2 * h + c + 1) * P],
                                  value[:, c, v0:v0 + HD], start=c == 0, stop=c == TB - 1)
                last.then_inc(o_full, 1)

            def z_scores(b):
                base = z_base(b)
                pe.wait_ge(proj_taken, 2 * (AB_GROUPS + (2, 2, 5, 6)[b]))
                if b == 0:
                    pe.wait_ge(pt_taken, 6)
                elif b < 3:
                    pe.wait_ge(clamp_done, b)
                for i in range(4):
                    tile, half = 2 * b + i // 2, i % 2
                    k = keyT[:, K_C + tile, :]
                    q = queryT[:, half, tile, :]
                    mm(psf[:, base + i * 256:base + (i + 1) * 256], k[:, 0:P], q, start=i % 2 == 0, stop=False,
                       skip_group_check=True)
                    last = mm(psf[:, base + 1024 + i * P:base + 1024 + (i + 1) * P], k[:, P:2 * P], q[:, P:2 * P],
                              start=i == 0, stop=False, skip_group_check=True)
                last.then_inc(z_done, 1)

            def suffix_sums(b):
                base = z_base(b)
                s = swork[b % 2]
                pe.wait_ge(lmask, 2 * (b + 1))
                for n in range(3):
                    mm(psf[:, base + n * BN:base + (n + 1) * BN], neg_tri[:], s[:, n * BN:(n + 1) * BN],
                       start=False, stop=False, skip_group_check=True)
                for n in range(2):
                    dst = psf[:, base + n * BN:base + (n + 1) * BN].rearrange("p (h q) -> p h q", h=2)[:, :, P:2 * P]
                    src = s[:, 1024 + n * 256:1024 + (n + 1) * 256].rearrange("p (h q) -> p h q", h=2)
                    last = mm(dst, neg_ones[:], src, start=False, stop=True, skip_group_check=True)
                last.then_inc(zr_done, 1)

            def stick_values(b):
                s = swork[b % 2]
                pe.wait_ge(a_masked, 2 * (b + 1))
                pe.wait_ge(proj_taken, 2 * (AB_GROUPS + 3) if b < 2 else 2 * len(WIN_GROUPS))
                bank3("sticks", b, 0)
                for i in range(4):
                    v0 = V_C + (4 * b + i) * HD
                    mm(ps[:, 3, i * HD:(i + 1) * HD], s[:, i * 256:i * 256 + P], value[:, 0, v0:v0 + HD],
                       start=True, stop=True)
                    mm(ps[:, 3, 256 + i * HD:256 + (i + 1) * HD], s[:, i * 256 + P:(i + 1) * 256],
                       value[:, 0, v0:v0 + HD], start=True, stop=False)
                    last = mm(ps[:, 3, 256 + i * HD:256 + (i + 1) * HD], s[:, 1024 + i * P:1024 + (i + 1) * P],
                              value[:, 1, v0:v0 + HD], start=False, stop=True)
                last.then_inc(oc_full, 1)

            pe.wait_ge(xnT_copied, 8)
            for kind, a, b in SCHEDULE[:FIRST_WOUT]:
                if kind == "win":
                    project(a, b)
                elif kind == "w1":
                    cmp_hidden(a, b)
                elif kind == "scores":
                    scores(a)
                elif kind == "turn":
                    turn_probabilities(a)
                elif kind == "values":
                    weigh(a)
                elif kind == "modulate":
                    pe.wait_ge(dve_freed, need[UNITS.index(("mod", a, KC // 2 - 1))][1])
                    ada_columns(acc_col[:, (a % 2) * 1024:(a % 2 + 1) * 1024], 7, 8 * a).then_inc(mod_sums, 1)
                elif kind == "rows":
                    pe.wait_ge(pt_taken, 2)
                    bank3(kind, a, b)
                    pe.wait_ge(dve_freed, ada_done(a))
                    ada_rows(g1b[:], 0)
                elif kind == "columns":
                    bank3(kind, a, b)
                    pe.wait_ge(dve_freed, ada_done(a))
                    ada_columns(acc_col[:], 3, 0).then_inc(ada_sums, 1)
                elif kind == "gates":
                    gate_products()
                elif kind == "cmp_kv":
                    cmp_keys_values()
                elif kind == "cmp_s":
                    cmp_scores()
                elif kind == "cmp_t":
                    cmp_transpose()
                elif kind == "cmp_o":
                    cmp_values(a)
                elif kind == "z":
                    z_scores(a)
                elif kind == "suffix":
                    suffix_sums(a)
                elif kind == "sticks":
                    stick_values(a)

            pe.wait_ge(merged_ready, 6)
            for b in range(8):
                for k in (2 * b, 2 * b + 1):
                    for c in range(TB):
                        last = pe.transpose(ps[:, b, (k % 2) * SEQ + c * P:(k % 2) * SEQ + (c + 1) * P],
                                            merged[:, c, k * P:(k + 1) * P], ident[:])
                last.then_inc(mT_full, 1)
            pe.wait_ge(mT_even, KC // 2)
            pe.wait_ge(mT_odd, KC // 2)

            def out_product(c, j, k):
                n = index_of("wout", k, 0)
                return mm(ps[:, 4 * c + j, :], featT[:, k, c * P:(c + 1) * P], ring[:, n % SLOTS, j * BN:(j + 1) * BN],
                          start=k == 0, stop=k == KC - 1)

            def turn_x2(c):
                pe.wait_ge(xn2_ready, c + 1)
                for b in range(4):
                    for k in range(4 * b, 4 * b + 4):
                        last = pe.transpose(ps[:, 4 * c + b, (k % 4) * P:(k % 4 + 1) * P], xn2[:, c, k * P:(k + 1) * P],
                                            ident[:])
                    last.then_inc(x2T_full, 1)

            for k in range(KC - HELD):
                arrived(pe, index_of("wout", k, 0))
                for c in range(TB):
                    for j in range(4):
                        last = out_product(c, j, k)
                last.then_inc(pe_freed, 1)
            for c in range(TB):
                for j in range(4):
                    for k in range(KC - HELD, KC):
                        if (c, j) == (0, 0):
                            arrived(pe, index_of("wout", k, 0))
                        last = out_product(c, j, k)
                        if (c, j) == (1, 3):
                            last.then_inc(pe_freed, 1)
                    if (c, j) != (1, 3):
                        last.then_inc(y_full, 1)
            for c in range(TB):
                turn_x2(c)
                for k in range(KC):
                    if k % 4 == 0:
                        pe.wait_ge((x2T_even, x2T_odd)[k // 4 % 2], 8 * c + 4 * (k // 8) + 4)
                    last = mm(ps[:, 0, c * 36:(c + 1) * 36], featT[:, k, c * P:(c + 1) * P], wr[:, k, :],
                              start=k == 0, stop=k == KC - 1)
            last.then_inc(route_mm, 1)
            pe.wait_ge(dve_freed, ada_done(5))
            for n in range(4):
                last = mm(ps[:, 4 + n, :], ones[:], g2b[:, n * BN:(n + 1) * BN], start=True, stop=True)
            last.then_inc(g2_sum, 1)
            routed = rt[:, 2]
            pe.wait_ge(rtab_ready, 1)
            mm(ps[:, 1, 0:NE], before[:], routed[:, 0, :], start=True, stop=True)
            mm(ps[:, 1, NE:2 * NE], ones[:], routed[:, 0, :], start=True, stop=False)
            mm(ps[:, 1, NE:2 * NE], before[:], routed[:, 1, :], start=False, stop=True)
            mm(ps[:, 1, 2 * NE:3 * NE], ones[:], routed[:, 0, :], start=True, stop=False)
            mm(ps[:, 1, 2 * NE:3 * NE], ones[:], routed[:, 1, :], start=False, stop=True).then_inc(rank_full, 1)

            def scatter_pair(use):
                for c in range(TB):
                    for n in range(4):
                        mm(use(), scatter[:, c * P:(c + 1) * P], y_pair[:, n * BN:(n + 1) * BN],
                           start=True, stop=True).then_inc(misc_full, 1)

            def misc(turn):
                count = [0]

                def use():
                    count[0] += 1
                    pe.wait_ge(misc_free, turn + count[0])
                    return ps[:, 6 + (count[0] - 1) % 2, :]
                return use

            def pair_pe(q, w):
                turn = q * MISC_PAIR + w * MISC_FLUSH
                use = misc(turn)
                pe.wait_ge(sel_ready, q + 1)
                for b in range(4):
                    bank = use()
                    for k in range(4 * b, 4 * b + 4):
                        for c in range(TB):
                            last = mm(bank[:, (k % 4) * P:(k % 4 + 1) * P], xn2[:, c, k * P:(k + 1) * P],
                                      sel[:, c].rearrange("p e s -> p (e s)"), start=c == 0, stop=c == TB - 1)
                    last.then_inc(misc_full, 1)
                pe.wait_ge(misc_free, turn + 6)
                pe.wait_ge(hid_ready, q)
                for quarter in range(4):
                    for m in (0, 1):
                        j = 4 * quarter + 2 * m
                        for e in (0, 1):
                            pe.wait_ge(full[pair_slot(j + e)], q * PAIR_FULL + pair_value(j + e))
                        for kk in range(4):
                            k = 4 * quarter + kk
                            for e in (0, 1):
                                last = mm(ps[e * WIN:(e + 1) * WIN, m, :], x_pair[:, k, e * WIN:(e + 1) * WIN],
                                          slots[pair_slot(j + e)][:, kk * BN:(kk + 1) * BN],
                                          start=k == 0, stop=k == KC - 1)
                                if kk == 3:
                                    last.then_inc(pe_freed, 1)
                pe.wait_ge(ysb_ready, q)
                scatter_pair(use)
                pe.wait_ge(selg_ready, q + 1)
                bank = use()
                for c in range(TB):
                    last = pe.transpose(bank[:, c * P:(c + 1) * P], selg[:, c].rearrange("p e s -> p (e s)"), ident[:])
                last.then_inc(misc_full, 1)
                pe.wait_ge(hid_ready, q + 1)
                bank = use()
                for k in range(DE // P):
                    last = pe.transpose(bank[:, k * P:(k + 1) * P], hid[:, k * P:(k + 1) * P], ident[:])
                last.then_inc(misc_full, 1)
                pe.wait_ge(misc_free, turn + 16)
                for k in range(DE // P):
                    j = 16 + 2 * k
                    for e in (0, 1):
                        pe.wait_ge(full[pair_slot(j + e)], q * PAIR_FULL + pair_value(j + e))
                    for n in range(4):
                        for e in (0, 1):
                            last = mm(ps[e * WIN:(e + 1) * WIN, 2 + n, :],
                                      hidT[:, k * P + e * WIN:k * P + (e + 1) * WIN],
                                      slots[pair_slot(j + e)][:, n * BN:(n + 1) * BN],
                                      start=k == 0, stop=k == DE // P - 1)
                            if n == 3:
                                last.then_inc(pe_freed, 1)

            def flush_pe(w):
                use = misc((w + 1) * (PAIRS * MISC_PAIR) + w * MISC_FLUSH)
                pe.wait_ge(ysb_ready, (w + 1) * PAIRS)
                pe.wait_ge(misc_free, (w + 1) * (PAIRS * MISC_PAIR) + w * MISC_FLUSH + 1)
                scatter_pair(use)

            pe.wait_ge(g2_taken, 1)
            pe.wait_ge(moe_zeroed, 3)
            with pe.Fori(0, PAIRS) as p:
                pair_pe(p, 0)
            flush_pe(0)
            pe.wait_ge(route_ready, PASSES)
            with pe.Fori(1, PASSES) as w:
                go = pe.value_load(more[0:1, bass.ds(w, 1)])
                with pe.If(go > 0):
                    with pe.Fori(0, PAIRS) as p:
                        pair_pe(w * PAIRS + p, w)
                    flush_pe(w)

        @block.vector
        def _(dve):
            st = Steps(dve, dve_s)
            freed = [0]

            def ada(k, sixth):
                n = index_of("ada", k, sixth)
                dst = {2: g1b, 3: acc_col, 4: acc_col, 5: g2b}[sixth][:]
                src, scalar = ring[:, n % SLOTS, :], cs[:, k:k + 1]
                arrived(dve, n)
                if k == 0 and sixth == 2:
                    dve.wait_ge(gate_bias_in, 32)
                if k:
                    dve.wait_ge(dve_freed, need[n][1] - 1)
                if k == 0 and sixth in (3, 4):
                    if sixth == 3:
                        dve.wait_ge(mod_sums, 4)
                    else:
                        dve.wait_ge(ada_sums, 2)
                    dve.tensor_scalar(dst, src, scalar, None, ALU.mult).then_inc(dve_freed, 1)
                else:
                    dve.scalar_tensor_tensor(out=dst, in0=src, scalar=scalar, in1=dst,
                                             op0=ALU.mult, op1=ALU.add).then_inc(dve_freed, 1)

            def mod_unit(q, i):
                n = index_of("mod", q, i)
                dst = acc_col[:, (q % 2) * 1024:(q % 2 + 1) * 1024]
                arrived(dve, n)
                if i == 0 and q >= 2:
                    dve.wait_ge(mod_sums, q - 1)
                for kk in (0, 1):
                    k = 2 * i + kk
                    src, scalar = ring[:, n % SLOTS, kk * 1024:(kk + 1) * 1024], cs[:, k:k + 1]
                    if k == 0:
                        st(dve.tensor_scalar(dst, src, scalar, None, ALU.mult))
                        continue
                    if kk:
                        st.wait()
                    else:
                        dve.wait_ge(dve_freed, need[n][1] - 1)
                    ins = dve.scalar_tensor_tensor(out=dst, in0=src, scalar=scalar, in1=dst, op0=ALU.mult, op1=ALU.add)
                    if kk:
                        ins.then_inc(dve_freed, 1)
                    else:
                        st(ins)

            def modulate(q):
                dve.wait_ge(mod_sums, q + 1)
                if q == 0:
                    dve.wait_ge(cols_in, 16)
                f = slice(4 * q, 4 * q + 4)
                st(dve.tensor_tensor(cols[:, 0, f], ps[:, 7, 8 * q:8 * q + 4], bcols[:, 0, f], ALU.add))
                dve.scalar_tensor_tensor(out=cols[:, 1, f], in0=ps[:, 7, 8 * q + 4:8 * q + 8], scalar=1.0,
                                         in1=bcols[:, 1, f], op0=ALU.add, op1=ALU.add).then_inc(mod_taken, 1)
                st.wait()
                dve.wait_ge(mod_taken, q + 1)
                dve.wait_ge(xnT_copied, 8)
                for k in range(4 * q, 4 * q + 4):
                    dve.tensor_scalar(featT[:, k, :], featT[:, k, :], cols[:, 1, k:k + 1], cols[:, 0, k:k + 1],
                                      ALU.mult, ALU.add).then_inc(hT_ready, 1)

            norms = [0]

            def inverse_deviation(c):
                st.wait()
                st(dve.bn_aggr(mv[:, c, :], stats[:, c].rearrange("p n s -> p (n s)")))
                st.wait()
                dve.tensor_scalar(rstd[:, c:c + 1], mv[:, c, 1:2], 1e-5, None, ALU.add).then_inc(var_ready, 1)
                norms[0] += 1
                dve.wait_ge(rstd_ready, norms[0])

            def normalise(src, dst, c):
                for n in range(4):
                    st(dve.bn_stats(stats[:, c, n, :], src[:, n * BN:(n + 1) * BN]))
                inverse_deviation(c)
                return dve.tensor_scalar(dst, src, mv[:, c, 0:1], rstd[:, c:c + 1], ALU.subtract, ALU.mult)

            for c in range(TB):
                dve.wait_ge(x_in[c], 16)
                normalise(tokens[:, c, :], tokens[:, c, :], c).then_inc(xn_ready, 1)
            dve.wait_ge(ec_ready, 1)
            st(dve.tensor_scalar(ctmp[:], ctmp[:], 1.0, None, ALU.add))
            st.wait()
            st(dve.reciprocal(ctmp[:], ctmp[:]))
            st.wait()
            st(dve.tensor_tensor(cs[:], cvec[:], ctmp[:], ALU.mult))
            st.wait()
            H = [hidc[:, i, :, :, 0:NCMP] for i in range(4)]
            gf = gates[:].rearrange("p c h g -> p (c h g)")

            def windows():
                dve.wait_ge(kpe_zeroed, 2)
                dve.wait_ge(small_in, 16 * N_SMALL)
                dve.wait_ge(proj_taken, 8)
                for s in (0, 1):
                    for v in (0, 1):
                        for g in (0, 1):
                            rows = slice(g * HD, (g + 1) * HD)
                            pe16 = pe2[rows, s, v * 16:(v + 1) * 16].unsqueeze(1).broadcast_to([HD, 16, 16])
                            dve.tensor_tensor(kpe_side[s][rows, v, g].rearrange("p (n j) -> p n j", n=16),
                                              keyT[rows, K_CMP + s, :].rearrange("p (n j) -> p n j", n=16), pe16,
                                              ALU.add).then_inc(cmp_in_ready, 1)
                st(dve.memset(pc, 0.0))

            def gate_values():
                dve.wait_ge(gate_mm, 1)
                dve.tensor_copy(gf, ps[:, 3, 0:TB * 3 * HB]).then_inc(bank3_taken, 1)
                dve.wait_ge(gate_e, 1)
                st(dve.tensor_scalar(gf, gf, 1.0, None, ALU.add))
                st.wait()
                st(dve.reciprocal(gf, gf))

            def gelu():
                dve.wait_ge(pe_freed, freed_after("w1", 1, 1))
                dve.tensor_copy(H[0], ps[:, 3, 0:P].rearrange("p (s x) -> p s x", s=2)[:, :, 0:2 * NCMP]
                                .rearrange("p s (g n) -> p s g n", g=2)).then_inc(bank3_taken, 1)
                dve.wait_ge(bank3_taken, bank3_turn("w1", 1, 1) + 1)
                st(dve.tensor_tensor(H[1], H[0], H[0], ALU.mult))
                st.wait()
                st(dve.tensor_scalar(H[1], H[1], 0.044715, 1.0, ALU.mult, ALU.add))
                st.wait()
                dve.tensor_tensor(H[2], H[1], H[0], ALU.mult).then_inc(cmp_h_ready, 1)
                dve.wait_ge(cmp_e, 1)
                st(dve.tensor_scalar(H[1], H[2], 1.0, None, ALU.add))
                st.wait()
                st(dve.reciprocal(H[1], H[1]))
                st.wait()
                dve.tensor_tensor(H[3], H[0], H[1], ALU.mult).then_inc(cmp_act, 1)

            def cmp_take():
                dve.wait_ge(cmp_kv, 1)
                for i in range(4):
                    rows = slice(32 * i, 32 * i + NCMP)
                    st(dve.tensor_copy(vblk[rows, :, i * HD:(i + 1) * HD],
                                       ps[rows, 3, P:2 * P].rearrange("p (g d) -> p g d", g=2)))
                dve.tensor_copy(kcmpT[:, 0:NCMP], ps[:, 3, 0:NCMP]).then_inc(bank3_taken, 1)

            def cmp_softmax():
                pcv = pc.rearrange("p (a n) -> p a n", n=32)[:, :, 0:NCMP]
                sv = ps[:, 3, 0:256].rearrange("p (a n) -> p a n", n=16)[:, :, 0:NCMP]
                dve.wait_ge(cmp_s, 1)
                dve.scalar_tensor_tensor(out=pcv, in0=sv, scalar=SCALE, in1=cmp_bias[:].rearrange("p c h n -> p (c h) n"),
                                         op0=ALU.mult, op1=ALU.add).then_inc(bank3_taken, 1)
                dve.wait_ge(bank3_taken, bank3_turn("cmp_s", 0, 0) + 1)
                st(dve.tensor_reduce(cst[:, 0, :], pcv, AX.X, ALU.max))
                st.wait()
                wide = [P, TB * HB, NCMP]
                dve.tensor_tensor(pcv, pcv, cst[:, 0, :].unsqueeze(2).broadcast_to(wide), ALU.subtract).then_inc(cmp_sm, 1)
                dve.wait_ge(cmp_ex, 1)
                dve.tensor_tensor(pcv, pcv, cmp_mask[:], ALU.mult).then_inc(cmp_p, 1)
                dve.wait_ge(cmp_p, 1)
                st(dve.tensor_reduce(cst[:, 1, :], pcv, AX.X, ALU.add))
                st.wait()
                st(dve.tensor_scalar(cst[:, 2, :], cst[:, 1, :], 1e-30, None, ALU.max))
                st.wait()
                st(dve.reciprocal(cst[:, 2, :], cst[:, 2, :]))
                st.wait()
                st(dve.tensor_tensor(cst[:, 3, :], cst[:, 2, :], gf.rearrange("p (x g) -> p x g", g=3)[:, :, 0], ALU.mult))

            def cmp_take_turned():
                dve.wait_ge(cmp_pt, 1)
                dve.tensor_copy(pcT, ps[:, 3, :]).then_inc(bank3_taken, 1)

            def cmp_outputs(c):
                dve.wait_ge(cmp_o, c + 1)
                st.wait()
                o = ps[:, 3, :].rearrange("p (h d) -> p h d", h=HB)
                r = cst[:, 3, c * HB:(c + 1) * HB].unsqueeze(2).broadcast_to([P, HB, HD])
                dve.tensor_tensor(merged[:, c, 512:1024].rearrange("p (h d) -> p h d", h=HB), o, r,
                                  ALU.mult).then_inc(bank3_taken, 1)

            def front(b):
                s, m, nm = swork[b % 2], mx[:, b % 2], nmx[:, b % 2]
                h0 = (0 if b < 2 else HA) + (b % 2) * 4
                if b == 0:
                    dve.wait_ge(pool_s, POOL_MASKS)
                    dve.wait_ge(small_in, 16 * N_SMALL)
                dve.wait_ge(s_done, b + 1)
                X, Y = s[:, 0:1024].rearrange("p (h k) -> p h k", h=4), s[:, 1024:1536].rearrange("p (h k) -> p h k", h=4)
                st(dve.scalar_tensor_tensor(out=X, in0=psf[:, 0:1024].rearrange("p (h k) -> p h k", h=4), scalar=SCALE,
                                            in1=biasX[:, h0:h0 + 4, :], op0=ALU.mult, op1=ALU.add))
                dve.scalar_tensor_tensor(out=Y, in0=psf[:, 1024:1536].rearrange("p (h k) -> p h k", h=4), scalar=SCALE,
                                         in1=biasY[:, h0:h0 + 4, :], op0=ALU.mult, op1=ALU.add).then_inc(s_taken, 1)
                st.wait()
                st(dve.tensor_reduce(m[:, 1, :], X, AX.X, ALU.max))
                dve.wait_ge(s_taken, b + 1)
                st(dve.tensor_reduce(m[:, 0, :], Y, AX.X, ALU.max))
                st.wait()
                if b < 2:
                    sink = sinkb[:, 4 * b:4 * b + 4].unsqueeze(1).broadcast_to([P, TB, 4])
                    st(dve.tensor_tensor(m, m, sink, ALU.max))
                    st.wait()
                    st(dve.tensor_tensor(den2[:, b], sink, m, ALU.subtract))
                    st.wait()
                dve.tensor_scalar(nm, m, -1.0, None, ALU.mult).then_inc(m_ready, 1)

            def back(b):
                s, dn = swork[b % 2], den[:, b % 2]
                dve.wait_ge(exp_done, 8 * (b + 1))
                if b < 2:
                    dve.wait_ge(sink_done, b + 1)
                    st(dve.tensor_tensor(dn, dn, den2[:, b], ALU.add))
                    st.wait()
                st(dve.reciprocal(dn, dn))
                st.wait()
                if b >= 2:
                    gate = gates[:, :, (b % 2) * 4:(b % 2) * 4 + 4, 1 + (b - 2) // 2]
                    st(dve.tensor_tensor(dn, dn, gate, ALU.mult))
                    st.wait()
                r = dn.unsqueeze(3).broadcast_to([P, TB, 4, HD])
                o = ps[:, 3, :].rearrange("p (c h d) -> p c h d", c=TB, h=4)
                n0 = (0 if b < 2 else 512) + (b % 2) * 256
                dst = merged[:, :, n0:n0 + 256].rearrange("p c (h d) -> p c h d", h=4)
                dve.wait_ge(o_full, b + 1)
                if b < 2:
                    dve.tensor_tensor(dst, o, r, ALU.mult).then_inc(bank3_taken, 1)
                else:
                    tmp = s[:, 0:512].rearrange("p (c h d) -> p c h d", c=TB, h=4)
                    dve.tensor_tensor(tmp, o, r, ALU.mult).then_inc(bank3_taken, 1)
                    dve.wait_ge(bank3_taken, bank3_turn("values", b, 0) + 1)
                    dve.tensor_tensor(dst, dst, tmp, ALU.add).then_inc(ab_merged, 1)

            def softplus(b):
                s = swork[b % 2]
                dve.wait_ge(l_done, b + 1)
                dve.scalar_tensor_tensor(out=s, in0=psf[:, z_base(b):z_base(b) + 1536], scalar=0.0, in1=s,
                                         op0=ALU.max, op1=ALU.add).then_inc(sp_done, 1)

            def take_sticks(b):
                dve.wait_ge(oc_full, b + 1)
                dve.tensor_copy(merged[:, :, 1024 + b * 256:1024 + (b + 1) * 256],
                                ps[:, 3, :].rearrange("p (c n) -> p c n", c=TB)).then_inc(bank3_taken, 1)

            for kind, a, b in SCHEDULE[:FIRST_WOUT]:
                if kind == "ada":
                    ada(a, b)
                elif kind == "mod":
                    mod_unit(a, b)
                elif kind == "modulate":
                    modulate(a)
                elif kind == "cmp_in":
                    windows()
                elif kind == "gates":
                    gate_values()
                elif (kind, a, b) == ("w1", 1, 1):
                    gelu()
                elif kind == "cmp_kv":
                    cmp_take()
                elif kind == "cmp_s":
                    cmp_softmax()
                elif kind == "cmp_t":
                    cmp_take_turned()
                elif kind == "cmp_o":
                    cmp_outputs(a)
                elif kind == "scores":
                    front(a)
                elif kind == "values":
                    back(a)
                elif kind == "rows":
                    dve.wait_ge(ada_sums, 1)
                    dve.tensor_scalar(g1b[:, 0:3 * BN], psf[:, 0:3 * BN], 1.0, None, ALU.add).then_inc(ada_taken, 1)
                    dve.tensor_scalar(g1b[:, 3 * BN:], ps[:, 3, :], 1.0, None, ALU.add).then_inc(bank3_taken, 1)
                elif kind == "columns":
                    dve.wait_ge(ada_sums, a - 1)
                    dve.scalar_tensor_tensor(out=cols[:, a - 1, :], in0=ps[:, 3, 0:KC], scalar=float(a - 3),
                                             in1=bcols[:, a - 1, :], op0=ALU.add, op1=ALU.add).then_inc(bank3_taken, 1)
                elif kind == "z":
                    softplus(a)
                elif kind == "suffix":
                    dve.wait_ge(zr_done, a + 1)
                    dve.tensor_scalar(swork[a % 2], psf[:, z_base(a):z_base(a) + 1536], 0.0, None,
                                      ALU.min).then_inc(clamp_done, 1)
                elif kind == "sticks":
                    take_sticks(a)

            dve.wait_ge(sq_done, 3 * TB)
            dve.tensor_scalar(ssq[:, :, 0:2], ssq[:, :, 0:2], 1.0 / 512, 1e-6, ALU.mult, ALU.add)
            dve.tensor_scalar(ssq[:, :, 2:3], ssq[:, :, 2:3], 1.0 / 1024, 1e-6, ALU.mult, ALU.add).then_inc(var_ready, 1)
            norms[0] += 1
            dve.wait_ge(rstd_ready, norms[0])
            for c in range(TB):
                for gi, (lo, hi) in enumerate(((0, 512), (512, 1024), (1024, 2048))):
                    dve.tensor_scalar(merged[:, c, lo:hi], merged[:, c, lo:hi], ssq[:, c, gi:gi + 1], None,
                                      ALU.mult).then_inc(merged_ready, 1)
            for b in range(0, 8, 2):
                dve.wait_ge(mT_full, b + 1)
                for k in (2 * b, 2 * b + 1):
                    dve.tensor_scalar(featT[:, k, :], ps[:, b, (k % 2) * SEQ:(k % 2 + 1) * SEQ], gaincol[:, k:k + 1],
                                      None, ALU.mult).then_inc(mT_even, 1)
            for kind, a, b in SCHEDULE[FIRST_WOUT:]:
                if kind == "ada":
                    ada(a, b)
            dve.wait_ge(xr_in, 16)
            dve.wait_ge(ln_in, 32)

            def residual(c, n):
                f = slice(n * BN, (n + 1) * BN)
                if (c, n) == (1, 3):
                    dve.wait_ge(pe_freed, PE_BASE)
                else:
                    dve.wait_ge(y_full, 4 * c + n + 1)
                st(dve.tensor_tensor(xn2[:, c, f], ps[:, 4 * c + n, :], g1b[:, f], ALU.mult))
                st.wait()
                st(dve.scalar_tensor_tensor(out=tokens[:, c, f], in0=tokens[:, c, f], scalar=ALPHA, in1=xn2[:, c, f],
                                            op0=ALU.mult, op1=ALU.add))
                st.wait()
                st(dve.bn_stats(stats[:, c, n, :], tokens[:, c, f]))

            def layer_norm(c, g, b):
                inverse_deviation(c)
                st(dve.scalar_tensor_tensor(out=tokens[:, c, :], in0=tokens[:, c, :], scalar=mv[:, c, 0:1], in1=g,
                                            op0=ALU.subtract, op1=ALU.mult))
                st.wait()
                return dve.scalar_tensor_tensor(out=tokens[:, c, :], in0=tokens[:, c, :], scalar=rstd[:, c:c + 1],
                                                in1=b, op0=ALU.mult, op1=ALU.add)

            def first_norms(c):
                st(layer_norm(c, rowg, rowb))
                st.wait()
                for n in range(4):
                    st(dve.bn_stats(stats[:, c, n, :], tokens[:, c, n * BN:(n + 1) * BN]))
                inverse_deviation(c)
                dve.scalar_tensor_tensor(out=nb[:, c:c + 1], in0=mv[:, c, 0:1], scalar=-1.0, in1=rstd[:, c:c + 1],
                                         op0=ALU.mult, op1=ALU.mult).then_inc(nb_ready, 1)

            def modulate2(c):
                for b in (0, 2):
                    dve.wait_ge(x2T_full, 4 * c + b + 1)
                    for k in range(4 * b, 4 * b + 4):
                        dve.tensor_scalar(featT[:, k, c * P:(c + 1) * P], ps[:, 4 * c + b, (k % 4) * P:(k % 4 + 1) * P],
                                          cols[:, 3, k:k + 1], cols[:, 2, k:k + 1], ALU.mult,
                                          ALU.add).then_inc(x2T_even, 1)

            for n in range(4):
                residual(0, n)
            first_norms(0)
            for n in range(3):
                residual(1, n)
            modulate2(0)
            residual(1, 3)
            first_norms(1)
            modulate2(1)

            dve.wait_ge(route_mm, 1)
            st(dve.tensor_tensor(lg[:], ps[:, 0, 0:TB * (NG + NE)].rearrange("p (c n) -> p c n", c=TB),
                                 brow[:].unsqueeze(1).broadcast_to([P, TB, NG + NE]), ALU.add))
            st.wait()

            def bc(v, n):
                return v.unsqueeze(2).broadcast_to([P, TB, n])

            def first_max(values, n, top, onehot, tmp, index):
                st(dve.tensor_reduce(top, values, AX.X, ALU.max))
                st.wait()
                st(dve.tensor_tensor(tmp, values, bc(top, n), ALU.not_equal))
                st.wait()
                st(dve.scalar_tensor_tensor(out=tmp, in0=tmp, scalar=64.0,
                                            in1=number[:, 0:n].unsqueeze(1).broadcast_to([P, TB, n]),
                                            op0=ALU.mult, op1=ALU.add))
                st.wait()
                st(dve.tensor_reduce(index, tmp, AX.X, ALU.min))
                st.wait()
                st(dve.tensor_tensor(onehot, number[:, 0:n].unsqueeze(1).broadcast_to([P, TB, n]), bc(index, n),
                                     ALU.is_equal))
                st.wait()

            def T(i, n):
                return rt[:, i, :, 0:n]

            number = slot_id[:, 0, :]
            glog = lg[:, :, 0:NG]
            gmax, gidx, psum_g, m8, v1, i1, v2, i2, tot, cnt = (r1[:, i, :] for i in range(10))
            first_max(glog, NG, gmax, T(3, NG), T(4, NG), gidx)
            dve.tensor_tensor(T(0, NG), glog, bc(gmax, NG), ALU.subtract).then_inc(rexp_in, 1)
            gone = T(3, NG)
            prod = T(5, NE).rearrange("p c (g e) -> p c g e", g=NG)
            st(dve.tensor_tensor(prod, lg[:, :, NG:].rearrange("p c (g e) -> p c g e", g=NG),
                                 gone.unsqueeze(3).broadcast_to([P, TB, NG, EPG]), ALU.mult))
            st.wait()
            st(dve.tensor_reduce(T(6, EPG), T(5, NE).rearrange("p c (g e) -> p c e g", g=NG), AX.X, ALU.add))
            st.wait()
            st(dve.tensor_reduce(m8, T(6, EPG), AX.X, ALU.max))
            st.wait()
            dve.tensor_tensor(T(1, EPG), T(6, EPG), bc(m8, EPG), ALU.subtract).then_inc(rexp_in, 1)
            dve.wait_ge(rexp_out, 1)
            st(dve.tensor_reduce(psum_g, T(0, NG), AX.X, ALU.add))
            st.wait()
            dve.wait_ge(rexp_out, 2)
            first_max(T(1, EPG), EPG, v1, T(7, EPG), T(4, EPG), i1)
            st(dve.scalar_tensor_tensor(out=T(8, EPG), in0=T(7, EPG), scalar=-2.0, in1=T(1, EPG), op0=ALU.mult, op1=ALU.add))
            st.wait()
            first_max(T(8, EPG), EPG, v2, T(9, EPG), T(4, EPG), i2)
            st(dve.tensor_tensor(tot, v1, v2, ALU.add))
            st.wait()
            st(dve.tensor_tensor(tot, tot, psum_g, ALU.mult))
            st.wait()
            st(dve.reciprocal(tot, tot))
            st.wait()
            st(dve.tensor_tensor(v1, v1, tot, ALU.mult))
            st(dve.tensor_tensor(v2, v2, tot, ALU.mult))
            st.wait()
            st(dve.tensor_tensor(T(10, EPG), T(7, EPG), bc(v1, EPG), ALU.mult))
            st(dve.tensor_tensor(T(11, EPG), T(9, EPG), bc(v2, EPG), ALU.mult))
            st.wait()
            st(dve.tensor_tensor(T(10, EPG), T(10, EPG), T(11, EPG), ALU.add))
            st(dve.tensor_tensor(T(7, EPG), T(7, EPG), T(9, EPG), ALU.add))
            st.wait()
            for dst, per, done in ((gate_te[:], T(10, EPG), None), (T(2, NE), T(7, EPG), rtab_ready)):
                for g in range(NG):
                    ins = dve.tensor_tensor(dst[:, :, g * EPG:(g + 1) * EPG], per, bc(T(3, NG)[:, :, g], EPG), ALU.mult)
                    if done is not None and g == NG - 1:
                        ins.then_inc(done, 1)
                    else:
                        st(ins)
            dve.wait_ge(rank_full, 1)
            dve.wait_ge(rtab_ready, 1)
            st(dve.scalar_tensor_tensor(out=rankm[:], in0=ps[:, 1, 0:2 * NE].rearrange("p (c e) -> p c e", c=TB),
                                        scalar=1.0, in1=T(2, NE), op0=ALU.add, op1=ALU.mult))
            st(dve.tensor_reduce(cnt[:, 0:1], ps[:, 1, 2 * NE:3 * NE], AX.X, ALU.max))
            st.wait()
            st(dve.tensor_scalar(rankm[:], rankm[:], -1.0, None, ALU.add))
            for w in range(PASSES):
                dve.tensor_scalar(more[:, w:w + 1], cnt[:, 0:1], float(WIN * w), None,
                                  ALU.is_gt).then_inc(route_ready, 1)
            dve.wait_ge(g2_taken, 1)
            for i in range(2):
                dve.memset(free_mark[:, i:i + 1], 0.0).then_inc(misc_free, 1)
            dve.wait_ge(misc_free, 2)
            dve.wait_ge(moe_zeroed, 3)
            st.wait()

            mo = Steps(dve, moe_s)

            def scatter_add(full_at):
                for i in range(8):
                    dst = ysum[:, i // 4, (i % 4) * BN:(i % 4 + 1) * BN]
                    dve.wait_ge(misc_full, full_at + (i + 1))
                    dve.tensor_tensor(dst, dst, ps[:, 6 + i % 2, :], ALU.add).then_inc(misc_free, 1)

            def pair_dve(p, q, w):
                turn = q * MISC_PAIR + w * MISC_FLUSH
                mo.turn, mo.n = q * MOE_STEPS + w * MOE_FLUSH_STEPS, 0
                two = [P, TB, 2, WIN]
                ranks = rankm[:, :, bass.ds(p * 2, 2)].unsqueeze(3).broadcast_to(two)
                weights = gate_te[:, :, bass.ds(p * 2, 2)].unsqueeze(3).broadcast_to(two)
                mo.wait()
                dve.tensor_tensor(sel, slot_id[:].unsqueeze(1).broadcast_to(two), ranks,
                                  ALU.is_equal).then_inc(sel_ready, 1)
                dve.wait_ge(sel_ready, q + 1)
                dve.tensor_tensor(selg, sel, weights, ALU.mult).then_inc(selg_ready, 1)
                dve.wait_ge(pe_freed, q * PAIR_UNITS + (PE_BASE + 16 - PAIR_UNITS))
                for b in range(4):
                    dve.wait_ge(misc_full, turn + (b + 1))
                    for k in range(4 * b, 4 * b + 4):
                        ins = dve.tensor_scalar(x_pair[:, k, :], ps[:, 6 + b % 2, (k % 4) * P:(k % 4 + 1) * P],
                                                cols[:, 3, k:k + 1], cols[:, 2, k:k + 1], ALU.mult, ALU.add)
                    ins.then_inc(misc_free, 1)
                dve.wait_ge(e_ready, q + 1)
                mo(dve.tensor_scalar(e_gate, e_gate, 1.0, None, ALU.add))
                mo.wait()
                mo(dve.reciprocal(e_gate, e_gate))
                mo.wait()
                mo(dve.tensor_tensor(e_gate, e_gate, ps[:, 0, :], ALU.mult))
                mo.wait()
                dve.tensor_tensor(hid, e_gate, ps[:, 1, :], ALU.mult).then_inc(hid_ready, 1)
                scatter_add(turn + 4)
                dve.wait_ge(misc_full, turn + 13)
                dve.tensor_copy(scatter, ps[:, 6, 0:SEQ]).then_inc(misc_free, 1)
                dve.wait_ge(misc_full, turn + 14)
                dve.wait_ge(pe_freed, q * PAIR_UNITS + PE_BASE)
                dve.tensor_copy(hidT, ps[:, 7, :]).then_inc(misc_free, 1)
                assert mo.n == MOE_STEPS, mo.n

            def flush_dve(w):
                mo.turn, mo.n = (w + 1) * (PAIRS * MOE_STEPS) + w * MOE_FLUSH_STEPS, 0
                turn = (w + 1) * (PAIRS * MISC_PAIR) + w * MISC_FLUSH
                scatter_add(turn)
                dve.wait_ge(misc_free, turn + 10)
                mo(dve.memset(scatter, 0.0))
                mo(dve.tensor_scalar(rankm[:], rankm[:], -float(WIN), None, ALU.add))
                assert mo.n == MOE_FLUSH_STEPS, mo.n

            with dve.Fori(0, PAIRS) as p:
                pair_dve(p, p, 0)
            flush_dve(0)
            with dve.Fori(1, PASSES) as w:
                go = dve.value_load(more[0:1, bass.ds(w, 1)])
                with dve.If(go > 0):
                    with dve.Fori(0, PAIRS) as p:
                        pair_dve(p, w * PAIRS + p, w)
                    flush_dve(w)

            st.sem, st.n = fin_s, 0
            dve.wait_ge(ln_in, 64)
            for c in range(TB):
                st(dve.tensor_tensor(xn2[:, c, :], ysum[:, c, :], g2b[:], ALU.mult))
                st.wait()
                st(dve.scalar_tensor_tensor(out=tokens[:, c, :], in0=tokens[:, c, :], scalar=ALPHA, in1=xn2[:, c, :],
                                            op0=ALU.mult, op1=ALU.add))
                st.wait()
                for n in range(4):
                    st(dve.bn_stats(stats[:, c, n, :], tokens[:, c, n * BN:(n + 1) * BN]))
                layer_norm(c, row2g, row2b).then_inc(out_ready, 1)


def softmax_parts(s):
    for h in range(4):
        yield 1, h, s[:, h * 256:(h + 1) * 256]
    for h in range(4):
        yield 0, h, s[:, 1024 + h * P:1024 + (h + 1) * P]


def kernel(x, c, w_ada, b_ada, w_in, sinks, cmp_pe_k, cmp_w1_k, cmp_w2_k, cmp_pe_v, cmp_w1_v, cmp_w2_v,
           mix_gain, w_out, ln1_g, ln1_b, w_rg, b_rg, w_re, b_re, w_gate, w_up, w_down, ln2_g, ln2_b):
    import concourse.bacc as bacc
    from concourse.bass_utils import run_bass_kernel_spmd

    def a(v):
        return np.asarray(v)

    def by_feature(v):
        return v.reshape(-1, P).T

    def w1(v):
        return a(v)[0].reshape(CMP_LEN, HD, P).transpose(1, 0, 2).reshape(HD, CMP_LEN * P)

    route = np.concatenate([a(w_rg)[0], a(w_re)[0].transpose(1, 0, 2).reshape(D, NE)], axis=1)
    arrays = {
        "x": a(x)[0],
        "cT": by_feature(a(c)[0]),
        "w_ada": a(w_ada)[0],
        "w_mod": w_mod_units(a(w_ada)[0]),
        "b_ada": a(b_ada),
        "b_cols": a(b_ada)[0].reshape(6, KC, P)[[0, 1, 3, 4]].transpose(2, 0, 1),
        "w_in": w_in_units(a(w_in)[0]),
        "w_gb": a(w_in)[0][:, GATE_COL:GATE_COL + 3 * HB].reshape(KC, P, 3 * HB).transpose(1, 0, 2),
        "sinks": a(sinks),
        "pe_k": a(cmp_pe_k)[0].T,
        "pe_v": a(cmp_pe_v)[0].T,
        "w1_k": np.concatenate([w1(cmp_w1_k)] * 2),
        "w1_v": np.concatenate([w1(cmp_w1_v)] * 2),
        "w2_k": a(cmp_w2_k)[0],
        "w2_v": a(cmp_w2_v)[0],
        "gain": by_feature(a(mix_gain)[0]),
        "w_out": a(w_out)[0],
        "ln1_g": a(ln1_g),
        "ln1_b": a(ln1_b),
        "w_route": route.reshape(KC, P, NG + NE).transpose(1, 0, 2),
        "b_route": np.concatenate([a(b_rg), a(b_re).reshape(1, NE)], axis=1),
        "w_gate": a(w_gate)[0].reshape(NE * D, DE),
        "w_up": a(w_up)[0].reshape(NE * D, DE),
        "w_down": a(w_down)[0].reshape(NE * DE, D),
        "ln2_g": a(ln2_g),
        "ln2_b": a(ln2_b),
    }
    nc = bacc.Bacc("TRN2", target_bir_lowering=False, num_devices=1, dynamic_dma_scratch_size=4096)
    named, aps = {}, []
    for name, v in arrays.items():
        v = np.ascontiguousarray(v)
        named[f"in_{name}"] = v
        aps.append(nc.dram_tensor(f"in_{name}", v.shape, mybir.dt.from_np(v.dtype), kind="ExternalInput").ap())
    out = nc.dram_tensor("out", (SEQ, D), F32, kind="ExternalOutput").ap()
    build(nc, *aps, out)
    r = run_bass_kernel_spmd(nc, [named], core_ids=[0])
    return r.results[0]["out"].reshape(1, SEQ, D)
```

```python
from contextlib import ExitStack

import numpy as np
import concourse.bass as bass
from concourse import mybir

ALU = mybir.AluOpType
ACT = mybir.ActivationFunctionType
F32 = mybir.dt.float32
I32 = mybir.dt.int32
AX = mybir.AxisListType

P = 128
D = 2048
SEQ = 256
TB = SEQ // P
KC = D // P
HD = 64
HA = HB = 8
HC = 16
SCALE = HD ** -0.5
ALPHA = 2.0 ** 0.25
MASKED = -1e30
CMP_LEN, CMP_STEP = 32, 16
NCMP = (SEQ - CMP_LEN) // CMP_STEP + 1
NG, EPG, NE, DE = 4, 8, 32, 512
WIN = 64
PAIRS = NE // 2
PASSES = SEQ // WIN
BN = 512
SLOTS = 8
MOE_SLOTS = 12
SMALL = 7
HELD = 6
UNIT = 2048
SLOPES = [2.0 ** (-8.0 * (h + 1) / (HA + HB)) for h in range(HA + HB)]
GELU_C = 2.0 * (2.0 / np.pi) ** 0.5

WIN_GROUPS = [(0, 512), (512, 256), (768, 512), (1536, 512), (1280, 256)] + [
    (2072 + 512 * j, 512) for j in (0, 2, 4, 1, 3, 5)]
AB_GROUPS = 5
GATE_COL = 2048
K_A, K_CMP, V_CMP, K_SEL, K_WIN, K_C = 0, 1, 2, 3, 4, 5
V_A, V_SEL, V_WIN, V_C = 0, 128, 256, 384
VCOLS = 384 + HC * HD


def first_unit(group):
    return sum(KC * width // UNIT for _, width in WIN_GROUPS[:group])


def w_in_units(w):
    units = []
    for gi, (c0, width) in enumerate(WIN_GROUPS):
        cols = w[:, c0:c0 + width]
        if gi in (0, 2):
            cols = cols.reshape(D, 2, 4, HD).transpose(0, 2, 1, 3).reshape(D, width)
        kn = UNIT // width
        units.append(cols.reshape(KC // kn, kn, P, width).transpose(0, 2, 1, 3).reshape(-1, P, UNIT))
    return np.concatenate(units)


def w_mod_units(w):
    w = w[:, 0:2 * D].reshape(KC // 2, 2, P, 2, 4, BN)
    return w.transpose(4, 0, 2, 1, 3, 5).reshape(-1, P, UNIT)


def tile2(k):
    first = (k // 4) * 4 * P + k % 4
    return slice(first, first + 4 * P - 3, 4)


def by_tile2(v):
    return v.reshape(KC // 4, P, 4, -1).transpose(1, 0, 2, 3).reshape(P, KC, -1)


def units_of(group):
    return KC * WIN_GROUPS[group][1] // UNIT


def weave(items, extra, tail=0):
    total = sum(u[0] in BIG_UNITS for u in items) - tail
    out, done = [], 0
    for u in items:
        out.append(u)
        if u[0] in BIG_UNITS:
            done += 1
            out += extra[(done - 1) * len(extra) // total:done * len(extra) // total]
    return out


PE_UNITS = ("win", "w1", "wout")
BIG_UNITS = ("win", "wout")


def schedule():
    items = [("mod", 0, i) for i in range(KC // 2)]
    for q in range(4):
        group_units = [("win", 0, q), ("win", 2, q), ("win", 3, q)]
        if q % 2:
            group_units.insert(1, ("win", 1, q // 2))
        items.append(("modulate", q, 0))
        if q < 3:
            mods = [("mod", q + 1, i) for i in range(KC // 2)]
            items += mods[:2] + weave(group_units, mods[2:])
    rest = iter([("win", g, i) for g in range(4, len(WIN_GROUPS)) for i in range(units_of(g))])

    def w(n):
        return [next(rest) for _ in range(n)]

    def do(kind, a, b=0):
        return [(kind, a, b)]

    segments = [
        (2, group_units + do("scores", 0) + w(2) + do("turn", 0) + w(1) + do("values", 0)
            + do("scores", 1) + do("gates", 0) + w(1) + do("cmp_in", 0) + w(1) + do("turn", 1) + w(1)
            + do("values", 1) + w(1)),
        (3, do("rows", 2) + w(1) + do("w1", 0) + do("scores", 2) + w(1) + do("w1", 1) + w(1)
            + do("turn", 2) + w(2) + do("cmp_kv", 0)
            + do("scores", 3) + w(1) + do("cmp_s", 0) + w(1)
            + do("cmp_t", 0) + do("turn", 3) + do("cmp_o", 0) + do("cmp_o", 1)
            + do("values", 2) + w(1) + do("values", 3) + do("scores", 4) + w(1)),
        (4, do("columns", 3) + do("turn", 4) + w(1) + do("values", 4) + do("scores", 5) + w(1)
            + do("turn", 5) + w(1) + do("values", 5) + do("z", 0) + w(1) + do("suffix", 0) + w(1)
            + do("sticks", 0) + do("z", 1) + w(1) + do("suffix", 1) + w(1) + do("sticks", 1)
            + do("z", 2) + do("z", 3) + w(1) + do("suffix", 2) + w(1) + do("suffix", 3) + w(1)
            + do("sticks", 2) + do("sticks", 3) + do("columns", 4)),
        (5, [("wout", k, 0) for k in range(KC)]),
    ]
    assert next(rest, None) is None
    ada = {sixth: [("ada", k, sixth) for k in range(KC)] for sixth in (2, 3, 4, 5)}
    early = KC // 2
    ada[4] += ada[5][:early]
    ada[5] = ada[5][early:]
    for sixth, segment in segments:
        items += weave(segment, ada[sixth], HELD if sixth == 5 else 0)
    return items


SCHEDULE = schedule()
UNITS = [u for u in SCHEDULE if u[0] in PE_UNITS + ("ada", "mod")]
FIRST_WOUT = SCHEDULE.index(("wout", 0, 0))
N_UNITS = len(UNITS)
PAIR_UNITS = 24
N_SMALL = 11
MISC_PAIR, MISC_FLUSH = 14, 8
MOE_STEPS, MOE_FLUSH_STEPS, MOE_START_STEPS = 1, 12, 3
MOE_PASS_STEPS = MOE_FLUSH_STEPS + MOE_START_STEPS
POOL_CONST, POOL_ROWS, POOL_SETUP, POOL_MASKS = 7, 9, 11, 21 + HB + 2 * (HA + HB)


def pair_unit(j):
    if j < 16:
        quarter, r = divmod(j, 4)
        return ("gate", "up")[r // 2], r % 2, quarter
    quarter, r = divmod(j - 16, 2)
    return "down", r, quarter


class Steps:

    def __init__(self, eng, sem):
        self.eng, self.sem, self.n, self.turn = eng, sem, 0, 0

    def __call__(self, ins, k=1):
        ins.then_inc(self.sem, k)
        self.n += k

    def wait(self, eng=None):
        (eng or self.eng).wait_ge(self.sem, self.turn + self.n)


def build(nc, x, cT, w_ada, w_mod, b_ada, b_cols, w_in, w_gb, sinks, pe_k, pe_v, w1_k, w1_v, w2_k, w2_v, gain, w_out,
          ln1_g, ln1_b, w_route, b_route, w_gate, w_up, w_down, ln2_g, ln2_b, out):
    with ExitStack() as ctx:
        def sb(name, shape, dt=F32):
            return ctx.enter_context(nc.sbuf_tensor(name, shape, dt))

        def sem(name):
            return ctx.enter_context(nc.semaphore(name))

        ps = ctx.enter_context(nc.psum_tensor("ps", [P, 8, BN], F32))
        psf = ps[:].rearrange("p b n -> p (b n)")

        ring = sb("ring", [P, SLOTS, UNIT])
        tokens = sb("tokens", [P, TB, D])
        featT = sb("featT", [P, KC, SEQ])
        queryT = sb("queryT", [P, 2, 8, SEQ])
        keyval = sb("keyval", [P, 13 * SEQ + TB * VCOLS])
        work = sb("work", [P, 3 * 1536])
        bias = sb("bias", [P, 2 * 8 * 384])
        g1b = sb("g1b", [P, D])
        g2b = sb("g2b", [P, D])

        acc_col = sb("acc_col", [P, D])
        windows_of = [tokens[:, s, D // 2:D // 2 + 2 * SEQ].rearrange("p (g t) -> p g t", g=2) for s in (0, 1)]
        merged = tokens
        keyT = keyval[:, 0:13 * SEQ].rearrange("p (k t) -> p k t", k=13)
        value = keyval[:, 13 * SEQ:].rearrange("p (c n) -> p c n", c=TB)
        xn2 = queryT[:].rearrange("p a b t -> p (a b t)").rearrange("p (c d) -> p c d", c=TB)
        ysum = featT[:].rearrange("p k t -> p (k t)").rearrange("p (c d) -> p c d", c=TB)
        x_pair = keyval[:, 0:KC * P].rearrange("p (k s) -> p k s", k=KC)
        y_pair = keyval[:, KC * P:2 * KC * P]
        biasX = bias[:, 0:16 * 256].rearrange("p (h k) -> p h k", h=16)
        biasY = bias[:, 16 * 256:].rearrange("p (h k) -> p h k", h=16)
        rowg, rowb = bias[:, 0:D], bias[:, D:2 * D]
        row2g, row2b = bias[:, D:2 * D], keyval[:, 2 * KC * P:2 * KC * P + D]
        slots = [ring[:, i, :] for i in range(SLOTS)] + [acc_col[:], bias[:, 2 * D:3 * D], g1b[:], bias[:, 0:D]]
        pc = keyT[:, 11:13, :].rearrange("p k t -> p (k t)")
        pcT = value[:, 1, V_C + 512:V_C + 1024]
        swork = [work[:, 0:1536], work[:, 1536:3072]]
        ptw = work[:, 3072:4608]
        e_gate, hid, hidT = work[:, 0:DE], work[:, DE:2 * DE], work[:, 2 * DE:3 * DE]

        dist = work[:, 0:384]
        rt = work[:, 3072:3840].rearrange("p (i c e) -> p i c e", i=12, c=TB)
        sel = work[:, 3840:4096].rearrange("p (c e s) -> p c e s", c=TB, e=2)
        selg = work[:, 4096:4352].rearrange("p (c e s) -> p c e s", c=TB, e=2)
        scatter = work[:, 4352:4608]

        ident = sb("ident", [P, P])
        ones = sb("ones", [P, P])
        neg_ones = sb("neg_ones", [P, P])
        neg_tri = sb("neg_tri", [P, P])
        before = sb("before", [P, P])
        slot_id = sb("slot_id", [P, 2, WIN])
        cmp_bias = sb("cmp_bias", [P, TB, HB, NCMP])
        cmp_mask = sb("cmp_mask", [P, TB * HB, NCMP])
        cvec = sb("cvec", [P, KC])
        cs = sb("cs", [P, KC])
        ctmp = sb("ctmp", [P, KC])
        sinkb = sb("sinkb", [P, HA])
        gaincol = sb("gaincol", [P, KC])
        pe2 = sb("pe2", [P, 2, CMP_STEP])
        w2 = sb("w2", [P, 2, HD])
        wr = sb("wr", [P, KC, NG + NE])
        bcols = sb("bcols", [P, 4, KC])
        brow = sb("brow", [P, NG + NE])
        gbw = sb("gbw", [P, KC, 3 * HB])
        gates = sb("gates", [P, TB, HB, 3])
        cols = sb("cols", [P, 4, KC])
        stats = sb("stats", [P, TB, 4, 6])
        mv = sb("mv", [P, TB, 2])
        rstd = sb("rstd", [P, TB])
        free_mark = sb("free_mark", [P, 2])
        nb = sb("nb", [P, TB])
        mx = sb("mx", [P, 2, TB, 4])
        nmx = sb("nmx", [P, 2, TB, 4])
        den = sb("den", [P, 2, TB, 4])
        den2 = sb("den2", [P, 2, TB, 4])
        hidc = sb("hidc", [P, 4, 2, 2, 16])
        kcmpT = sb("kcmpT", [P, 16])
        vblk = sb("vblk", [P, 2, 256])
        cst = sb("cst", [P, 4, TB * HB])
        ssq = sb("ssq", [P, TB, 3])
        minus_half = sb("minus_half", [P, TB * 3])
        lg = sb("lg", [P, TB, NG + NE])
        r1 = sb("r1", [P, 10, TB])
        rankm = sb("rankm", [P, TB, NE])
        gate_te = sb("gate_te", [P, TB, NE])
        more = sb("more", [P, PASSES], I32)

        full = [sem(f"ring_full_{i}") for i in range(MOE_SLOTS)]
        pe_freed = sem("pe_freed")
        dve_freed = sem("dve_freed")
        x_in = [sem(f"x_in_{c}") for c in range(TB)]
        c_in, small_in, ln_in, xr_in = (sem(n) for n in ("c_in", "small_in", "ln_in", "xr_in"))
        gate_bias_in, cols_in = sem("gate_bias_in"), sem("cols_in")
        small_taken = sem("small_taken")
        ab_merged = sem("ab_merged")
        g2_sum, g2_taken = sem("g2_sum"), sem("g2_taken")
        stored = sem("stored")
        pool_s = sem("pool_steps")
        dve_s = sem("dve_steps")
        act_s = sem("act_steps")
        ec_ready = sem("ec_ready")
        xn_ready = sem("xn_ready")
        xnT_full = sem("xnT_full")
        xnT_copied = sem("xnT_copied")
        windows_moved = sem("windows_moved")
        ada_sums = sem("ada_sums")
        mod_sums, mod_taken = sem("mod_sums"), sem("mod_taken")
        ada_taken = sem("ada_taken")
        hT_ready = sem("hT_ready")
        gate_mm = sem("gate_mm")
        var_ready, rstd_ready = sem("var_ready"), sem("rstd_ready")
        x2T_dve, x2T_act = sem("x2T_dve"), sem("x2T_act")
        proj_taken = sem("proj_taken")
        cmp_in_ready, cmp_act, cmp_kv, cmp_s, cmp_p, cmp_pt, cmp_o = (
            sem(n) for n in ("cmp_in_ready", "cmp_act", "cmp_kv", "cmp_s", "cmp_p",
                             "cmp_pt", "cmp_o"))
        cmp_h_ready, cmp_e, cmp_sm, cmp_ex = (sem(n) for n in ("cmp_h_ready", "cmp_e", "cmp_sm", "cmp_ex"))
        gate_e = sem("gate_e")
        s_done, s_taken, m_ready, exp_done, sink_done, pt_full, pt_taken, o_full = (
            sem(n) for n in ("s_done", "s_taken", "m_ready", "exp_done", "sink_done", "pt_full", "pt_taken",
                             "o_full"))
        z_done, l_done, sp_done, lmask, zr_done, clamp_done, a_done, a_masked, oc_full = (
            sem(n) for n in ("z_done", "l_done", "sp_done", "lmask", "zr_done", "clamp_done", "a_done",
                             "a_masked", "oc_full"))
        sq_done, merged_ready, mT_full, mT_even, mT_odd = (
            sem(n) for n in ("sq_done", "merged_ready", "mT_full", "mT_even", "mT_odd"))
        y_full, nb_ready, xn2_ready, x2T_full, route_mm, rtab_ready, rank_full, route_ready = (
            sem(n) for n in ("y_full", "nb_ready", "xn2_ready", "x2T_full", "route_mm", "rtab_ready",
                             "rank_full", "route_ready"))
        moe_zeroed = sem("moe_zeroed")
        rexp_in, rexp_out = sem("rexp_in"), sem("rexp_out")
        misc_full, misc_free, sel_ready, e_ready, hid_ready = (
            sem(n) for n in ("misc_full", "misc_free", "sel_ready", "e_ready", "hid_ready"))
        ysb_ready, selg_ready, moe_s, fin_s, out_ready = (
            sem(n) for n in ("ysb_ready", "selg_ready", "moe_steps", "fin_steps", "out_ready"))

        uses = [0] * SLOTS
        unit_at, need = [], []
        seen = {"pe": 0, "dve": 0}
        for n, u in enumerate(UNITS):
            s = n % SLOTS
            uses[s] += 1
            unit_at.append((s, 16 * uses[s]))
            reader = "pe" if u[0] in PE_UNITS else "dve"
            seen[reader] += 1
            need.append((reader, seen[reader]))
        PE_BASE = seen["pe"]

        def arrived(eng, n):
            eng.wait_ge(full[unit_at[n][0]], unit_at[n][1])

        def index_of(kind, a, b):
            return UNITS.index((kind, a, b))

        def freed_after(kind, a, b):
            return need[index_of(kind, a, b)][1]

        def group_done(gi):
            return freed_after("win", gi, units_of(gi) - 1)

        def bank_of(gi):
            return 2 * gi if gi < 2 else 3 + 2 * (gi % 2)

        small_uses = [u for u in SCHEDULE if u[0] in ("values", "rows", "gates", "w1", "cmp_kv", "cmp_s", "cmp_t",
                                                      "cmp_o", "columns", "sticks")
                      and (u[0] != "w1" or u[1:] == (1, 0)) and u != ("columns", 4, 0)]

        def small_turn(*item):
            return small_uses.index(item)

        def z_base(b):
            return (0, 0, 0, 5)[b] * BN

        def ada_done(sixth):
            return need[UNITS.index(("ada", KC - 1, sixth))][1]

        def pair_slot(j):
            j %= MOE_SLOTS
            return SLOTS + j if j < 2 else (N_UNITS + j - 2) % SLOTS if j < SLOTS + 2 else j

        def pair_value(j):
            s = pair_slot(j)
            return 16 * ((uses[s] if s < SLOTS else 0) + j // MOE_SLOTS + 1)

        PAIR_FULL = 16 * PAIR_UNITS // MOE_SLOTS

        block = ctx.enter_context(nc.Block())

        @block.sync
        def _(sp):
            for c in range(TB):
                sp.dma_start(tokens[:, c, :], x[c * P:(c + 1) * P, :]).then_inc(x_in[c], 16)
            for n, (kind, a, b) in enumerate(UNITS):
                slot = ring[:, n % SLOTS, :]
                if n >= SLOTS:
                    who, count = need[n - SLOTS]
                    sp.wait_ge(pe_freed if who == "pe" else dve_freed, count)
                if kind == "ada":
                    sp.dma_start(slot, w_ada[a * P:(a + 1) * P, b * D:(b + 1) * D]).then_inc(full[n % SLOTS], 16)
                elif kind == "mod":
                    sp.dma_start(slot, w_mod[a * (KC // 2) + b]).then_inc(full[n % SLOTS], 16)
                elif kind == "win":
                    sp.dma_start(slot, w_in[first_unit(a) + b]).then_inc(full[n % SLOTS], 16)
                elif kind == "w1":
                    w1 = (w1_k, w1_v)[a]
                    sp.dma_start(slot, w1).then_inc(full[n % SLOTS], 16)
                else:
                    sp.dma_start(slot, w_out[a * P:(a + 1) * P, :]).then_inc(full[n % SLOTS], 16)

            def load(j, p, q):
                what, which, quarter = pair_unit(j)
                slot = slots[pair_slot(j)]
                if what == "down":
                    off = sp.snap((p * 2 + which) * DE + quarter * P)
                    src = w_down[bass.ds(off, P), :]
                    dst = slot
                else:
                    w = w_gate if what == "gate" else w_up
                    off = sp.snap((p * 2 + which) * D + quarter * 4 * P)
                    src = w[bass.ds(off, 4 * P), :].rearrange("(p k) n -> p k n", k=4)
                    dst = slot.rearrange("p (k n) -> p k n", k=4)
                value = sp.snap(q * PAIR_UNITS + (PE_BASE + j - MOE_SLOTS + 1))
                sp.wait_ge(pe_freed, value)
                sp.dma_start(dst, src).then_inc(full[pair_slot(j)], 16)

            HALF = PAIR_UNITS // 2
            for j in range(MOE_SLOTS):
                what, which, quarter = pair_unit(j)
                w = w_gate if what == "gate" else w_up
                if j == 0:
                    sp.wait_ge(ada_sums, 3)
                    sp.wait_ge(m_ready, 6)
                elif 2 <= j < SLOTS + 2:
                    who, count = need[N_UNITS + j - 2 - SLOTS]
                    sp.wait_ge(pe_freed if who == "pe" else dve_freed, count)
                elif j == SLOTS + 2:
                    sp.wait_ge(xn2_ready, 2)
                sp.dma_start(slots[pair_slot(j)].rearrange("p (k n) -> p k n", k=4),
                             w[which * D + quarter * 4 * P:which * D + (quarter + 1) * 4 * P, :]
                             .rearrange("(p k) n -> p k n", k=4)).then_inc(full[pair_slot(j)], 16)
            with sp.Fori(0, PAIRS - 1) as p:
                for j in range(HALF, PAIR_UNITS):
                    load(j, p, p)
                for j in range(HALF):
                    load(j, p + 1, p + 1)
            for j in range(HALF, PAIR_UNITS):
                load(j, PAIRS - 1, PAIRS - 1)
            sp.wait_ge(route_ready, PASSES)
            again = sp.value_load(more[0:1, 1:2])
            with sp.If(again > 0):
                with sp.Fori(1, PASSES) as w:
                    go = sp.value_load(more[0:1, bass.ds(w, 1)])
                    with sp.If(go > 0):
                        with sp.Fori(0, PAIRS) as p:
                            for j in range(PAIR_UNITS):
                                load(j, p, w * PAIRS + p)
            for c in range(TB):
                for half in (0, 1):
                    f = slice(half * D // 2, (half + 1) * D // 2)
                    sp.wait_ge(out_ready, 2 * c + half + 1)
                    sp.dma_start(out[c * P:(c + 1) * P, f], tokens[:, c, f]).then_inc(stored, 16)
            sp.wait_ge(stored, 32 * TB)

        @block.gpsimd
        def _(pool):
            st = Steps(pool, pool_s)
            g = nc.gpsimd
            st(g.memset(minus_half[:], -0.5))
            st(g.memset(ident[:], 0.0))
            st(g.memset(ones[:], 1.0))
            st(g.memset(neg_ones[:], -1.0))
            st.wait()
            st(g.affine_select(out=ident[:], in_=ident[:], compare_op=ALU.not_equal, fill=1.0, base=0,
                               pattern=[[-1, P]], channel_multiplier=1))
            st(g.affine_select(out=neg_tri[:], in_=neg_ones[:], compare_op=ALU.is_ge, fill=0.0, base=0,
                               pattern=[[-1, P]], channel_multiplier=1))
            st(g.affine_select(out=before[:], in_=ones[:], compare_op=ALU.is_gt, fill=0.0, base=0,
                               pattern=[[1, P]], channel_multiplier=-1))
            norms = [0]

            def rsqrt_variance(c):
                norms[0] += 1
                pool.wait_ge(var_ready, norms[0])
                g.tensor_tensor(rstd[:, c:c + 1], rstd[:, c:c + 1], minus_half[:, 0:1], ALU.pow).then_inc(rstd_ready, 1)

            for c in range(TB):
                rsqrt_variance(c)
            st(g.memset(g1b[:], 0.0))
            st(g.memset(g2b[:], 0.0))
            st(g.iota(slot_id[:], pattern=[[0, 2], [1, WIN]], base=0, channel_multiplier=0,
                      allow_small_or_imprecise_dtypes=True))
            st(g.memset(queryT[:].rearrange("p a b t -> p (a b t)"), 0.0))
            st(g.iota(dist[:, 0:256], pattern=[[-1, 256]], base=P, channel_multiplier=1,
                      allow_small_or_imprecise_dtypes=True))
            st(g.iota(dist[:, 256:384], pattern=[[-1, P]], base=0, channel_multiplier=1,
                      allow_small_or_imprecise_dtypes=True))
            st(g.iota(cmp_bias[:], pattern=[[P, TB], [0, HB], [-CMP_STEP, NCMP]], base=1 - CMP_LEN,
                      channel_multiplier=1, allow_small_or_imprecise_dtypes=True))
            st(g.memset(cmp_mask[:], 1.0))
            st(g.memset(vblk[:], 0.0))
            st.wait()
            st(g.affine_select(out=cmp_mask[:], in_=cmp_mask[:], compare_op=ALU.is_ge, fill=0.0,
                               base=1 - CMP_LEN, pattern=[[P, TB], [0, HB], [-CMP_STEP, NCMP]],
                               channel_multiplier=1))
            for h in range(HB):
                st(g.tensor_scalar(cmp_bias[:, :, h, :], cmp_bias[:, :, h, :], -SLOPES[HA + h], None, ALU.mult))
            for h in range(HA + HB):
                st(g.tensor_scalar(biasX[:, h, :], dist[:, 0:256], -SLOPES[h], None, ALU.mult))
                st(g.tensor_scalar(biasY[:, h, :], dist[:, 256:384], -SLOPES[h], None, ALU.mult))
            st.wait()
            st(g.affine_select(out=cmp_bias[:], in_=cmp_bias[:], compare_op=ALU.is_ge, fill=MASKED,
                               base=1 - CMP_LEN, pattern=[[P, TB], [0, HB], [-CMP_STEP, NCMP]],
                               channel_multiplier=1))
            st(g.affine_select(out=biasY, in_=biasY, compare_op=ALU.is_ge, fill=MASKED, base=0,
                               pattern=[[0, 16], [-1, P]], channel_multiplier=1))
            st(g.affine_select(out=biasX, in_=biasX, compare_op=ALU.is_ge, fill=MASKED, base=P,
                               pattern=[[0, 16], [-1, 256]], channel_multiplier=1))
            st.wait()
            st(g.affine_select(out=biasX[:, 0:HA, :], in_=biasX[:, 0:HA, :], compare_op=ALU.is_ge, fill=MASKED,
                               base=-1, pattern=[[0, HA], [1, 256]], channel_multiplier=-1))
            st.wait()
            assert st.n == POOL_MASKS, st.n
            def diagonal(b, ready, done):
                s = swork[b % 2]
                pool.wait_ge(ready, b + 1)
                for v in (s[:, 0:1024].rearrange("p (h q) -> p h q", h=4)[:, :, 0:P],
                          s[:, 1024:1536].rearrange("p (h q) -> p h q", h=4)):
                    g.affine_select(out=v, in_=v, compare_op=ALU.is_gt, fill=0.0, base=0,
                                    pattern=[[0, 4], [1, P]], channel_multiplier=-1).then_inc(done, 1)

            for kind, b, _ in SCHEDULE:
                if kind == "suffix":
                    diagonal(b, sp_done, lmask)
                elif kind == "sticks":
                    diagonal(b, a_done, a_masked)
            norms[0] += 1
            pool.wait_ge(var_ready, norms[0])
            flat = ssq[:].rearrange("p c g -> p (c g)")
            g.tensor_tensor(flat, flat, minus_half[:], ALU.pow).then_inc(rstd_ready, 1)
            for c in (0, 0, 1, 1):
                rsqrt_variance(c)
            g.memset(y_pair, 0.0).then_inc(moe_zeroed, 1)
            g.memset(scatter, 0.0).then_inc(moe_zeroed, 1)
            pool.wait_ge(route_mm, 1)
            g.memset(ysum, 0.0).then_inc(moe_zeroed, 1)
            for c in (0, 1):
                rsqrt_variance(c)

        @block.scalar
        def _(act):
            sc = nc.scalar
            act.dma_start(cvec[:], cT).then_inc(c_in, 16)
            act.dma_start(bcols[:], b_cols).then_inc(cols_in, 16)
            smalls = [(gaincol[:], gain), (sinkb[:], sinks[0:1, :].partition_broadcast(P)),
                      (brow[:], b_route[0:1, :].partition_broadcast(P)), (wr[:], w_route),
                      (pe2[0:HD, 0, :], pe_k[:, 0:CMP_STEP]), (pe2[HD:P, 0, :], pe_k[:, CMP_STEP:]),
                      (pe2[0:HD, 1, :], pe_v[:, 0:CMP_STEP]), (pe2[HD:P, 1, :], pe_v[:, CMP_STEP:]),
                      (w2[:, 0, :], w2_k), (w2[:, 1, :], w2_v),
                      (gbw[:], w_gb)]
            for dst, src in smalls:
                act.dma_start(dst, src).then_inc(small_in, 16)
            assert len(smalls) == N_SMALL
            act.wait_ge(c_in, 16)
            sc.activation(ctmp[:], cvec[:], ACT.Exp, scale=-1.0).then_inc(ec_ready, 1)
            for b in range(8):
                act.wait_ge(xnT_full, b + 1)
                sc.copy(featT[:, 2 * b:2 * b + 2, :].rearrange("p k t -> p (k t)"), ps[:, b, :]).then_inc(xnT_copied, 1)
            act.wait_ge(pool_s, POOL_ROWS)
            act.dma_start(g1b[0:1, :], b_ada[0:1, 2 * D:3 * D]).then_inc(gate_bias_in, 16)
            act.dma_start(g2b[0:1, :], b_ada[0:1, 5 * D:6 * D]).then_inc(gate_bias_in, 16)

            def split_heads(banks, tiles, scale):
                src = psf[:, banks * BN:(banks + 2) * BN]
                for half in (0, 1):
                    rows = slice(half * HD, (half + 1) * HD)
                    dst = queryT[rows, half, tiles:tiles + 4, :].rearrange("p a t -> p (a t)")
                    sc.mul(dst, src[rows, :], scale).then_inc(proj_taken, 1)

            def take(dst, src):
                sc.copy(dst, src).then_inc(proj_taken, 1)

            def take_group(gi):
                bank = bank_of(gi)
                act.wait_ge(pe_freed, group_done(gi))
                if gi == 0:
                    act.wait_ge(pool_s, POOL_SETUP)
                    split_heads(bank, 0, 1.0)
                elif gi == 1:
                    take(keyT[:, K_A, :], ps[:, bank, 0:SEQ])
                    take(value[:, :, V_A:V_A + P], ps[:, bank, SEQ:2 * SEQ].rearrange("p (c n) -> p c n", c=TB))
                elif gi == 2:
                    split_heads(bank, 4, 1.0)
                elif gi == 4:
                    take(keyT[:, K_CMP, :], ps[:, bank, 0:SEQ])
                    take(keyT[:, V_CMP, :], ps[:, bank, SEQ:2 * SEQ])
                    act.wait_ge(proj_taken, 2 * AB_GROUPS)
                    for s in (0, 1):
                        act.dma_start(windows_of[s][0:HD, 1, :], keyT[HD:P, K_CMP + s, :]).then_inc(windows_moved, 16)
                        act.dma_start(windows_of[s][HD:P, 0, 0:SEQ - CMP_STEP],
                                      keyT[0:HD, K_CMP + s, CMP_STEP:]).then_inc(windows_moved, 16)
                elif gi == 3:
                    take(keyT[:, K_SEL:K_WIN + 1, :].rearrange("p k t -> p (k t)"), ps[:, bank, :])
                    take(value[:, :, V_SEL:V_WIN + P], ps[:, bank + 1, :].rearrange("p (c n) -> p c n", c=TB))
                else:
                    what, half = (gi - AB_GROUPS) % 3, (gi - AB_GROUPS) // 3
                    if what == 0:
                        split_heads(bank, 4 * half, SCALE)
                    elif what == 1:
                        k0 = K_C + 4 * half
                        for j in (0, 1):
                            take(keyT[:, k0 + 2 * j:k0 + 2 * j + 2, :].rearrange("p k t -> p (k t)"), ps[:, bank + j, :])
                    else:
                        v0 = V_C + 512 * half
                        for c in range(TB):
                            take(value[:, c, v0:v0 + 512], ps[:, bank + c, :])

            def gates_exp():
                act.wait_ge(small_taken, small_turn("gates", 0, 0) + 1)
                gf = gates[:].rearrange("p c h g -> p (c h g)")
                sc.activation(gf, gf, ACT.Exp, scale=-1.0).then_inc(gate_e, 1)

            def gelu_exp():
                act.wait_ge(cmp_h_ready, 1)
                sc.activation(hidc[:, 2, :, :, 0:NCMP], hidc[:, 2, :, :, 0:NCMP], ACT.Exp, scale=-GELU_C).then_inc(cmp_e, 1)

            def cmp_exp():
                act.wait_ge(cmp_sm, 1)
                v = pc.rearrange("p (a n) -> p a n", n=32)[:, :, 0:NCMP]
                sc.activation(v, v, ACT.Exp).then_inc(cmp_ex, 1)

            def softmax_exp(b):
                s = swork[b % 2]
                act.wait_ge(m_ready, b + 1)
                for blk, h, v in softmax_parts(s):
                    sc.activation(v, v, ACT.Exp, bias=nmx[:, b % 2, blk, h:h + 1],
                                  accum_out=den[:, b % 2, blk, h:h + 1]).then_inc(exp_done, 1)
                if b < 2:
                    sc.activation(den2[:, b], den2[:, b], ACT.Exp).then_inc(sink_done, 1)

            def take_turned(b):
                act.wait_ge(pt_full, b + 1)
                if b >= 1:
                    act.wait_ge(o_full, b)
                sc.copy(ptw, psf[:, 0:3 * BN]).then_inc(pt_taken, 1)

            def squares(blocks, groups):
                for blk in blocks:
                    for gi in groups:
                        lo, hi = ((0, 512), (512, 1024), (1024, 2048))[gi]
                        if squared[0]:
                            act.wait_ge(sq_done, squared[0])
                        sc.activation(ptw[:, 0:hi - lo], merged[:, blk, lo:hi], ACT.Square,
                                      accum_out=ssq[:, blk, gi:gi + 1]).then_inc(sq_done, 1)
                        squared[0] += 1

            squared = [0]

            def log_part(b):
                s = swork[b % 2]
                act.wait_ge(z_done, b + 1)
                if b < 2:
                    act.wait_ge(ab_merged, b + 3)
                else:
                    act.wait_ge(oc_full, b - 1)
                sc.activation(s, psf[:, z_base(b):z_base(b) + 1536], ACT.Abs).then_inc(act_s, 1)
                act.wait_ge(act_s, 2 * b + 1)
                sc.activation(s, s, ACT.Exp, scale=-1.0).then_inc(act_s, 1)
                act.wait_ge(act_s, 2 * b + 2)
                sc.activation(s, s, ACT.Ln, bias=1.0).then_inc(l_done, 1)

            for kind, a, b in SCHEDULE[:FIRST_WOUT]:
                if kind == "win" and b == units_of(a) - 1:
                    take_group(a)
                elif kind == "gates":
                    gates_exp()
                elif (kind, a, b) == ("w1", 1, 0):
                    gelu_exp()
                elif kind == "cmp_s":
                    cmp_exp()
                elif kind == "scores":
                    softmax_exp(a)
                elif kind == "turn":
                    take_turned(a)
                elif kind == "z":
                    log_part(a)
                elif kind == "suffix":
                    act.wait_ge(clamp_done, a + 1)
                    sc.activation(swork[a % 2], swork[a % 2], ACT.Exp).then_inc(a_done, 1)
                if (kind, a) == ("turn", 5):
                    act.dma_start(rowg, ln1_g[0:1, :].partition_broadcast(P)).then_inc(ln_in, 16)
                    act.dma_start(rowb, ln1_b[0:1, :].partition_broadcast(P)).then_inc(ln_in, 16)
                if (kind, a) == ("z", 1):
                    squares(range(TB), (0, 1))
            act.wait_ge(small_taken, len(small_uses))
            squares(range(TB), (2,))
            for b in range(1, 8, 2):
                act.wait_ge(mT_full, b + 1)
                for k in (2 * b, 2 * b + 1):
                    sc.mul(featT[:, k, :], ps[:, b, (k % 2) * SEQ:(k % 2 + 1) * SEQ],
                           gaincol[:, k:k + 1]).then_inc(mT_odd, 1)
            act.wait_ge(mT_full, 8)
            act.dma_start(tokens[:], x.rearrange("(c p) d -> p c d", p=P)).then_inc(xr_in, 16)
            for c in range(TB):
                act.wait_ge(nb_ready, c + 1)
                sc.activation(xn2[:, c, :], tokens[:, c, :], ACT.Identity, bias=nb[:, c:c + 1],
                              scale=rstd[:, c:c + 1]).then_inc(xn2_ready, 1)
                for b in ((0, 1, 2, 3), (1, 3))[c]:
                    act.wait_ge(x2T_full, 4 * c + b + 1)
                    for k in range(4 * b, 4 * b + 4):
                        sc.activation(featT[:, k, c * P:(c + 1) * P], ps[:, 4 * c + b, (k % 4) * P:(k % 4 + 1) * P],
                                      ACT.Identity, bias=cols[:, 2, k:k + 1],
                                      scale=cols[:, 3, k:k + 1]).then_inc(x2T_act, 1)
            act.wait_ge(rexp_in, 1)
            sc.activation(rt[:, 0, :, 0:NG], rt[:, 0, :, 0:NG], ACT.Exp).then_inc(rexp_out, 1)
            act.wait_ge(rexp_in, 2)
            sc.activation(rt[:, 1, :, 0:EPG], rt[:, 1, :, 0:EPG], ACT.Exp).then_inc(rexp_out, 1)

            act.wait_ge(g2_sum, 1)
            sc.activation(g2b[:], psf[:, 4 * BN:8 * BN], ACT.Identity, bias=1.0).then_inc(g2_taken, 1)

            def pair_act(q, w):
                act.wait_ge(pe_freed, q * PAIR_UNITS + (PE_BASE + 16))
                sc.activation(e_gate, ps[:, 0, :], ACT.Sigmoid).then_inc(e_ready, 1)
                act.wait_ge(pe_freed, q * PAIR_UNITS + (PE_BASE + 24))
                act.wait_ge(misc_full, q * MISC_PAIR + w * MISC_FLUSH + 12)
                sc.copy(y_pair, psf[:, 2 * BN:6 * BN]).then_inc(ysb_ready, 1)

            with act.Fori(0, PAIRS) as p:
                pair_act(p, 0)
            act.wait_ge(xn2_ready, 2)
            act.dma_start(row2g, ln2_g[0:1, :].partition_broadcast(P)).then_inc(ln_in, 16)
            act.dma_start(row2b, ln2_b[0:1, :].partition_broadcast(P)).then_inc(ln_in, 16)
            act.wait_ge(route_ready, PASSES)
            again = act.value_load(more[0:1, 1:2])
            with act.If(again > 0):
                with act.Fori(1, PASSES) as w:
                    go = act.value_load(more[0:1, bass.ds(w, 1)])
                    with act.If(go > 0):
                        with act.Fori(0, PAIRS) as p:
                            pair_act(w * PAIRS + p, w)

        @block.tensor
        def _(pe):
            mm = pe.matmul
            pe.wait_ge(pool_s, POOL_CONST)
            pe.wait_ge(xn_ready, TB)
            for b in range(8):
                for k in (2 * b, 2 * b + 1):
                    for c in range(TB):
                        last = pe.transpose(ps[:, b, (k % 2) * SEQ + c * P:(k % 2) * SEQ + (c + 1) * P],
                                            tokens[:, c, k * P:(k + 1) * P], ident[:])
                last.then_inc(xnT_full, 1)

            def ada_columns(tiles, bank, c0):
                for k, tile in enumerate(tiles):
                    last = mm(ps[:, bank, c0 + k:c0 + k + 1], tile, ones[:, 0:1],
                              start=True, stop=True)
                return last

            def ada_rows(acc):
                for n in range(4):
                    last = mm(ps[:, (0, 1, 2, SMALL)[n], :], ones[:], acc[:, n * BN:(n + 1) * BN], start=True, stop=True)
                last.then_inc(ada_sums, 1)

            def project(gi, i):
                bank = bank_of(gi)
                if i == 0 and gi >= 4:
                    pe.wait_ge(proj_taken, 2 * (gi - 1))
                width = WIN_GROUPS[gi][1]
                kn = UNIT // width
                pe.wait_ge(hT_ready, (i + 1) * kn)
                n = index_of("win", gi, i)
                arrived(pe, n)
                slot = ring[:, n % SLOTS, :].rearrange("p (k n) -> p k n", k=kn)
                for kk in range(kn):
                    k = i * kn + kk
                    first, final = k == 0, k == KC - 1
                    w = slot[:, kk, :]

                    def tile_T(lhsT, b, half):
                        return mm(ps[:, b, half * SEQ:(half + 1) * SEQ], lhsT, featT[:, k, :],
                                  start=first and half == 0, stop=final, skip_group_check=True)

                    if gi in (0, 2):
                        for j in range(4):
                            last = tile_T(w[:, j * P:(j + 1) * P], bank + j // 2, j % 2)
                    elif gi == 1:
                        tile_T(w[:, 0:P], bank, 0)
                        for c in range(TB):
                            last = mm(ps[:, bank, SEQ + c * P:SEQ + (c + 1) * P], featT[:, k, c * P:(c + 1) * P],
                                      w[:, P:2 * P], start=False, stop=final, skip_group_check=True)
                    elif gi == 4:
                        tile_T(w[:, 0:P], bank, 0)
                        last = tile_T(w[:, P:2 * P], bank, 1)
                    elif gi == 3:
                        tile_T(w[:, 0:P], bank, 0)
                        tile_T(w[:, 2 * P:3 * P], bank, 1)
                        vals = w.rearrange("p (s n) -> p s n", s=4)[:, 1:4:2, :]
                        for c in range(TB):
                            last = mm(ps[:, bank + 1, c * 2 * P:(c + 1) * 2 * P], featT[:, k, c * P:(c + 1) * P],
                                      vals, start=first and c == 0, stop=final, skip_group_check=True)
                    elif (gi - AB_GROUPS) % 3 < 2:
                        for j in range(4):
                            last = tile_T(w[:, j * P:(j + 1) * P], bank + j // 2, j % 2)
                    else:
                        for c in range(TB):
                            last = mm(ps[:, bank + c, :], featT[:, k, c * P:(c + 1) * P], w,
                                      start=first, stop=final)
                last.then_inc(pe_freed, 1)


            def small_bank(*item):
                turn = small_turn(*item)
                if turn:
                    pe.wait_ge(small_taken, turn)
                else:
                    pe.wait_ge(mod_taken, 4)

            def gate_products():
                small_bank("gates", 0, 0)
                pe.wait_ge(small_in, 16 * N_SMALL)
                for c in range(TB):
                    for k in range(KC):
                        last = mm(ps[:, SMALL, c * 24:(c + 1) * 24], featT[:, k, c * P:(c + 1) * P], gbw[:, k, :],
                                  start=k == 0, stop=k == KC - 1)
                last.then_inc(gate_mm, 1)

            def cmp_hidden(s):
                if s == 0:
                    small_bank("w1", 1, 0)
                    pe.wait_ge(cmp_in_ready, 8)
                n = index_of("w1", s, 0)
                arrived(pe, n)
                for j in range(CMP_STEP):
                    win = windows_of[s].rearrange("p g (n j) -> p g n j", j=CMP_STEP)[:, :, 0:NCMP, j]
                    last = mm(ps[:, SMALL, s * 64:s * 64 + 2 * NCMP], ring[:, n % SLOTS, j * P:(j + 1) * P], win,
                              start=j == 0, stop=j == CMP_STEP - 1)
                last.then_inc(pe_freed, 1)

            def cmp_keys_values():
                pe.wait_ge(cmp_act, 1)
                small_bank("cmp_kv", 0, 0)
                for g in (0, 1):
                    mm(ps[g * HD:(g + 1) * HD, SMALL, 0:NCMP], w2[:, 0, :], hidc[:, 3, 0, g, 0:NCMP], start=True, stop=True)
                for g in (0, 1):
                    for i in range(4):
                        last = mm(ps[32 * i:32 * i + NCMP, SMALL, P + g * HD:P + (g + 1) * HD], hidc[:, 3, 1, g, 0:NCMP],
                                  w2[:, 1, :], start=True, stop=True)
                last.then_inc(cmp_kv, 1)

            def cmp_scores():
                small_bank("cmp_s", 0, 0)
                for blk in range(TB):
                    for h in range(HB):
                        last = mm(ps[:, SMALL, (blk * HB + h) * 16:(blk * HB + h) * 16 + NCMP],
                                  queryT[:, h // 4, 4 + h % 4, blk * P:(blk + 1) * P], kcmpT[:, 0:NCMP],
                                  start=True, stop=True)
                last.then_inc(cmp_s, 1)

            def cmp_transpose():
                small_bank("cmp_t", 0, 0)
                pe.wait_ge(cmp_p, 1)
                for a in range(4):
                    last = pe.transpose(ps[:, SMALL, a * P:(a + 1) * P], pc[:, a * P:(a + 1) * P], ident[:])
                last.then_inc(cmp_pt, 1)

            def cmp_values(c):
                small_bank("cmp_o", c, 0)
                for a in (2 * c, 2 * c + 1):
                    last = mm(ps[:, SMALL, (a % 2) * 256:(a % 2 + 1) * 256], pcT[:, a * P:(a + 1) * P], vblk[:, a % 2, :],
                              start=True, stop=True)
                last.then_inc(cmp_o, 1)

            def scores(b):
                tiles, ktile = (0, K_A) if b < 2 else (4, (K_SEL, K_WIN)[(b - 2) // 2])
                g = b % 2
                pe.wait_ge(proj_taken, 4 if b < 2 else 8)
                if b >= 1:
                    pe.wait_ge(pt_taken, b)
                if b == 2:
                    pe.wait_ge(ada_taken, 1)
                for h in range(4):
                    q = queryT[:, g, tiles + h, :]
                    mm(psf[:, h * 256:(h + 1) * 256], q[:, P:2 * P], keyT[:, ktile, :], start=True, stop=True)
                    last = mm(psf[:, 2 * BN + h * P:2 * BN + (h + 1) * P], q[:, 0:P], keyT[:, ktile, 0:P],
                              start=True, stop=True)
                last.then_inc(s_done, 1)

            def turn_probabilities(b):
                s = swork[b % 2]
                pe.wait_ge(s_taken, b + 1)
                pe.wait_ge(exp_done, 8 * (b + 1))
                for n in range(12):
                    last = pe.transpose(psf[:, n * P:(n + 1) * P], s[:, n * P:(n + 1) * P], ident[:])
                last.then_inc(pt_full, 1)

            def weigh(b):
                v0 = (V_A, V_SEL, V_WIN)[b // 2] + (b % 2) * HD
                pe.wait_ge(pt_taken, b + 1)
                small_bank("values", b, 0)
                for h in range(4):
                    mm(ps[:, SMALL, h * HD:(h + 1) * HD], ptw[:, (8 + h) * P:(9 + h) * P], value[:, 0, v0:v0 + HD],
                       start=True, stop=True)
                    for c in range(TB):
                        last = mm(ps[:, SMALL, 256 + h * HD:256 + (h + 1) * HD], ptw[:, (2 * h + c) * P:(2 * h + c + 1) * P],
                                  value[:, c, v0:v0 + HD], start=c == 0, stop=c == TB - 1)
                last.then_inc(o_full, 1)

            def z_scores(b):
                base = z_base(b)
                pe.wait_ge(proj_taken, 2 * (AB_GROUPS + (2, 2, 5, 5)[b]))
                if b == 0:
                    pe.wait_ge(pt_taken, 6)
                elif b < 3:
                    pe.wait_ge(clamp_done, b)
                else:
                    small_bank("sticks", 2, 0)
                for i in range(4):
                    tile, half = 2 * b + i // 2, i % 2
                    k = keyT[:, K_C + tile, :]
                    q = queryT[:, half, tile, :]
                    mm(psf[:, base + i * 256:base + (i + 1) * 256], k[:, 0:P], q, start=i % 2 == 0, stop=False,
                       skip_group_check=True)
                    last = mm(psf[:, base + 1024 + i * P:base + 1024 + (i + 1) * P], k[:, P:2 * P], q[:, P:2 * P],
                              start=i == 0, stop=False, skip_group_check=True)
                last.then_inc(z_done, 1)

            def suffix_sums(b):
                base = z_base(b)
                s = swork[b % 2]
                pe.wait_ge(lmask, 2 * (b + 1))
                for n in range(3):
                    mm(psf[:, base + n * BN:base + (n + 1) * BN], neg_tri[:], s[:, n * BN:(n + 1) * BN],
                       start=False, stop=False, skip_group_check=True)
                for n in range(2):
                    dst = psf[:, base + n * BN:base + (n + 1) * BN].rearrange("p (h q) -> p h q", h=2)[:, :, P:2 * P]
                    src = s[:, 1024 + n * 256:1024 + (n + 1) * 256].rearrange("p (h q) -> p h q", h=2)
                    last = mm(dst, neg_ones[:], src, start=False, stop=True, skip_group_check=True)
                last.then_inc(zr_done, 1)

            def stick_values(b):
                s = swork[b % 2]
                pe.wait_ge(a_masked, 2 * (b + 1))
                pe.wait_ge(proj_taken, 2 * (AB_GROUPS + 3) if b < 2 else 2 * len(WIN_GROUPS))
                bank = (SMALL, SMALL, 0, 1)[b]
                if b < 2:
                    small_bank("sticks", b, 0)
                else:
                    pe.wait_ge(clamp_done, 3)
                for i in range(4):
                    v0 = V_C + (4 * b + i) * HD
                    mm(ps[:, bank, i * HD:(i + 1) * HD], s[:, i * 256:i * 256 + P], value[:, 0, v0:v0 + HD],
                       start=True, stop=True)
                    mm(ps[:, bank, 256 + i * HD:256 + (i + 1) * HD], s[:, i * 256 + P:(i + 1) * 256],
                       value[:, 0, v0:v0 + HD], start=True, stop=False)
                    last = mm(ps[:, bank, 256 + i * HD:256 + (i + 1) * HD], s[:, 1024 + i * P:1024 + (i + 1) * P],
                              value[:, 1, v0:v0 + HD], start=False, stop=True)
                last.then_inc(oc_full, 1)

            pe.wait_ge(xnT_copied, 8)
            for kind, a, b in SCHEDULE[:FIRST_WOUT]:
                if kind == "win":
                    project(a, b)
                elif kind == "w1":
                    cmp_hidden(a)
                elif kind == "scores":
                    scores(a)
                elif kind == "turn":
                    turn_probabilities(a)
                elif kind == "values":
                    weigh(a)
                elif kind == "modulate":
                    pe.wait_ge(dve_freed, need[UNITS.index(("mod", a, KC // 2 - 1))][1])
                    ada_columns([acc_col[:, (a % 2) * 1024 + i * P:(a % 2) * 1024 + (i + 1) * P] for i in range(8)], SMALL,
                                8 * a).then_inc(mod_sums, 1)
                elif kind == "rows":
                    pe.wait_ge(pt_taken, 2)
                    small_bank(kind, a, b)
                    pe.wait_ge(dve_freed, ada_done(a))
                    ada_rows(g1b[:])
                elif kind == "columns":
                    if a == 3:
                        small_bank(kind, a, b)
                    pe.wait_ge(dve_freed, ada_done(a))
                    ada_columns([acc_col[:, tile2(k)] for k in range(KC)], SMALL if a == 3 else 2, 0).then_inc(ada_sums, 1)
                elif kind == "gates":
                    gate_products()
                elif kind == "cmp_kv":
                    cmp_keys_values()
                elif kind == "cmp_s":
                    cmp_scores()
                elif kind == "cmp_t":
                    cmp_transpose()
                elif kind == "cmp_o":
                    cmp_values(a)
                elif kind == "z":
                    z_scores(a)
                elif kind == "suffix":
                    suffix_sums(a)
                elif kind == "sticks":
                    stick_values(a)

            pe.wait_ge(merged_ready, 6)
            pe.wait_ge(ada_taken, 2)
            for b in range(8):
                for k in (2 * b, 2 * b + 1):
                    for c in range(TB):
                        last = pe.transpose(ps[:, b, (k % 2) * SEQ + c * P:(k % 2) * SEQ + (c + 1) * P],
                                            merged[:, c, k * P:(k + 1) * P], ident[:])
                last.then_inc(mT_full, 1)
            pe.wait_ge(mT_even, KC // 2)
            pe.wait_ge(mT_odd, KC // 2)

            def out_product(c, j, k):
                n = index_of("wout", k, 0)
                return mm(ps[:, 4 * c + j, :], featT[:, k, c * P:(c + 1) * P], ring[:, n % SLOTS, j * BN:(j + 1) * BN],
                          start=k == 0, stop=k == KC - 1)

            def turn_x2(c):
                pe.wait_ge(xn2_ready, c + 1)
                for b in range(4):
                    for k in range(4 * b, 4 * b + 4):
                        last = pe.transpose(ps[:, 4 * c + b, (k % 4) * P:(k % 4 + 1) * P], xn2[:, c, tile2(k)],
                                            ident[:])
                    last.then_inc(x2T_full, 1)

            for k in range(KC - HELD):
                arrived(pe, index_of("wout", k, 0))
                for c in range(TB):
                    for j in range(4):
                        last = out_product(c, j, k)
                last.then_inc(pe_freed, 1)
            for c in range(TB):
                for j in range(4):
                    for k in range(KC - HELD, KC):
                        if (c, j) == (0, 0):
                            arrived(pe, index_of("wout", k, 0))
                        last = out_product(c, j, k)
                        if (c, j) == (1, 3):
                            last.then_inc(pe_freed, 1)
                    if (c, j) != (1, 3):
                        last.then_inc(y_full, 1)
            for c in range(TB):
                turn_x2(c)
                for k in range(KC):
                    if k % 4 == 0 and c == 0:
                        pe.wait_ge(x2T_act, k + 4)
                    elif k % 8 == 0:
                        pe.wait_ge(x2T_dve, k // 2 + 4)
                    elif k % 4 == 0:
                        pe.wait_ge(x2T_act, KC + (k - 4) // 2 + 4)
                    last = mm(ps[:, 0, c * 36:(c + 1) * 36], featT[:, k, c * P:(c + 1) * P], wr[:, k, :],
                              start=k == 0, stop=k == KC - 1)
            last.then_inc(route_mm, 1)
            pe.wait_ge(dve_freed, ada_done(5))
            for n in range(4):
                last = mm(ps[:, 4 + n, :], ones[:], g2b[:, n * BN:(n + 1) * BN], start=True, stop=True)
            last.then_inc(g2_sum, 1)
            routed = rt[:, 2]
            pe.wait_ge(rtab_ready, 1)
            mm(ps[:, 1, 0:NE], before[:], routed[:, 0, :], start=True, stop=True)
            mm(ps[:, 1, NE:2 * NE], ones[:], routed[:, 0, :], start=True, stop=False)
            mm(ps[:, 1, NE:2 * NE], before[:], routed[:, 1, :], start=False, stop=True)
            mm(ps[:, 1, 2 * NE:3 * NE], ones[:], routed[:, 0, :], start=True, stop=False)
            mm(ps[:, 1, 2 * NE:3 * NE], ones[:], routed[:, 1, :], start=False, stop=True).then_inc(rank_full, 1)

            def scatter_bank(use, i):
                c, n = i // 4, i % 4
                mm(use(), scatter[:, c * P:(c + 1) * P], y_pair[:, n * BN:(n + 1) * BN],
                   start=True, stop=True).then_inc(misc_full, 1)

            def misc(turn):
                count = [0]

                def use():
                    count[0] += 1
                    pe.wait_ge(misc_free, turn + count[0])
                    return ps[:, 6 + (count[0] - 1) % 2, :]
                return use

            def pair_pe(q, w):
                turn = q * MISC_PAIR + w * MISC_FLUSH
                use = misc(turn)
                pe.wait_ge(sel_ready, q + 1)

                def gather(quarter):
                    bank = use()
                    for k in range(4 * quarter, 4 * quarter + 4):
                        for c in range(TB):
                            last = mm(bank[:, (k % 4) * P:(k % 4 + 1) * P], xn2[:, c, tile2(k)],
                                      sel[:, c].rearrange("p e s -> p (e s)"), start=c == 0, stop=c == TB - 1)
                    last.then_inc(misc_full, 1)

                gather(0)
                for quarter in range(4):
                    if quarter == 0:
                        pe.wait_ge(ysb_ready, q)
                    for i in (0, 1):
                        scatter_bank(use, 2 * quarter + i)
                    if quarter < 3:
                        gather(quarter + 1)
                    else:
                        pe.wait_ge(selg_ready, q + 1)
                        bank = use()
                        for c in range(TB):
                            last = pe.transpose(bank[:, c * P:(c + 1) * P], selg[:, c].rearrange("p e s -> p (e s)"),
                                                ident[:])
                        last.then_inc(misc_full, 1)
                    pe.wait_ge(misc_free, turn + 3 * quarter + 3)
                    if quarter == 0:
                        pe.wait_ge(hid_ready, q)
                    for m in (0, 1):
                        j = 4 * quarter + 2 * m
                        for e in (0, 1):
                            pe.wait_ge(full[pair_slot(j + e)], q * PAIR_FULL + pair_value(j + e))
                        for kk in range(4):
                            k = 4 * quarter + kk
                            for e in (0, 1):
                                last = mm(ps[e * WIN:(e + 1) * WIN, m, :], x_pair[:, k, e * WIN:(e + 1) * WIN],
                                          slots[pair_slot(j + e)][:, kk * BN:(kk + 1) * BN],
                                          start=k == 0, stop=k == KC - 1)
                                if kk == 3:
                                    last.then_inc(pe_freed, 1)
                pe.wait_ge(hid_ready, q + 1)
                bank = use()
                for k in range(DE // P):
                    last = pe.transpose(bank[:, k * P:(k + 1) * P], hid[:, k * P:(k + 1) * P], ident[:])
                last.then_inc(misc_full, 1)
                pe.wait_ge(misc_free, turn + 16)
                for k in range(DE // P):
                    j = 16 + 2 * k
                    for e in (0, 1):
                        pe.wait_ge(full[pair_slot(j + e)], q * PAIR_FULL + pair_value(j + e))
                    for n in range(4):
                        for e in (0, 1):
                            last = mm(ps[e * WIN:(e + 1) * WIN, 2 + n, :],
                                      hidT[:, k * P + e * WIN:k * P + (e + 1) * WIN],
                                      slots[pair_slot(j + e)][:, n * BN:(n + 1) * BN],
                                      start=k == 0, stop=k == DE // P - 1)
                            if n == 3:
                                last.then_inc(pe_freed, 1)

            def flush_pe(w):
                use = misc((w + 1) * (PAIRS * MISC_PAIR) + w * MISC_FLUSH)
                pe.wait_ge(ysb_ready, (w + 1) * PAIRS)
                pe.wait_ge(misc_free, (w + 1) * (PAIRS * MISC_PAIR) + w * MISC_FLUSH + 1)
                for i in range(8):
                    scatter_bank(use, i)

            pe.wait_ge(g2_taken, 1)
            pe.wait_ge(moe_zeroed, 3)
            with pe.Fori(0, PAIRS) as p:
                pair_pe(p, 0)
            flush_pe(0)
            pe.wait_ge(route_ready, PASSES)
            again = pe.value_load(more[0:1, 1:2])
            with pe.If(again > 0):
                with pe.Fori(1, PASSES) as w:
                    go = pe.value_load(more[0:1, bass.ds(w, 1)])
                    with pe.If(go > 0):
                        with pe.Fori(0, PAIRS) as p:
                            pair_pe(w * PAIRS + p, w)
                        flush_pe(w)

        @block.vector
        def _(dve):
            st = Steps(dve, dve_s)
            freed = [0]

            def ada(k, sixth):
                n = index_of("ada", k, sixth)
                dst = {2: g1b, 3: acc_col, 4: acc_col, 5: g2b}[sixth][:]
                src, scalar = ring[:, n % SLOTS, :], cs[:, k:k + 1]
                arrived(dve, n)
                if k == 0 and sixth == 2:
                    dve.wait_ge(gate_bias_in, 32)
                if k:
                    dve.wait_ge(dve_freed, need[n][1] - 1)
                if k == 0 and sixth in (3, 4):
                    if sixth == 3:
                        dve.wait_ge(mod_sums, 4)
                    else:
                        dve.wait_ge(ada_sums, 2)
                    dve.tensor_scalar(dst, src, scalar, None, ALU.mult).then_inc(dve_freed, 1)
                else:
                    dve.scalar_tensor_tensor(out=dst, in0=src, scalar=scalar, in1=dst,
                                             op0=ALU.mult, op1=ALU.add).then_inc(dve_freed, 1)

            def mod_unit(q, i):
                n = index_of("mod", q, i)
                dst = acc_col[:, (q % 2) * 1024:(q % 2 + 1) * 1024]
                arrived(dve, n)
                if i == 0 and q >= 2:
                    dve.wait_ge(mod_sums, q - 1)
                for kk in (0, 1):
                    k = 2 * i + kk
                    src, scalar = ring[:, n % SLOTS, kk * 1024:(kk + 1) * 1024], cs[:, k:k + 1]
                    if k == 0:
                        st(dve.tensor_scalar(dst, src, scalar, None, ALU.mult))
                        continue
                    if kk:
                        st.wait()
                    else:
                        dve.wait_ge(dve_freed, need[n][1] - 1)
                    ins = dve.scalar_tensor_tensor(out=dst, in0=src, scalar=scalar, in1=dst, op0=ALU.mult, op1=ALU.add)
                    if kk:
                        ins.then_inc(dve_freed, 1)
                    else:
                        st(ins)

            def modulate(q):
                dve.wait_ge(mod_sums, q + 1)
                if q == 0:
                    dve.wait_ge(cols_in, 16)
                f = slice(4 * q, 4 * q + 4)
                st(dve.tensor_tensor(cols[:, 0, f], ps[:, 7, 8 * q:8 * q + 4], bcols[:, 0, f], ALU.add))
                dve.scalar_tensor_tensor(out=cols[:, 1, f], in0=ps[:, 7, 8 * q + 4:8 * q + 8], scalar=1.0,
                                         in1=bcols[:, 1, f], op0=ALU.add, op1=ALU.add).then_inc(mod_taken, 1)
                st.wait()
                dve.wait_ge(mod_taken, q + 1)
                dve.wait_ge(xnT_copied, 8)
                for k in range(4 * q, 4 * q + 4):
                    dve.tensor_scalar(featT[:, k, :], featT[:, k, :], cols[:, 1, k:k + 1], cols[:, 0, k:k + 1],
                                      ALU.mult, ALU.add).then_inc(hT_ready, 1)

            norms = [0]

            def variance(c):
                st.wait()
                st(dve.bn_aggr(mv[:, c, :], stats[:, c].rearrange("p n s -> p (n s)")))
                st.wait()
                dve.tensor_scalar(rstd[:, c:c + 1], mv[:, c, 1:2], 1e-5, None, ALU.add).then_inc(var_ready, 1)

            def deviation():
                norms[0] += 1
                dve.wait_ge(rstd_ready, norms[0])

            def inverse_deviation(c):
                variance(c)
                deviation()

            def normalise(src, dst, c):
                for n in range(4):
                    st(dve.bn_stats(stats[:, c, n, :], src[:, n * BN:(n + 1) * BN]))
                inverse_deviation(c)
                return dve.tensor_scalar(dst, src, mv[:, c, 0:1], rstd[:, c:c + 1], ALU.subtract, ALU.mult)

            for c in range(TB):
                dve.wait_ge(x_in[c], 16)
                normalise(tokens[:, c, :], tokens[:, c, :], c).then_inc(xn_ready, 1)
            dve.wait_ge(ec_ready, 1)
            st(dve.tensor_scalar(ctmp[:], ctmp[:], 1.0, None, ALU.add))
            st.wait()
            st(dve.reciprocal(ctmp[:], ctmp[:]))
            st.wait()
            st(dve.tensor_tensor(cs[:], cvec[:], ctmp[:], ALU.mult))
            st.wait()
            H = [hidc[:, i, :, :, 0:NCMP] for i in range(4)]
            gf = gates[:].rearrange("p c h g -> p (c h g)")

            def windows():
                dve.wait_ge(small_in, 16 * N_SMALL)
                dve.wait_ge(proj_taken, 2 * AB_GROUPS)
                cut = NCMP * CMP_STEP

                def add(rows, s, g, src):
                    pe16 = pe2[rows, s, :].unsqueeze(1).broadcast_to([HD, NCMP, CMP_STEP])
                    dve.tensor_tensor(windows_of[s][rows, g, 0:cut].rearrange("p (n j) -> p n j", n=NCMP),
                                      src.rearrange("p (n j) -> p n j", n=NCMP), pe16, ALU.add).then_inc(cmp_in_ready, 1)

                for s in (0, 1):
                    add(slice(0, HD), s, 0, keyT[0:HD, K_CMP + s, 0:cut])
                    add(slice(HD, P), s, 1, keyT[HD:P, K_CMP + s, CMP_STEP:])
                dve.wait_ge(windows_moved, 4 * 16)
                for s in (0, 1):
                    add(slice(0, HD), s, 1, windows_of[s][0:HD, 1, 0:cut])
                    add(slice(HD, P), s, 0, windows_of[s][HD:P, 0, 0:cut])
                st(dve.memset(pc, 0.0))

            def gate_values():
                dve.wait_ge(gate_mm, 1)
                dve.tensor_copy(gf, ps[:, SMALL, 0:TB * 3 * HB]).then_inc(small_taken, 1)
                dve.wait_ge(gate_e, 1)
                st(dve.tensor_scalar(gf, gf, 1.0, None, ALU.add))
                st.wait()
                st(dve.reciprocal(gf, gf))

            def gelu():
                dve.wait_ge(pe_freed, freed_after("w1", 1, 0))
                dve.tensor_copy(H[0], ps[:, SMALL, 0:P].rearrange("p (s x) -> p s x", s=2)[:, :, 0:2 * NCMP]
                                .rearrange("p s (g n) -> p s g n", g=2)).then_inc(small_taken, 1)
                dve.wait_ge(small_taken, small_turn("w1", 1, 0) + 1)
                st(dve.tensor_tensor(H[1], H[0], H[0], ALU.mult))
                st.wait()
                st(dve.tensor_scalar(H[1], H[1], 0.044715, 1.0, ALU.mult, ALU.add))
                st.wait()
                dve.tensor_tensor(H[2], H[1], H[0], ALU.mult).then_inc(cmp_h_ready, 1)
                dve.wait_ge(cmp_e, 1)
                st(dve.tensor_scalar(H[1], H[2], 1.0, None, ALU.add))
                st.wait()
                st(dve.reciprocal(H[1], H[1]))
                st.wait()
                dve.tensor_tensor(H[3], H[0], H[1], ALU.mult).then_inc(cmp_act, 1)

            def cmp_take():
                dve.wait_ge(cmp_kv, 1)
                for i in range(4):
                    rows = slice(32 * i, 32 * i + NCMP)
                    st(dve.tensor_copy(vblk[rows, :, i * HD:(i + 1) * HD],
                                       ps[rows, SMALL, P:2 * P].rearrange("p (g d) -> p g d", g=2)))
                dve.tensor_copy(kcmpT[:, 0:NCMP], ps[:, SMALL, 0:NCMP]).then_inc(small_taken, 1)

            def cmp_softmax():
                pcv = pc.rearrange("p (a n) -> p a n", n=32)[:, :, 0:NCMP]
                sv = ps[:, SMALL, 0:256].rearrange("p (a n) -> p a n", n=16)[:, :, 0:NCMP]
                dve.wait_ge(cmp_s, 1)
                dve.scalar_tensor_tensor(out=pcv, in0=sv, scalar=SCALE, in1=cmp_bias[:].rearrange("p c h n -> p (c h) n"),
                                         op0=ALU.mult, op1=ALU.add).then_inc(small_taken, 1)
                dve.wait_ge(small_taken, small_turn("cmp_s", 0, 0) + 1)
                st(dve.tensor_reduce(cst[:, 0, :], pcv, AX.X, ALU.max))
                st.wait()
                wide = [P, TB * HB, NCMP]
                dve.tensor_tensor(pcv, pcv, cst[:, 0, :].unsqueeze(2).broadcast_to(wide), ALU.subtract).then_inc(cmp_sm, 1)
                dve.wait_ge(cmp_ex, 1)
                dve.tensor_tensor(pcv, pcv, cmp_mask[:], ALU.mult).then_inc(cmp_p, 1)
                dve.wait_ge(cmp_p, 1)
                st(dve.tensor_reduce(cst[:, 1, :], pcv, AX.X, ALU.add))
                st.wait()
                st(dve.tensor_scalar(cst[:, 2, :], cst[:, 1, :], 1e-30, None, ALU.max))
                st.wait()
                st(dve.reciprocal(cst[:, 2, :], cst[:, 2, :]))
                st.wait()
                st(dve.tensor_tensor(cst[:, 3, :], cst[:, 2, :], gf.rearrange("p (x g) -> p x g", g=3)[:, :, 0], ALU.mult))

            def cmp_take_turned():
                dve.wait_ge(cmp_pt, 1)
                dve.tensor_copy(pcT, ps[:, SMALL, :]).then_inc(small_taken, 1)

            def cmp_outputs(c):
                dve.wait_ge(cmp_o, c + 1)
                st.wait()
                o = ps[:, SMALL, :].rearrange("p (h d) -> p h d", h=HB)
                r = cst[:, 3, c * HB:(c + 1) * HB].unsqueeze(2).broadcast_to([P, HB, HD])
                dve.tensor_tensor(merged[:, c, 512:1024].rearrange("p (h d) -> p h d", h=HB), o, r,
                                  ALU.mult).then_inc(small_taken, 1)

            def front(b):
                s, m, nm = swork[b % 2], mx[:, b % 2], nmx[:, b % 2]
                h0 = (0 if b < 2 else HA) + (b % 2) * 4
                if b == 0:
                    dve.wait_ge(pool_s, POOL_MASKS)
                    dve.wait_ge(small_in, 16 * N_SMALL)
                dve.wait_ge(s_done, b + 1)
                X, Y = s[:, 0:1024].rearrange("p (h k) -> p h k", h=4), s[:, 1024:1536].rearrange("p (h k) -> p h k", h=4)
                st(dve.scalar_tensor_tensor(out=X, in0=psf[:, 0:1024].rearrange("p (h k) -> p h k", h=4), scalar=SCALE,
                                            in1=biasX[:, h0:h0 + 4, :], op0=ALU.mult, op1=ALU.add))
                dve.scalar_tensor_tensor(out=Y, in0=psf[:, 1024:1536].rearrange("p (h k) -> p h k", h=4), scalar=SCALE,
                                         in1=biasY[:, h0:h0 + 4, :], op0=ALU.mult, op1=ALU.add).then_inc(s_taken, 1)
                st.wait()
                st(dve.tensor_reduce(m[:, 1, :], X, AX.X, ALU.max))
                dve.wait_ge(s_taken, b + 1)
                st(dve.tensor_reduce(m[:, 0, :], Y, AX.X, ALU.max))
                st.wait()
                if b < 2:
                    sink = sinkb[:, 4 * b:4 * b + 4].unsqueeze(1).broadcast_to([P, TB, 4])
                    st(dve.tensor_tensor(m, m, sink, ALU.max))
                    st.wait()
                    st(dve.tensor_tensor(den2[:, b], sink, m, ALU.subtract))
                    st.wait()
                dve.tensor_scalar(nm, m, -1.0, None, ALU.mult).then_inc(m_ready, 1)

            def back(b):
                s, dn = swork[b % 2], den[:, b % 2]
                dve.wait_ge(exp_done, 8 * (b + 1))
                if b < 2:
                    dve.wait_ge(sink_done, b + 1)
                    st(dve.tensor_tensor(dn, dn, den2[:, b], ALU.add))
                    st.wait()
                st(dve.reciprocal(dn, dn))
                st.wait()
                if b >= 2:
                    gate = gates[:, :, (b % 2) * 4:(b % 2) * 4 + 4, 1 + (b - 2) // 2]
                    st(dve.tensor_tensor(dn, dn, gate, ALU.mult))
                    st.wait()
                r = dn.unsqueeze(3).broadcast_to([P, TB, 4, HD])
                o = ps[:, SMALL, :].rearrange("p (c h d) -> p c h d", c=TB, h=4)
                n0 = (0 if b < 2 else 512) + (b % 2) * 256
                dst = merged[:, :, n0:n0 + 256].rearrange("p c (h d) -> p c h d", h=4)
                dve.wait_ge(o_full, b + 1)
                if b < 2:
                    dve.tensor_tensor(dst, o, r, ALU.mult).then_inc(small_taken, 1)
                else:
                    tmp = s[:, 0:512].rearrange("p (c h d) -> p c h d", c=TB, h=4)
                    dve.tensor_tensor(tmp, o, r, ALU.mult).then_inc(small_taken, 1)
                    dve.wait_ge(small_taken, small_turn("values", b, 0) + 1)
                    dve.tensor_tensor(dst, dst, tmp, ALU.add).then_inc(ab_merged, 1)

            def softplus(b):
                s = swork[b % 2]
                dve.wait_ge(l_done, b + 1)
                dve.scalar_tensor_tensor(out=s, in0=psf[:, z_base(b):z_base(b) + 1536], scalar=0.0, in1=s,
                                         op0=ALU.max, op1=ALU.add).then_inc(sp_done, 1)

            def take_sticks(b):
                dve.wait_ge(oc_full, b + 1)
                dve.tensor_copy(merged[:, :, 1024 + b * 256:1024 + (b + 1) * 256],
                                ps[:, (SMALL, SMALL, 0, 1)[b], :].rearrange("p (c n) -> p c n", c=TB)).then_inc(small_taken, 1)

            for kind, a, b in SCHEDULE[:FIRST_WOUT]:
                if kind == "ada":
                    ada(a, b)
                elif kind == "mod":
                    mod_unit(a, b)
                elif kind == "modulate":
                    modulate(a)
                elif kind == "cmp_in":
                    windows()
                elif kind == "gates":
                    gate_values()
                elif (kind, a, b) == ("w1", 1, 0):
                    gelu()
                elif kind == "cmp_kv":
                    cmp_take()
                elif kind == "cmp_s":
                    cmp_softmax()
                elif kind == "cmp_t":
                    cmp_take_turned()
                elif kind == "cmp_o":
                    cmp_outputs(a)
                elif kind == "scores":
                    front(a)
                elif kind == "values":
                    back(a)
                elif kind == "rows":
                    dve.wait_ge(ada_sums, 1)
                    dve.tensor_scalar(g1b[:, 0:3 * BN], psf[:, 0:3 * BN], 1.0, None, ALU.add).then_inc(ada_taken, 1)
                    dve.tensor_scalar(g1b[:, 3 * BN:], ps[:, SMALL, :], 1.0, None, ALU.add).then_inc(small_taken, 1)
                elif (kind, a) == ("columns", 3):
                    dve.wait_ge(ada_sums, 2)
                    dve.tensor_tensor(cols[:, 2, :], ps[:, SMALL, 0:KC], bcols[:, 2, :], ALU.add).then_inc(small_taken, 1)
                elif kind == "z":
                    softplus(a)
                elif kind == "suffix":
                    dve.wait_ge(zr_done, a + 1)
                    dve.tensor_scalar(swork[a % 2], psf[:, z_base(a):z_base(a) + 1536], 0.0, None,
                                      ALU.min).then_inc(clamp_done, 1)
                elif kind == "sticks":
                    take_sticks(a)

            dve.wait_ge(sq_done, 3 * TB)
            dve.tensor_scalar(ssq[:, :, 0:2], ssq[:, :, 0:2], 1.0 / 512, 1e-6, ALU.mult, ALU.add)
            dve.tensor_scalar(ssq[:, :, 2:3], ssq[:, :, 2:3], 1.0 / 1024, 1e-6, ALU.mult, ALU.add).then_inc(var_ready, 1)
            norms[0] += 1
            dve.wait_ge(rstd_ready, norms[0])
            for c in range(TB):
                for gi, (lo, hi) in enumerate(((0, 512), (512, 1024), (1024, 2048))):
                    dve.tensor_scalar(merged[:, c, lo:hi], merged[:, c, lo:hi], ssq[:, c, gi:gi + 1], None,
                                      ALU.mult).then_inc(merged_ready, 1)
            dve.wait_ge(ada_sums, 3)
            dve.scalar_tensor_tensor(out=cols[:, 3, :], in0=ps[:, 2, 0:KC], scalar=1.0, in1=bcols[:, 3, :],
                                     op0=ALU.add, op1=ALU.add).then_inc(ada_taken, 1)
            for b in range(0, 8, 2):
                dve.wait_ge(mT_full, b + 1)
                for k in (2 * b, 2 * b + 1):
                    dve.tensor_scalar(featT[:, k, :], ps[:, b, (k % 2) * SEQ:(k % 2 + 1) * SEQ], gaincol[:, k:k + 1],
                                      None, ALU.mult).then_inc(mT_even, 1)
            for kind, a, b in SCHEDULE[FIRST_WOUT:]:
                if kind == "ada":
                    ada(a, b)
            dve.wait_ge(xr_in, 16)
            dve.wait_ge(ln_in, 32)

            def residual(c, n):
                f = slice(n * BN, (n + 1) * BN)
                if (c, n) == (1, 3):
                    dve.wait_ge(pe_freed, PE_BASE)
                else:
                    dve.wait_ge(y_full, 4 * c + n + 1)
                st(dve.tensor_tensor(xn2[:, c, f], ps[:, 4 * c + n, :], g1b[:, f], ALU.mult))
                st.wait()
                st(dve.scalar_tensor_tensor(out=tokens[:, c, f], in0=tokens[:, c, f], scalar=ALPHA, in1=xn2[:, c, f],
                                            op0=ALU.mult, op1=ALU.add))
                st.wait()
                st(dve.bn_stats(stats[:, c, n, :], tokens[:, c, f]))

            def layer_norm(c, g, b):
                inverse_deviation(c)
                st(dve.scalar_tensor_tensor(out=tokens[:, c, :], in0=tokens[:, c, :], scalar=mv[:, c, 0:1], in1=g,
                                            op0=ALU.subtract, op1=ALU.mult))
                st.wait()
                return dve.scalar_tensor_tensor(out=tokens[:, c, :], in0=tokens[:, c, :], scalar=rstd[:, c:c + 1],
                                                in1=b, op0=ALU.mult, op1=ALU.add)

            def first_norms(c):
                st(layer_norm(c, rowg, rowb))
                st.wait()
                for n in range(4):
                    st(dve.bn_stats(stats[:, c, n, :], tokens[:, c, n * BN:(n + 1) * BN]))
                inverse_deviation(c)
                dve.scalar_tensor_tensor(out=nb[:, c:c + 1], in0=mv[:, c, 0:1], scalar=-1.0, in1=rstd[:, c:c + 1],
                                         op0=ALU.mult, op1=ALU.mult).then_inc(nb_ready, 1)

            for n in range(4):
                residual(0, n)
            first_norms(0)
            for n in range(4):
                residual(1, n)
            first_norms(1)
            for b in (0, 2):
                dve.wait_ge(x2T_full, 4 + b + 1)
                for k in range(4 * b, 4 * b + 4):
                    dve.tensor_scalar(featT[:, k, P:2 * P], ps[:, 4 + b, (k % 4) * P:(k % 4 + 1) * P],
                                      cols[:, 3, k:k + 1], cols[:, 2, k:k + 1], ALU.mult, ALU.add).then_inc(x2T_dve, 1)

            dve.wait_ge(route_mm, 1)
            st(dve.tensor_tensor(lg[:], ps[:, 0, 0:TB * (NG + NE)].rearrange("p (c n) -> p c n", c=TB),
                                 brow[:].unsqueeze(1).broadcast_to([P, TB, NG + NE]), ALU.add))
            st.wait()

            def bc(v, n):
                return v.unsqueeze(2).broadcast_to([P, TB, n])

            def first_max(values, n, top, onehot, tmp, index):
                st(dve.tensor_reduce(top, values, AX.X, ALU.max))
                st.wait()
                st(dve.tensor_tensor(tmp, values, bc(top, n), ALU.not_equal))
                st.wait()
                st(dve.scalar_tensor_tensor(out=tmp, in0=tmp, scalar=64.0,
                                            in1=number[:, 0:n].unsqueeze(1).broadcast_to([P, TB, n]),
                                            op0=ALU.mult, op1=ALU.add))
                st.wait()
                st(dve.tensor_reduce(index, tmp, AX.X, ALU.min))
                st.wait()
                st(dve.tensor_tensor(onehot, number[:, 0:n].unsqueeze(1).broadcast_to([P, TB, n]), bc(index, n),
                                     ALU.is_equal))
                st.wait()

            def T(i, n):
                return rt[:, i, :, 0:n]

            number = slot_id[:, 0, :]
            glog = lg[:, :, 0:NG]
            gmax, gidx, psum_g, m8, v1, i1, v2, i2, tot, cnt = (r1[:, i, :] for i in range(10))
            first_max(glog, NG, gmax, T(3, NG), T(4, NG), gidx)
            dve.tensor_tensor(T(0, NG), glog, bc(gmax, NG), ALU.subtract).then_inc(rexp_in, 1)
            gone = T(3, NG)
            prod = T(5, NE).rearrange("p c (g e) -> p c g e", g=NG)
            st(dve.tensor_tensor(prod, lg[:, :, NG:].rearrange("p c (g e) -> p c g e", g=NG),
                                 gone.unsqueeze(3).broadcast_to([P, TB, NG, EPG]), ALU.mult))
            st.wait()
            st(dve.tensor_reduce(T(6, EPG), T(5, NE).rearrange("p c (g e) -> p c e g", g=NG), AX.X, ALU.add))
            st.wait()
            st(dve.tensor_reduce(m8, T(6, EPG), AX.X, ALU.max))
            st.wait()
            dve.tensor_tensor(T(1, EPG), T(6, EPG), bc(m8, EPG), ALU.subtract).then_inc(rexp_in, 1)
            dve.wait_ge(rexp_out, 1)
            st(dve.tensor_reduce(psum_g, T(0, NG), AX.X, ALU.add))
            st.wait()
            dve.wait_ge(rexp_out, 2)
            first_max(T(1, EPG), EPG, v1, T(7, EPG), T(4, EPG), i1)
            st(dve.scalar_tensor_tensor(out=T(8, EPG), in0=T(7, EPG), scalar=-2.0, in1=T(1, EPG), op0=ALU.mult, op1=ALU.add))
            st.wait()
            first_max(T(8, EPG), EPG, v2, T(9, EPG), T(4, EPG), i2)

            def over_groups(dst, per):
                for g in range(NG):
                    ins = dve.tensor_tensor(dst[:, :, g * EPG:(g + 1) * EPG], per, bc(T(3, NG)[:, :, g], EPG), ALU.mult)
                    if g < NG - 1:
                        st(ins)
                return ins

            st(dve.tensor_tensor(T(6, EPG), T(7, EPG), T(9, EPG), ALU.add))
            st.wait()
            over_groups(T(2, NE), T(6, EPG)).then_inc(rtab_ready, 1)
            st(dve.tensor_tensor(tot, v1, v2, ALU.add))
            st.wait()
            st(dve.tensor_tensor(tot, tot, psum_g, ALU.mult))
            st.wait()
            st(dve.reciprocal(tot, tot))
            st.wait()
            st(dve.tensor_tensor(v1, v1, tot, ALU.mult))
            st(dve.tensor_tensor(v2, v2, tot, ALU.mult))
            st.wait()
            st(dve.tensor_tensor(T(10, EPG), T(7, EPG), bc(v1, EPG), ALU.mult))
            st(dve.tensor_tensor(T(11, EPG), T(9, EPG), bc(v2, EPG), ALU.mult))
            st.wait()
            st(dve.tensor_tensor(T(10, EPG), T(10, EPG), T(11, EPG), ALU.add))
            st.wait()
            st(over_groups(gate_te[:], T(10, EPG)))
            dve.wait_ge(rank_full, 1)
            dve.wait_ge(rtab_ready, 1)
            st(dve.scalar_tensor_tensor(out=rankm[:], in0=ps[:, 1, 0:2 * NE].rearrange("p (c e) -> p c e", c=TB),
                                        scalar=1.0, in1=T(2, NE), op0=ALU.add, op1=ALU.mult))
            st(dve.tensor_reduce(cnt[:, 0:1], ps[:, 1, 2 * NE:3 * NE], AX.X, ALU.max))
            st.wait()
            st(dve.tensor_scalar(rankm[:], rankm[:], -1.0, None, ALU.add))
            for w in range(PASSES):
                dve.tensor_scalar(more[:, w:w + 1], cnt[:, 0:1], float(WIN * w), None,
                                  ALU.is_gt).then_inc(route_ready, 1)
            dve.wait_ge(g2_taken, 1)
            for i in range(2):
                dve.memset(free_mark[:, i:i + 1], 0.0).then_inc(misc_free, 1)
            dve.wait_ge(misc_free, 2)
            dve.wait_ge(moe_zeroed, 3)
            st.wait()

            mo = Steps(dve, moe_s)

            def scatter_add(i, turn, used):
                dst = ysum[:, i // 4, (i % 4) * BN:(i % 4 + 1) * BN]
                dve.wait_ge(misc_full, turn + (used + 1))
                dve.tensor_tensor(dst, dst, ps[:, 6 + used % 2, :], ALU.add).then_inc(misc_free, 1)

            def pair_dve(p, q, w):
                turn = q * MISC_PAIR + w * MISC_FLUSH
                mo.turn, mo.n = q * MOE_STEPS + w * MOE_PASS_STEPS, 0
                two = [P, TB, 2, WIN]
                ranks = rankm[:, :, bass.ds(p * 2, 2)].unsqueeze(3).broadcast_to(two)
                weights = gate_te[:, :, bass.ds(p * 2, 2)].unsqueeze(3).broadcast_to(two)
                mo.wait()
                dve.tensor_tensor(sel, slot_id[:].unsqueeze(1).broadcast_to(two), ranks,
                                  ALU.is_equal).then_inc(sel_ready, 1)
                dve.wait_ge(sel_ready, q + 1)
                dve.tensor_tensor(selg, sel, weights, ALU.mult).then_inc(selg_ready, 1)
                dve.wait_ge(pe_freed, q * PAIR_UNITS + (PE_BASE + 16 - PAIR_UNITS))
                for b in range(4):
                    dve.wait_ge(misc_full, turn + (3 * b + 1))
                    for k in range(4 * b, 4 * b + 4):
                        ins = dve.tensor_scalar(x_pair[:, k, :], ps[:, 6 + 3 * b % 2, (k % 4) * P:(k % 4 + 1) * P],
                                                cols[:, 3, k:k + 1], cols[:, 2, k:k + 1], ALU.mult, ALU.add)
                    ins.then_inc(misc_free, 1)
                    for i in (0, 1):
                        scatter_add(2 * b + i, turn, 3 * b + 1 + i)
                dve.wait_ge(misc_full, turn + 13)
                dve.tensor_copy(scatter, ps[:, 6, 0:SEQ]).then_inc(misc_free, 1)
                dve.wait_ge(e_ready, q + 1)
                mo(dve.tensor_tensor(e_gate, ps[:, 0, :], e_gate, ALU.mult))
                mo.wait()
                dve.tensor_tensor(hid, e_gate, ps[:, 1, :], ALU.mult).then_inc(hid_ready, 1)
                dve.wait_ge(misc_full, turn + 14)
                dve.wait_ge(pe_freed, q * PAIR_UNITS + PE_BASE)
                dve.tensor_copy(hidT, ps[:, 7, :]).then_inc(misc_free, 1)
                assert mo.n == MOE_STEPS, mo.n

            def flush_dve(w, alpha):
                mo.turn, mo.n = (w + 1) * (PAIRS * MOE_STEPS) + w * MOE_PASS_STEPS, 0
                turn = (w + 1) * (PAIRS * MISC_PAIR) + w * MISC_FLUSH
                dve.wait_ge(misc_free, turn + 2)
                for c in range(TB):
                    mo(dve.tensor_tensor(ysum[:, c, :], ysum[:, c, :], g2b[:], ALU.mult))
                for c in range(TB):
                    mo.wait()
                    mo(dve.scalar_tensor_tensor(out=tokens[:, c, :], in0=tokens[:, c, :], scalar=alpha,
                                                in1=ysum[:, c, :], op0=ALU.mult, op1=ALU.add))
                mo.wait()
                for i in range(8):
                    c, f = i // 4, slice((i % 4) * BN, (i % 4 + 1) * BN)
                    dve.wait_ge(misc_full, turn + (i + 1))
                    dve.tensor_tensor(ysum[:, c, f], ps[:, 6 + i % 2, :], g2b[:, f], ALU.mult).then_inc(misc_free, 1)
                    dve.wait_ge(misc_free, turn + (i + 3))
                    mo(dve.tensor_tensor(tokens[:, c, f], tokens[:, c, f], ysum[:, c, f], ALU.add))
                assert mo.n == MOE_FLUSH_STEPS, mo.n

            def start_pass(w):
                mo.turn, mo.n = w * (PAIRS * MOE_STEPS + MOE_PASS_STEPS) - MOE_START_STEPS, 0
                mo.wait()
                mo(dve.memset(scatter, 0.0))
                mo(dve.memset(ysum, 0.0))
                mo(dve.tensor_scalar(rankm[:], rankm[:], -float(WIN), None, ALU.add))
                assert mo.n == MOE_START_STEPS, mo.n

            with dve.Fori(0, PAIRS) as p:
                pair_dve(p, p, 0)
            flush_dve(0, ALPHA)
            again = dve.value_load(more[0:1, 1:2])
            with dve.If(again > 0):
                with dve.Fori(1, PASSES) as w:
                    go = dve.value_load(more[0:1, bass.ds(w, 1)])
                    with dve.If(go > 0):
                        start_pass(w)
                        with dve.Fori(0, PAIRS) as p:
                            pair_dve(p, w * PAIRS + p, w)
                        flush_dve(w, 1.0)

            st.sem, st.n = fin_s, 0
            dve.wait_ge(ln_in, 64)
            for c in range(TB):
                for n in range(4):
                    st(dve.bn_stats(stats[:, c, n, :], tokens[:, c, n * BN:(n + 1) * BN]))
                variance(c)
            for c in range(TB):
                deviation()
                st(dve.scalar_tensor_tensor(out=tokens[:, c, :], in0=tokens[:, c, :], scalar=mv[:, c, 0:1], in1=row2g,
                                            op0=ALU.subtract, op1=ALU.mult))
                st.wait()
                for half in (0, 1):
                    f = slice(half * D // 2, (half + 1) * D // 2)
                    dve.scalar_tensor_tensor(out=tokens[:, c, f], in0=tokens[:, c, f], scalar=rstd[:, c:c + 1],
                                             in1=row2b[:, f], op0=ALU.mult, op1=ALU.add).then_inc(out_ready, 1)


def softmax_parts(s):
    for h in range(4):
        yield 1, h, s[:, h * 256:(h + 1) * 256]
    for h in range(4):
        yield 0, h, s[:, 1024 + h * P:1024 + (h + 1) * P]


def kernel(x, c, w_ada, b_ada, w_in, sinks, cmp_pe_k, cmp_w1_k, cmp_w2_k, cmp_pe_v, cmp_w1_v, cmp_w2_v,
           mix_gain, w_out, ln1_g, ln1_b, w_rg, b_rg, w_re, b_re, w_gate, w_up, w_down, ln2_g, ln2_b):
    import concourse.bacc as bacc
    from concourse.bass_utils import run_bass_kernel_spmd

    def a(v):
        return np.asarray(v)

    def by_feature(v):
        return v.reshape(-1, P).T

    def w1(v):
        return a(v)[0].reshape(2, CMP_STEP, HD, P).transpose(0, 2, 1, 3).reshape(P, CMP_STEP * P)

    route = np.concatenate([a(w_rg)[0], a(w_re)[0].transpose(1, 0, 2).reshape(D, NE)], axis=1)
    arrays = {
        "x": a(x)[0],
        "cT": by_feature(a(c)[0]),
        "w_ada": a(w_ada)[0],
        "w_mod": w_mod_units(a(w_ada)[0]),
        "b_ada": a(b_ada),
        "b_cols": np.stack([by_feature(a(b_ada)[0, i * D:(i + 1) * D]) for i in (0, 1)]
                           + [by_tile2(a(b_ada)[0, i * D:(i + 1) * D])[:, :, 0] for i in (3, 4)], axis=1),
        "w_in": w_in_units(a(w_in)[0]),
        "w_gb": a(w_in)[0][:, GATE_COL:GATE_COL + 3 * HB].reshape(KC, P, 3 * HB).transpose(1, 0, 2),
        "sinks": a(sinks),
        "pe_k": a(cmp_pe_k)[0].T,
        "pe_v": a(cmp_pe_v)[0].T,
        "w1_k": w1(cmp_w1_k),
        "w1_v": w1(cmp_w1_v),
        "w2_k": a(cmp_w2_k)[0],
        "w2_v": a(cmp_w2_v)[0],
        "gain": by_feature(a(mix_gain)[0]),
        "w_out": a(w_out)[0],
        "ln1_g": a(ln1_g),
        "ln1_b": a(ln1_b),
        "w_route": by_tile2(route),
        "b_route": np.concatenate([a(b_rg), a(b_re).reshape(1, NE)], axis=1),
        "w_gate": a(w_gate)[0].reshape(NE * D, DE),
        "w_up": a(w_up)[0].reshape(NE * D, DE),
        "w_down": a(w_down)[0].reshape(NE * DE, D),
        "ln2_g": a(ln2_g),
        "ln2_b": a(ln2_b),
    }
    nc = bacc.Bacc("TRN2", target_bir_lowering=False, num_devices=1, dynamic_dma_scratch_size=4096)
    named, aps = {}, []
    for name, v in arrays.items():
        v = np.ascontiguousarray(v)
        named[f"in_{name}"] = v
        aps.append(nc.dram_tensor(f"in_{name}", v.shape, mybir.dt.from_np(v.dtype), kind="ExternalInput").ap())
    out = nc.dram_tensor("out", (SEQ, D), F32, kind="ExternalOutput").ap()
    build(nc, *aps, out)
    r = run_bass_kernel_spmd(nc, [named], core_ids=[0])
    return r.results[0]["out"].reshape(1, SEQ, D)
```
